# Optimizing a Trainium2 kernel written in Bass

```python
import jax, jax.numpy as jnp
from jax import lax
import numpy as np

D_MODEL = 1024
BATCH = 1
SEQ = 2048
DEPTH = 1

GRID_W = 64
CTX_LEN = 256
N_BRANCH = 4
BR_W = D_MODEL // 4
HEAD_DIM = 64
N_HEADS = BR_W // HEAD_DIM
CHUNK = 128
NA_ROWS = 8
NA_COLS = 16
LORA_W = 64
LORA_A = 64
RW_IN = 3 * BR_W + LORA_W + LORA_A
POOL_WINDOWS = (2, 4, 8, 16)
EPS = 1e-6
GN_EPS = 64e-5
IN_COLS = 10 * BR_W + RW_IN + N_BRANCH * D_MODEL
SEGMENTS = (("gm_u", BR_W), ("gm_v", BR_W), ("gm_g", BR_W),
            ("na_q", BR_W), ("na_k", BR_W), ("na_v", BR_W), ("na_g", BR_W),
            ("rw_in", RW_IN), ("rw_g", BR_W),
            ("pl_p", BR_W), ("pl_g", BR_W),
            ("merge", N_BRANCH * D_MODEL))

kernel_name = "hybrid_gmlp_natten_rwkv7_pool_dit"

def rmsnorm(x, g):
    xf = x.astype(jnp.float32)
    y = xf * lax.rsqrt(jnp.mean(xf * xf, axis=-1, keepdims=True) + EPS)
    return (y * g).astype(x.dtype)

def to_heads(t):
    return t.reshape(t.shape[:-1] + (N_HEADS, HEAD_DIM))

def split_cols(z):
    out = {}
    off = 0
    for name, width in SEGMENTS:
        out[name] = z[..., off:off + width]
        off += width
    return out

def gmlp_mix(u, v, ln_g, ln_b, w_s, b_s):
    B, T, _ = u.shape
    u = jax.nn.gelu(u)
    vh = to_heads(jax.nn.gelu(v)).astype(jnp.float32)
    mu = jnp.mean(vh, axis=-1, keepdims=True)
    var = jnp.mean(jnp.square(vh - mu), axis=-1, keepdims=True)
    vh = ((vh - mu) * lax.rsqrt(var + EPS) * ln_g + ln_b).astype(u.dtype)
    vc = vh.reshape(B, T // CHUNK, CHUNK, N_HEADS, HEAD_DIM)
    mixed = jnp.einsum('gpq,bnqgc->bnpgc', w_s, vc) + b_s.T[None, None, :, :, None]
    return u * mixed.reshape(B, T, BR_W)

def natten_latent(q, k, v, k_ctx, v_ctx, rpb):
    B, T, H, Dh = q.shape
    rows = T // GRID_W
    kr = min(NA_ROWS, rows)
    r_idx = jnp.arange(rows)
    c_idx = jnp.arange(GRID_W)
    r_start = jnp.clip(r_idx - kr // 2, 0, rows - kr)
    c_start = jnp.clip(c_idx - NA_COLS // 2, 0, GRID_W - NA_COLS)
    band_rows = r_start[:, None] + jnp.arange(kr)[None, :]
    qg = q.reshape(B, rows, GRID_W, H, Dh)
    kg = k.reshape(B, rows, GRID_W, H, Dh)[:, band_rows]
    vg = v.reshape(B, rows, GRID_W, H, Dh)[:, band_rows]
    scale = Dh ** -0.5
    s_band = jnp.einsum('brqhd,brikhd->bhrqik', qg, kg).astype(jnp.float32) * scale
    col_ok = (c_idx[None, :] >= c_start[:, None]) & (c_idx[None, :] < c_start[:, None] + NA_COLS)
    dr = band_rows - r_idx[:, None]
    dc = jnp.clip(c_idx[None, :] - c_idx[:, None], -(NA_COLS - 1), NA_COLS - 1)
    bias = rpb[:, dr[:, None, :, None] + (NA_ROWS - 1), dc[None, :, None, :] + (NA_COLS - 1)]
    s_band = jnp.where(col_ok[None, None, None, :, None, :], s_band + bias[None].astype(jnp.float32), -jnp.inf)
    s_ctx = jnp.einsum('brqhd,blhd->bhrql', qg, k_ctx).astype(jnp.float32) * scale
    s_all = jnp.concatenate([s_band.reshape(B, H, rows, GRID_W, kr * GRID_W), s_ctx], axis=-1)
    p = jax.nn.softmax(s_all, axis=-1).astype(v.dtype)
    p_band = p[..., :kr * GRID_W].reshape(B, H, rows, GRID_W, kr, GRID_W)
    p_ctx = p[..., kr * GRID_W:]
    o = jnp.einsum('bhrqik,brikhd->brqhd', p_band, vg) + jnp.einsum('bhrql,blhd->brqhd', p_ctx, v_ctx)
    return o.reshape(B, T, H * Dh)

def ctx_attention(q, k, v):
    B, L, H, Dh = q.shape
    s = jnp.einsum('blhd,bmhd->bhlm', q, k).astype(jnp.float32) * (Dh ** -0.5)
    p = jax.nn.softmax(s, axis=-1).astype(v.dtype)
    return jnp.einsum('bhlm,bmhd->blhd', p, v).reshape(B, L, H * Dh)

def centred_shift_mix(z, mu):
    prev = jnp.pad(z[:, :-1], ((0, 0), (1, 0), (0, 0)))
    nxt = jnp.pad(z[:, 1:], ((0, 0), (0, 1), (0, 0)))
    return z + (0.5 * (prev + nxt) - z) * mu

def wkv7_scan(r, w, k, v, a, b, s0, reverse):
    def step(S, inp):
        r_t, w_t, k_t, v_t, a_t, b_t = inp
        sa = jnp.einsum('bhvk,bhk->bhv', S, a_t)
        S = S * w_t[:, :, None, :] + sa[..., :, None] * b_t[..., None, :] + v_t[..., :, None] * k_t[..., None, :]
        return S, jnp.einsum('bhvk,bhk->bhv', S, r_t)
    xs = tuple(jnp.moveaxis(t, 1, 0) for t in (r, w, k, v, a, b))
    s_fin, ys = lax.scan(step, s0, xs, reverse=reverse)
    return jnp.moveaxis(ys, 0, 1), s_fin

def rwkv_branch(z_in, s0_f, s0_b, lp):
    dt = z_in.dtype
    B, T, _ = z_in.shape
    zf = centred_shift_mix(z_in, lp['rw_mu']).astype(jnp.float32)
    r, k, v, w_lo, a_lo = jnp.split(zf, [BR_W, 2 * BR_W, 3 * BR_W, 3 * BR_W + LORA_W], axis=-1)
    kk = to_heads(k * lp['rw_kk'])
    kk = kk / jnp.maximum(jnp.sqrt(jnp.sum(kk * kk, axis=-1, keepdims=True)), 1e-12)
    rh, vh, kh = to_heads(r), to_heads(v), to_heads(k)
    r_k = lp['rw_rk'].astype(jnp.float32)
    k_a = to_heads(lp['rw_ka'])
    s0 = (s0_f, s0_b)
    ys, finals, bonus = [], [], []
    for d in range(2):
        w = -jax.nn.softplus(-(lp['rw_w0'][d] + jnp.tanh(w_lo) @ lp['rw_w2'][d])) - 0.5
        decay = to_heads(jnp.exp(-jnp.exp(w)))
        a = to_heads(jax.nn.sigmoid(lp['rw_a0'][d] + a_lo @ lp['rw_a2'][d]))
        kd = kh * (1.0 + (a - 1.0) * k_a)
        y, s_fin = wkv7_scan(rh, decay, kd, vh, -kk, kk * a, s0[d], reverse=(d == 1))
        ys.append(y)
        finals.append(s_fin)
        bonus.append(jnp.sum(rh * kd * r_k, axis=-1, keepdims=True) * vh)
    o = ys[0] + ys[1]
    mu = jnp.mean(o, axis=-1, keepdims=True)
    var = jnp.mean(jnp.square(o - mu), axis=-1, keepdims=True)
    o = (o - mu) * lax.rsqrt(var + GN_EPS) * to_heads(lp['rw_gn_g']) + to_heads(lp['rw_gn_b'])
    o = (o + bonus[0] + bonus[1]).reshape(B, T, BR_W).astype(dt)
    return o, finals[0], finals[1]

def centred_mean(x, w):
    B, T, C = x.shape
    cs = jnp.pad(jnp.cumsum(x.astype(jnp.float32), axis=1), ((0, 0), (1, 0), (0, 0)))
    t = jnp.arange(T)
    lo = jnp.clip(t - w // 2, 0, T)
    hi = jnp.clip(t + w - w // 2, 0, T)
    cnt = (hi - lo).astype(jnp.float32)
    return (cs[:, hi] - cs[:, lo]) / cnt[None, :, None]

def pool_mix(p, w_grp, scale):
    B, T, _ = p.shape
    groups = jnp.split(p, len(POOL_WINDOWS), axis=-1)
    d = jnp.stack([centred_mean(g, w) - g.astype(jnp.float32) for g, w in zip(groups, POOL_WINDOWS)], axis=2)
    y = jnp.einsum('btgc,gcd->btgd', d.astype(p.dtype), w_grp).reshape(B, T, BR_W)
    return y * scale

def merge_branches(branches, merge_logits, w_br, w_out):
    gates = jax.nn.sigmoid(merge_logits.astype(jnp.float32)).astype(merge_logits.dtype)
    y = gates[..., :D_MODEL] * (branches[0] @ w_br[0])
    for i in range(1, N_BRANCH):
        y = y + gates[..., i * D_MODEL:(i + 1) * D_MODEL] * (branches[i] @ w_br[i])
    return y @ w_out

def branch_outputs_local(zs, lp):
    gm = gmlp_mix(zs['gm_u'], zs['gm_v'], lp['gm_ln_g'], lp['gm_ln_b'], lp['gm_ws'], lp['gm_bs']) * jax.nn.silu(zs['gm_g'])
    pl = pool_mix(zs['pl_p'], lp['pl_w'], lp['pl_scale']) * jax.nn.silu(zs['pl_g'])
    return gm, pl

def hybrid_layer(x, ctx, c, c_ctx, lp, update_ctx):
    B = x.shape[0]
    mod = jax.nn.silu(c) @ lp['ada_w'] + lp['ada_b']
    shift, scale, gate = jnp.split(mod[:, None, :], 3, axis=-1)
    mod_c = jax.nn.silu(c_ctx) @ lp['ada_w'] + lp['ada_b']
    shift_c, scale_c, gate_c = jnp.split(mod_c, 3, axis=-1)
    h = rmsnorm(x, lp['norm_g']) * (1 + scale) + shift
    hc = rmsnorm(ctx, lp['norm_g']) * (1 + scale_c) + shift_c
    zs = split_cols(h @ lp['w_in'])
    zc = split_cols(hc @ lp['w_in'])

    k_na_c, v_na_c = to_heads(zc['na_k']), to_heads(zc['na_v'])
    s0 = jnp.zeros((B, N_HEADS, HEAD_DIM, HEAD_DIM), jnp.float32)
    rw_c, s_f, s_b = rwkv_branch(zc['rw_in'], s0, s0, lp)

    gm, pl = branch_outputs_local(zs, lp)
    na = natten_latent(to_heads(zs['na_q']), to_heads(zs['na_k']), to_heads(zs['na_v']),
                       k_na_c, v_na_c, lp['na_rpb']) * jax.nn.silu(zs['na_g'])
    rw = rwkv_branch(zs['rw_in'], s_f, s_b, lp)[0] * jax.nn.silu(zs['rw_g'])
    x = x + gate * merge_branches([gm, na, rw, pl], zs['merge'], lp['w_br'], lp['w_out'])

    if update_ctx:
        gm_c, pl_c = branch_outputs_local(zc, lp)
        na_c = ctx_attention(to_heads(zc['na_q']), k_na_c, v_na_c) * jax.nn.silu(zc['na_g'])
        rw_cg = rw_c * jax.nn.silu(zc['rw_g'])
        ctx = ctx + gate_c * merge_branches([gm_c, na_c, rw_cg, pl_c], zc['merge'], lp['w_br'], lp['w_out'])
    return x, ctx

def setup_inputs(seed: int = 0) -> dict:
    key = jax.random.key(seed)
    ks = jax.random.split(key, 32)
    f32 = jnp.float32

    def nrm(k, shape, s):
        return jax.random.normal(k, shape, f32) * s

    L, D, H, N = DEPTH, D_MODEL, N_HEADS, HEAD_DIM
    return {
        "x": nrm(ks[0], (BATCH, SEQ, D), 1.0),
        "c": nrm(ks[1], (BATCH, D), 1.0),
        "ctx": nrm(ks[2], (BATCH, CTX_LEN, D), 1.0),
        "c_ctx": nrm(ks[3], (D,), 1.0),
        "ada_w": nrm(ks[4], (L, D, 3 * D), 0.5 * D ** -0.5),
        "ada_b": nrm(ks[5], (L, 3 * D), 0.02),
        "norm_g": 1.0 + nrm(ks[6], (L, D), 0.05),
        "w_in": nrm(ks[7], (L, D, IN_COLS), D ** -0.5),
        "gm_ln_g": 1.0 + nrm(ks[8], (L, H, N), 0.05),
        "gm_ln_b": nrm(ks[9], (L, H, N), 0.02),
        "gm_ws": nrm(ks[10], (L, H, CHUNK, CHUNK), CHUNK ** -0.5),
        "gm_bs": 1.0 + nrm(ks[11], (L, H, CHUNK), 0.05),
        "na_rpb": nrm(ks[12], (L, H, 2 * NA_ROWS - 1, 2 * NA_COLS - 1), 0.1),
        "rw_mu": jax.random.uniform(ks[13], (L, RW_IN), f32, 0.0, 1.0),
        "rw_w0": jax.random.uniform(ks[14], (L, 2, BR_W), f32, -6.0, -1.0),
        "rw_w2": nrm(ks[15], (L, 2, LORA_W, BR_W), 0.1),
        "rw_a0": nrm(ks[16], (L, 2, BR_W), 0.1),
        "rw_a2": nrm(ks[17], (L, 2, LORA_A, BR_W), 0.1),
        "rw_kk": 0.85 + nrm(ks[18], (L, BR_W), 0.05),
        "rw_ka": 1.0 + nrm(ks[19], (L, BR_W), 0.05),
        "rw_rk": nrm(ks[20], (L, H, N), 0.1),
        "rw_gn_g": 1.0 + nrm(ks[21], (L, BR_W), 0.05),
        "rw_gn_b": nrm(ks[22], (L, BR_W), 0.02),
        "pl_w": nrm(ks[23], (L, H, N, N), N ** -0.5),
        "pl_scale": 1.0 + nrm(ks[24], (L, BR_W), 0.1),
        "w_br": nrm(ks[25], (L, N_BRANCH, BR_W, D), BR_W ** -0.5),
        "w_out": nrm(ks[26], (L, D, D), D ** -0.5),
        "final_g": 1.0 + nrm(ks[27], (D,), 0.05),
    }

def reference(x, c, ctx, c_ctx, ada_w, ada_b, norm_g, w_in, gm_ln_g, gm_ln_b, gm_ws, gm_bs, na_rpb,
              rw_mu, rw_w0, rw_w2, rw_a0, rw_a2, rw_kk, rw_ka, rw_rk, rw_gn_g, rw_gn_b,
              pl_w, pl_scale, w_br, w_out, final_g):
    for l in range(DEPTH):
        lp = {
            'ada_w': ada_w[l], 'ada_b': ada_b[l], 'norm_g': norm_g[l], 'w_in': w_in[l],
            'gm_ln_g': gm_ln_g[l], 'gm_ln_b': gm_ln_b[l], 'gm_ws': gm_ws[l], 'gm_bs': gm_bs[l],
            'na_rpb': na_rpb[l],
            'rw_mu': rw_mu[l], 'rw_w0': rw_w0[l], 'rw_w2': rw_w2[l], 'rw_a0': rw_a0[l], 'rw_a2': rw_a2[l],
            'rw_kk': rw_kk[l], 'rw_ka': rw_ka[l], 'rw_rk': rw_rk[l], 'rw_gn_g': rw_gn_g[l], 'rw_gn_b': rw_gn_b[l],
            'pl_w': pl_w[l], 'pl_scale': pl_scale[l], 'w_br': w_br[l], 'w_out': w_out[l],
        }
        x, ctx = hybrid_layer(x, ctx, c, c_ctx, lp, update_ctx=(l < DEPTH - 1))
    return rmsnorm(x, final_g)


_drawn_inputs = setup_inputs


def setup_inputs(seed=0):
    import zlib

    import numpy as np

    out = dict(_drawn_inputs(seed))
    spreads = {}
    factors = {'ctx': 3.475,
     'c_ctx': 2.74,
     'ada_b': 3.502,
     'norm_g': 3.258,
     'gm_ln_g': 22.473,
     'gm_ln_b': 50.59,
     'gm_bs': 21.47,
     'na_rpb': 200.0,
     'rw_w2': 6.31,
     'rw_a0': 8.0,
     'rw_kk': 199.707,
     'rw_ka': 4.63,
     'rw_gn_g': 51.897,
     'rw_gn_b': 200.0,
     'pl_scale': 16.559}
    for name, (base, spread) in spreads.items():
        noise = np.random.default_rng([zlib.crc32(name.encode()), seed]).standard_normal(out[name].shape)
        drawn = base * np.exp(spread * noise) if base else spread * noise
        out[name] = __import__('jax').numpy.asarray(drawn.astype(out[name].dtype))
    for name, factor in factors.items():
        out[name] = (out[name] * factor).astype(out[name].dtype)
    return out
```

```python
import numpy as np
import concourse.bass as bass
from concourse import mybir
from contextlib import ExitStack

F32 = mybir.dt.float32
F32R = mybir.dt.float32r
ALU = mybir.AluOpType
ACT = mybir.ActivationFunctionType
AX = mybir.AxisListType

P = 128
D = 1024
KT = D // P
CTX = 256
SEQ = 2048
NT = CTX + SEQ
BLK = 512
NB = SEQ // BLK
BR = 256
CH = 64
EPS = 1e-6
GN_EPS = 64e-5
ZPAD = NT + 3
Z_CTX, Z_LAT = 1, CTX + 2
GRID = 64

T_GU, T_GV, T_GG, T_Q, T_K, T_V, T_NG, T_RW, T_RG, T_PP, T_PG, T_END = 0, 2, 4, 6, 8, 10, 12, 14, 21, 23, 25, 27
MERGE0 = T_END * P


class Signal:

    def __init__(self, ctx, nc, name):
        self.sem = ctx.enter_context(nc.semaphore(name))
        self.n = 0
        self.base = 0

    def mark(self, ins, inc=1):
        ins.then_inc(self.sem, inc)
        self.n += inc
        return self.n

    def step(self, eng, ins):
        self.mark(ins)
        eng.wait_ge(self.sem, self.base + self.n)


def modulation_stage(nc, t, s):
    with ExitStack() as ctx:
        ada = ctx.enter_context(nc.sbuf_tensor("ada", [P, 6, KT, 512], F32))
        cc = ctx.enter_context(nc.sbuf_tensor("cc", [P, 2, KT], F32))
        sc = ctx.enter_context(nc.sbuf_tensor("sc", [P, KT, 2], F32))
        bias = ctx.enter_context(nc.sbuf_tensor("ada_bias", [P, 24], F32))
        ng = ctx.enter_context(nc.sbuf_tensor("norm_g_cols", [P, KT], F32))
        mp = ctx.enter_context(nc.psum_tensor("mod_ps", [P, 24, 2], F32))
        c_in = ctx.enter_context(nc.semaphore("c_in"))
        ada_in = [ctx.enter_context(nc.semaphore(f"ada_in{j}")) for j in range(6)]
        small_in = ctx.enter_context(nc.semaphore("mod_small_in"))
        silu_c = ctx.enter_context(nc.semaphore("silu_c"))
        mod_done = ctx.enter_context(nc.semaphore("mod_done"))
        ones_ready = ctx.enter_context(nc.semaphore("ones_ready"))
        step = Signal(ctx, nc, "mod_step")
        mod, gs = s["mod"], s["gscale"]
        block = ctx.enter_context(nc.Block())

        @block.sync
        def _(sp):
            sp.dma_start(cc[:, 0, :], t["c"].rearrange("a (k p) -> p (a k)", p=P)).then_inc(c_in, 16)
            sp.dma_start(cc[:, 1, :], t["c_ctx"].rearrange("(k p) -> p k", p=P)).then_inc(c_in, 16)
            w = t["ada_w"].rearrange("l (k p) n -> p (l k) n", p=P)
            for j in range(6):
                sp.dma_start(ada[:, j, :, :], w[:, :, j * 512:(j + 1) * 512]).then_inc(ada_in[j], 16)
            sp.dma_start(bias[:], t["ada_b"].rearrange("l (m p) -> p (l m)", p=P)).then_inc(small_in, 16)
            sp.dma_start(ng[:], t["norm_g"].rearrange("l (m p) -> p (l m)", p=P)).then_inc(small_in, 16)

        @block.scalar
        def _(act):
            act.wait_ge(c_in, 32)
            nc.scalar.activation(sc[:, :, :].rearrange("p k s -> p s k"), cc[:], ACT.Silu).then_inc(silu_c, 1)

        @block.tensor
        def _(pe):
            pe.wait_ge(silu_c, 1)
            for m in range(24):
                if m % 4 == 0:
                    pe.wait_ge(ada_in[m // 4], 16)
                for k in range(KT):
                    last = nc.tensor.matmul(mp[:, m, :], ada[:, m // 4, k, (m % 4) * P:(m % 4 + 1) * P],
                                            sc[:, k, :], start=(k == 0), stop=(k == KT - 1))
            last.then_inc(mod_done, 1)

        @block.vector
        def _(dve):
            nc.vector.memset(s["eps"][:], EPS)
            nc.vector.memset(s["gn_eps"][:], GN_EPS)
            step.step(dve, nc.vector.memset(s["heads"][:], 0.0))
            for h in range(2):
                step.mark(nc.vector.memset(s["heads"][h * CH:(h + 1) * CH, h * CH:(h + 1) * CH], 1.0))
            dve.wait_ge(step.sem, step.n)
            nc.vector.tensor_scalar(s["head_mean"][:], s["heads"][:], 1.0 / CH, None, ALU.mult)
            dve.wait_ge(small_in, 32)
            dve.wait_ge(mod_done, 1)
            for v in range(2):
                step.mark(nc.vector.tensor_tensor(mod[:, v, :], mp[:, :, v], bias[:], ALU.add))
            dve.wait_ge(step.sem, step.n)
            for v in range(2):
                nc.vector.scalar_tensor_tensor(gs[:, v, :], mod[:, v, KT:2 * KT], 1.0, ng[:], ALU.add, ALU.mult)

        @block.gpsimd
        def _(pool):
            nc.gpsimd.memset(s["ones"][:], 1.0).then_inc(ones_ready, 1)
            pool.wait_ge(ones_ready, 1)
            nc.gpsimd.affine_select(out=s["ident"][:], in_=s["ones"][:], compare_op=ALU.is_equal, fill=0.0,
                                    base=0, pattern=[[-1, P]], channel_multiplier=1)


def projection_stage(nc, t, s):
    with ExitStack() as ctx:
        sb = lambda name, shape, dt=F32: ctx.enter_context(nc.sbuf_tensor(name, shape, dt))
        sem = lambda name: ctx.enter_context(nc.semaphore(name))
        h_hi, h_lo = sb("h_hi", [P, KT, NT], F32R), sb("h_lo", [P, KT, NT], F32R)
        x_in = sb("x_rows", [P, 4, D])
        h_st = sb("h_stage", [P, KT, BLK])
        z_st = sb("z_stage", [P, ZPAD])
        w_raw = sb("w_raw", [P, KT, P])
        w_hi, w_lo = sb("w_hi", [P, KT, P], F32R), sb("w_lo", [P, KT, P], F32R)
        ss, rt, rs = sb("sum_sq", [P, 4]), sb("rms", [P, 4]), sb("rstd", [P, 4])
        ps = ctx.enter_context(nc.psum_tensor("proj_ps", [P, 8, BLK], F32))
        x_loaded, rms_done, x_normed = sem("x_loaded"), sem("rms_done"), sem("x_normed")
        sq_done, rs_done = sem("sq_done"), sem("rs_done")
        turned, h_ready, hi_ready, lo_ready, h_stored = (sem("turned"), sem("h_ready"), sem("hi_ready"),
                                                         sem("lo_ready"), sem("h_stored"))
        w_loaded, w_hi_ready, w_lo_ready, w_free = sem("w_loaded"), sem("w_hi_ready"), sem("w_lo_ready"), sem("w_free")
        z_ps_ready, z_act, z_dve, z_stored = sem("z_ps_ready"), sem("z_act"), sem("z_dve"), sem("z_stored")
        block = ctx.enter_context(nc.Block())
        x_rows = t["x"].rearrange("a (n p) d -> p (a n) d", p=P)
        ctx_rows = t["ctx"].rearrange("a (n p) d -> p (a n) d", p=P)
        w_cols = t["w_in"].rearrange("l (k p) n -> p (l k) n", p=P)
        zT, hT = t["zT"], t["hT"]
        RUNS = [(T_RW, T_RG, True), (T_K, T_NG, True), (T_GU, T_K, False), (T_NG, T_RW, False), (T_RG, T_END, False)]

        def over_blocks(eng, body):
            body(0, 2)
            with eng.Fori(1, NB + 1) as b:
                body(b, 4)

        def over_tiles(eng, body):
            turn = 0
            for a, e, with_ctx in RUNS:
                with eng.Fori(a, e) as tile:
                    body(tile, tile + (turn - a), with_ctx)
                turn += e - a

        @block.sync
        def _(sp):
            def load_x(b, n):
                if n == 4:
                    sp.wait_ge(turned, b * 8)
                src = ctx_rows if n == 2 else x_rows[:, bass.ds((b - 1) * 4, 4), :]
                sp.dma_start(x_in[:, 0:n, :], src).then_inc(x_loaded, 16)

            def store_h(b, n):
                if n == 4:
                    sp.wait_ge(h_ready, b * 8 + 8)
                    sp.dma_start(hT[:, :, bass.ds((b - 1) * BLK, BLK)].rearrange("k p t -> p k t"),
                                 h_st[:]).then_inc(h_stored, 16)

            load_x(0, 2)
            sp.dma_start(w_raw[:], w_cols[:, :, T_RW * P:(T_RW + 1) * P]).then_inc(w_loaded, 16)
            with sp.Fori(1, NB + 1) as b:
                load_x(b, 4)
                store_h(b, 4)

            def tile(col, turn, with_ctx, then):
                if then is not None:
                    sp.wait_ge(w_hi_ready, turn * 8 + 8)
                    sp.wait_ge(w_lo_ready, turn * 8 + 8)
                    sp.dma_start(w_raw[:], w_cols[:, :, bass.ds(then * P, P)]).then_inc(w_loaded, 16)
                sp.wait_ge(z_act, turn * 2 + 3)
                sp.wait_ge(z_dve, turn * 2 + 3)
                lo = 0 if with_ctx else Z_LAT
                sp.dma_start(zT[bass.ds(col, 1), :, lo:ZPAD].rearrange("a p t -> p (a t)"),
                             z_st[:, lo:ZPAD]).then_inc(z_stored, 16)

            turn = 0
            for n, (a, e, with_ctx) in enumerate(RUNS):
                with sp.Fori(a, e - 1) as col:
                    tile(col, col + (turn - a), with_ctx, col + 1)
                turn += e - a
                tile(e - 1, turn - 1, with_ctx, RUNS[n + 1][0] if n + 1 < len(RUNS) else None)
            sp.wait_ge(z_stored, 16 * T_END)
            sp.wait_ge(h_stored, 16 * NB)

        @block.gpsimd
        def _(pool):
            def split_lo(b, n):
                w = n * P
                lo = 0 if n == 2 else (b - 1) * BLK + CTX
                for k in range(KT):
                    pool.wait_ge(hi_ready, b * 8 + k + 1)
                    nc.gpsimd.tensor_tensor(h_lo[:, k, bass.ds(lo, w)], h_st[:, k, 0:w],
                                            h_hi[:, k, bass.ds(lo, w)].bitcast(F32),
                                            ALU.subtract).then_inc(lo_ready, 1)
            over_blocks(pool, split_lo)

        @block.scalar
        def _(act):
            def norm(b, n):
                act.wait_ge(x_loaded, b * 16 + 16)
                before = 0 if n == 2 else b * 4 - 2
                for j in range(n):
                    nc.scalar.activation(z_st[:, 0:D], x_in[:, j, :], ACT.Square,
                                         accum_out=ss[:, j:j + 1]).then_inc(sq_done, 1)
                    act.wait_ge(sq_done, before + j + 1)
                act.wait_ge(x_normed, b)
                nc.scalar.activation(rt[:, 0:n], ss[:, 0:n], ACT.Sqrt, bias=s["eps"][:], scale=1.0 / D).then_inc(rms_done, 1)
                lo = 0 if n == 2 else (b - 1) * BLK + CTX
                w = n * P
                for k in range(KT):
                    act.wait_ge(h_ready, b * 8 + k + 1)
                    nc.scalar.copy(h_hi[:, k, bass.ds(lo, w)], h_st[:, k, 0:w]).then_inc(hi_ready, 1)
            over_blocks(act, norm)

            def tile(col, turn, with_ctx):
                act.wait_ge(w_loaded, turn * 16 + 16)
                for k in range(KT):
                    if k < KT - 1:
                        act.wait_ge(w_free, turn * 7 + k + 1)
                    else:
                        act.wait_ge(z_ps_ready, turn * 5)
                    nc.scalar.copy(w_hi[:, k, :], w_raw[:, k, :]).then_inc(w_hi_ready, 1)
                act.wait_ge(z_stored, turn * 16)
                for m in (0, 2):
                    act.wait_ge(z_ps_ready, turn * 5 + m + 1)
                    nc.scalar.copy(z_st[:, Z_LAT + m * BLK:Z_LAT + (m + 1) * BLK], ps[:, m, :]).then_inc(z_act, 1)
            act.sem_inc(z_act, 1)
            over_tiles(act, tile)

        @block.vector
        def _(dve):
            def norm(b, n):
                dve.wait_ge(rms_done, b + 1)
                nc.vector.reciprocal(rs[:, 0:n], rt[:, 0:n]).then_inc(rs_done, 1)
                dve.wait_ge(rs_done, b + 1)
                for j in range(n):
                    last = nc.vector.tensor_scalar(x_in[:, j, :], x_in[:, j, :], rs[:, j:j + 1], None, ALU.mult)
                last.then_inc(x_normed, 1)
                v = 1 if n == 2 else 0
                w = n * P
                dve.wait_ge(lo_ready, b * 8)
                if n == 4:
                    dve.wait_ge(h_stored, b * 16 - 16)
                for k in range(KT):
                    dve.wait_ge(turned, b * 8 + k + 1)
                    nc.vector.tensor_scalar(h_st[:, k, 0:w], ps[:, k, 0:w], s["gscale"][:, v, k:k + 1],
                                            s["mod"][:, v, k:k + 1], ALU.mult, ALU.add).then_inc(h_ready, 1)
            over_blocks(dve, norm)

            def tile(col, turn, with_ctx):
                for k in range(KT):
                    dve.wait_ge(w_hi_ready, turn * 8 + k + 1)
                    nc.vector.tensor_tensor(w_lo[:, k, :], w_raw[:, k, :], w_hi[:, k, :].bitcast(F32),
                                            ALU.subtract).then_inc(w_lo_ready, 1)
                dve.wait_ge(z_stored, turn * 16)
                for m in (1, 3):
                    dve.wait_ge(z_ps_ready, turn * 5 + m + 1)
                    ins = nc.vector.tensor_copy(z_st[:, Z_LAT + m * BLK:Z_LAT + (m + 1) * BLK], ps[:, m, :])
                    if m == 1 or not with_ctx:
                        ins.then_inc(z_dve, 1)
                if with_ctx:
                    dve.wait_ge(z_ps_ready, turn * 5 + 5)
                    nc.vector.tensor_copy(z_st[:, Z_CTX:Z_CTX + CTX], ps[:, 4, 0:CTX]).then_inc(z_dve, 1)
            for col in (0, Z_CTX + CTX, ZPAD - 1):
                last = nc.vector.memset(z_st[:, col:col + 1], 0.0)
            last.then_inc(z_dve, 1)
            over_tiles(dve, tile)

        @block.tensor
        def _(pe):
            def turn_rows(b, n):
                pe.wait_ge(x_normed, b + 1)
                for k in range(KT):
                    if n == 4:
                        pe.wait_ge(h_ready, b * 8 + k - 7)
                    for j in range(n):
                        last = nc.tensor.transpose(ps[:, k, j * P:(j + 1) * P], x_in[:, j, k * P:(k + 1) * P],
                                                   s["ident"][:])
                    last.then_inc(turned, 1)
            over_blocks(pe, turn_rows)
            pe.wait_ge(lo_ready, 8 * (NB + 1))
            pe.sem_inc(w_free, 7)

            def product(m, k, w, h, first, last):
                cols = slice(CTX + m * BLK, CTX + (m + 1) * BLK) if m < NB else slice(0, CTX)
                out = ps[:, m, :] if m < NB else ps[:, m, 0:CTX]
                return nc.tensor.matmul(out, w[:, k, :], h[:, k, cols], start=first, stop=last)

            def tile(col, turn, with_ctx):
                ms = range(NB + 1) if with_ctx else range(NB)
                for k in range(KT):
                    pe.wait_ge(w_hi_ready, turn * 8 + k + 1)
                    pe.wait_ge(w_lo_ready, turn * 8 + k + 1)
                    if 0 < k < KT - 1:
                        for m in ms:
                            product(m, k, w_hi, h_hi, False, False)
                            product(m, k, w_hi, h_lo, False, False)
                        for m in ms:
                            last = product(m, k, w_lo, h_hi, False, False)
                        last.then_inc(w_free, 1)
                        continue
                    for m in ms:
                        if k == 0:
                            pe.wait_ge(z_dve if m % 2 or m == NB else z_act, turn * 2 + (m > 1))
                        product(m, k, w_hi, h_hi, k == 0, False)
                        product(m, k, w_hi, h_lo, False, False)
                        last = product(m, k, w_lo, h_hi, False, k == KT - 1)
                        if k == KT - 1:
                            last.then_inc(z_ps_ready, 2 if m == NB - 1 and not with_ctx else 1)
                    if k == 0:
                        last.then_inc(w_free, 1)
            over_tiles(pe, tile)


class Results:

    def __init__(self, ctx, nc, name, results):
        self.sem = ctx.enter_context(nc.semaphore(name))
        self.at = {r: n + 1 for n, r in enumerate(results)}
        self.each = len(results)
        assert len(self.at) == self.each
        self.names, self.n = results, 0

    def done(self, ins, result):
        assert self.names[self.n % self.each] == result, (self.names[self.n % self.each], result)
        self.n += 1
        ins.then_inc(self.sem, 1)

    def after(self, eng, turn, result):
        eng.wait_ge(self.sem, turn * self.each + self.at[result])

    def earlier(self, eng, turn, result):
        if not isinstance(turn, int) or turn > 0:
            self.after(eng, turn - 1, result)

    def own(self, eng, turn, ins, result):
        self.done(ins, result)
        self.after(eng, turn, result)


NC_ALL = NT // CH
RB = 256
LEVELS = (1, 2, 4, 8, 16, 32)
DECAY = -float(np.exp(-0.5))


def recurrence_local_stage(nc, t, s, chain):
    with ExitStack() as ctx:
        sb = lambda name, shape, dt=F32: ctx.enter_context(nc.sbuf_tensor(name, shape, dt))
        sem = lambda name: ctx.enter_context(nc.semaphore(name))
        zin, zf, nbr = sb("z_halo", [P, 7, RB + 2]), sb("z_mixed", [P, 7, RB]), sb("neighbours", [P, 7, RB])
        th = sb("tanh_w_lo", [CH, RB])
        kkr, ksq, kk, k1, k2, rrk, kds = (sb(n, [P, 2, RB]) for n in
                                          ("kk_raw", "kk_sq", "kk_unit", "k_1", "k_2", "r_rk", "kd_sum"))
        lw, aa, L, Lx, inc, exc = (sb(n, [P, 2, RB]) for n in ("log_w", "a_rate", "log_run", "log_before", "log_inc", "log_exc"))
        EI, EX, EN = (sb(n, [P, 2, RB]) for n in ("e_inc", "e_exc", "e_neg"))
        kka, kd = sb("kk_a", [P, 2, RB]), sb("k_d", [P, 2, RB])
        AR = sb("a_r_hat", [P, 2, 2, RB])
        Bh, Kh = sb("b_hat", [P, 2, RB]), sb("k_hat", [P, 2, RB])
        Vt = sb("v_rows", [P, 2, 2 * P])
        Bt, Kt = sb("b_rows", [P, 2, 2 * P]), sb("k_rows", [P, 2, 2 * P])
        MB, MK = sb("m_b", [P, 2, 4, 2, P]), sb("m_k", [P, 2, 4, 2, P])
        X, Z, G = sb("inv", [P, 2, 4, P]), sb("inv_t", [P, 2, 4, P]), sb("inv_g", [P, 2, 4, P])
        WI, W = sb("w_in_rows", [P, 2, 4, P]), sb("w_rows", [P, 2, 4, P])
        gst, yst, bst = sb("g_stage", [P, 2, 2, P]), sb("y_stage", [P, 2, 2, P]), sb("bonus_stage", [P, 2, RB])
        lev = sb("level_masks", [P, 2, len(LEVELS), P])
        tri = sb("chunk_masks", [P, 2, 2, P])
        run1, zero, i64, J = sb("scan_keep", [P, 2, RB]), sb("zeros", [P, P]), sb("ident_64", [P, CH]), s["heads"]
        mu, omu, hmu = sb("mu", [P, 7]), sb("one_less_mu", [P, 7]), sb("half_mu", [P, 7])
        par = sb("rw_params", [P, 7, 2])
        hpar = sb("rw_half_params", [P, 4, 2])
        lora = sb("lora", [P, 2, 2 * P])
        ps = ctx.enter_context(nc.psum_tensor("rw_ps", [P, 8, BLK], F32))
        consts_in, consts_set, masks = sem("rw_params_in"), Signal(ctx, nc, "rw_consts_set"), Signal(ctx, nc, "rw_masks")
        z_in, g_stored, y_stored, b_stored = sem("rw_z_in"), sem("g_stored"), sem("y_stored"), sem("bonus_stored")
        DG = [(d, g) for d in range(2) for g in range(2)]
        vec = Results(ctx, nc, "rw_vector_results", ["neighbours"] + [f"mix{j}" for j in range(7)]
                      + ["kkr0", "kkr1", "ksq", "k20", "k21", "k1", "rrk0", "rrk1", "kmax", "krec", "kk"]
                      + sum(([f"{n}{d}" for n in ["lw", "aa", "L", "Lx"] + ["inc", "exc"] * d
                              + ["kka", "kdm", "kd", "kds", "R", "A", "B", "K"]
                              + sum(([f"MB0.{g}.", f"MB1.{g}.", f"MK0.{g}.", f"MK1.{g}.", f"Xa.{g}.", f"Xb.{g}.",
                                      f"Za.{g}.", f"Zb.{g}."] for g in range(2)), [])
                              + sum(([f"G{v}.0.", f"G{v}.1."] + sum(([f"X{v}.{g}."] * (v < 5) + [f"Z{v}.{g}."]
                                                                       for g in range(2)), []) for v in range(1, 6)), [])
                              + ["P0.", "Q0.", "P1.", "Q1.", "Gs0.", "Gs1."]] for d in range(2)), [])
                      + ["bt", "bonus"])
        sca = Results(ctx, nc, "rw_scalar_results", [f"scaled{j}" for j in range(7)] + ["th", "V0", "V1", "knorm"]
                      + sum(([f"{n}{d}" for n in ["tw0.", "tw1.", "ta0.", "ta1.", "EI", "EX", "EN", "tot"]
                              + sum(([f"At{g}.", f"Bt{g}.", f"Kt{g}."] for g in range(2)), [])
                              + ["MV0.0.", "MV1.0.", "MV0.1.", "MV1.1.", "W0.", "W1.", "Y0.", "Y1."]] for d in range(2)), []))
        pro = Results(ctx, nc, "rw_products", ["V", "ksum"]
                      + sum(([f"{n}{d}" for n in ["lora", "At0.", "Kt0.", "SB0.", "SK0.", "SM0.", "At1.", "Kt1.", "SB1.", "SK1.", "SM1."]
                              + sum(([f"G{v}.0.", f"G{v}.1.", f"XZ{v}.0.", f"XZ{v}.1."] for v in range(1, 6)), [])
                              + ["MV0.", "MV1.", "W0.", "W1.", "GY0.", "GY1.", "PQ"]] for d in range(2)), [])
                      + ["bonus"])
        Pst, Qst, tot = chain["P"], chain["Q"], chain["tot"]
        block = ctx.enter_context(nc.Block())

        def turns(eng, body):
            body(0)
            with eng.Fori(1, NT // RB) as n:
                body(n)

        @block.sync
        def _(sp):
            row = lambda a: a.rearrange("l (m p) -> p (l m)", p=P)
            sp.dma_start(mu[:], row(t["rw_mu"])).then_inc(consts_in, 16)
            sp.dma_start(par[:, 0, :], row(t["rw_kk"])).then_inc(consts_in, 16)
            sp.dma_start(par[:, 1, :], row(t["rw_ka"])).then_inc(consts_in, 16)
            sp.dma_start(par[:, 2, :], t["rw_rk"].rearrange("l (m h) n -> (h n) (l m)", h=2)).then_inc(consts_in, 16)
            for d in range(2):
                sp.dma_start(par[:, 3 + d, :], row(t["rw_w0"][:, d, :])).then_inc(consts_in, 16)
                sp.dma_start(par[:, 5 + d, :], row(t["rw_a0"][:, d, :])).then_inc(consts_in, 16)
                sp.dma_start(lora[0:CH, d, :], t["rw_w2"][0, d, :, :]).then_inc(consts_in, 16)
                sp.dma_start(lora[CH:P, d, :], t["rw_a2"][0, d, :, :]).then_inc(consts_in, 16)
            def turn(n):
                vec.earlier(sp, n, "neighbours")
                sca.earlier(sp, n, "scaled6")
                c0 = 0 if isinstance(n, int) else n * RB + 1
                sp.dma_start(zin[:], t["zT"][T_RW:T_RG, :, bass.ds(c0, RB + 2)].rearrange("k p t -> p k t")).then_inc(z_in, 16)
                if isinstance(n, int):
                    return
                lat = (n - 1) * RB
                for d in range(2):
                    for g in range(2):
                        vec.after(sp, n, f"Gs{g}.{d}")
                        sp.dma_start(t["gT"][d, :, :, bass.ds(lat + g * P, P)].rearrange("m p t -> p m t"), gst[:, g, :, :]).then_inc(g_stored, 16)
                        sca.after(sp, n, f"Y{g}.{d}")
                        sp.dma_start(t["yT"][d, :, :, bass.ds(lat + g * P, P)].rearrange("m p t -> p m t"), yst[:, g, :, :]).then_inc(y_stored, 16)
                vec.after(sp, n, "bonus")
                sp.dma_start(t["bonusT"][:, :, bass.ds(lat, RB)].rearrange("m p t -> p m t"), bst[:]).then_inc(b_stored, 16)
            turns(sp, turn)
            sp.wait_ge(g_stored, 16 * 4 * (NT // RB - 1))
            sp.wait_ge(y_stored, 16 * 4 * (NT // RB - 1))
            sp.wait_ge(b_stored, 16 * (NT // RB - 1))

        @block.gpsimd
        def _(pool):
            masks.step(pool, nc.gpsimd.memset(zero[:], 0.0))
            masks.step(pool, nc.gpsimd.memset(lev[:], 0.0))
            one = s["ones"]
            for v, b in enumerate(LEVELS):
                n = P // (2 * b)
                view = lambda m: m.rearrange("p (n h b) -> p n h b", h=2, b=b)
                for d in range(2):
                    o = view(lev[:, d, v, :])[:, :, d, :]
                    masks.step(pool, nc.gpsimd.affine_select(out=o, in_=view(one[:, :])[:, :, 0, :], compare_op=ALU.is_ge, fill=0.0,
                                                             base=-b * (1 - d), pattern=[[-2 * b, n], [0, b]], channel_multiplier=1))
                    masks.step(pool, nc.gpsimd.affine_select(out=o, in_=o, compare_op=ALU.is_ge, fill=0.0, base=b * (2 - d) - 1,
                                                             pattern=[[2 * b, n], [0, b]], channel_multiplier=-1))
            for d in range(2):
                for incl in range(2):
                    o = tri[:, d, incl, :].rearrange("p (c j) -> p c j", c=2)
                    src = one[:, :].rearrange("p (c j) -> p c j", c=2)
                    op = ALU.is_ge if incl else ALU.is_gt
                    sign = 1 - 2 * d
                    masks.step(pool, nc.gpsimd.affine_select(out=o, in_=src, compare_op=op, fill=0.0, base=0,
                                                             pattern=[[CH * sign, 2], [sign, CH]], channel_multiplier=-sign))
                    masks.step(pool, nc.gpsimd.affine_select(out=o, in_=o, compare_op=ALU.is_ge, fill=0.0, base=0,
                                                             pattern=[[-CH, 2], [0, CH]], channel_multiplier=1))
                    masks.step(pool, nc.gpsimd.affine_select(out=o, in_=o, compare_op=ALU.is_ge, fill=0.0, base=CH - 1,
                                                             pattern=[[CH, 2], [0, CH]], channel_multiplier=-1))
            for h in range(2):
                masks.step(pool, nc.gpsimd.affine_select(out=i64[h * CH:(h + 1) * CH, :], in_=one[h * CH:(h + 1) * CH, 0:CH],
                                                         compare_op=ALU.is_equal, fill=0.0, base=0, pattern=[[-1, CH]],
                                                         channel_multiplier=1))

        N_MASKS = 2 + 4 * len(LEVELS) + 12 + 2
        V, A, T = nc.vector, nc.scalar, nc.tensor
        flat = lambda a: a.rearrange("p a b -> p (a b)")

        @block.vector
        def _(dve):
            dve.wait_ge(consts_in, 16 * 12)
            consts_set.mark(V.memset(run1[:], 1.0))
            dve.wait_ge(consts_set.sem, consts_set.n)
            consts_set.mark(V.memset(run1[:].rearrange("p a (c j) -> p a c j", j=CH)[:, :, :, 0:1], 0.0))
            consts_set.mark(V.tensor_scalar(omu[:], mu[:], -1.0, 1.0, ALU.mult, ALU.add))
            consts_set.mark(V.tensor_scalar(hmu[:], mu[:], 0.5, None, ALU.mult))
            consts_set.mark(V.tensor_scalar(hpar[:], par[:, 3:7, :], 0.5, None, ALU.mult))
            dve.wait_ge(consts_set.sem, consts_set.n)
            dve.wait_ge(masks.sem, N_MASKS)

            def turn(n):
                own = lambda ins, name: vec.own(dve, n, ins, name)
                dve.wait_ge(z_in, n * 16 + 16)
                own(V.tensor_tensor(nbr[:], zin[:, :, 0:RB], zin[:, :, 2:RB + 2], ALU.add), "neighbours")
                for j in range(7):
                    sca.after(dve, n, f"scaled{j}")
                    own(V.scalar_tensor_tensor(zf[:, j, :], nbr[:, j, :], hmu[:, j:j + 1], zf[:, j, :], ALU.mult, ALU.add), f"mix{j}")
                for p in range(2):
                    own(V.tensor_scalar(kkr[:, p, :], zf[:, 2 + p, :], par[:, 0, p:p + 1], None, ALU.mult), f"kkr{p}")
                own(V.tensor_tensor(ksq[:], kkr[:], kkr[:], ALU.mult), "ksq")
                for p in range(2):
                    own(V.tensor_scalar(k2[:, p, :], zf[:, 2 + p, :], par[:, 1, p:p + 1], None, ALU.mult), f"k2{p}")
                own(V.tensor_tensor(k1[:], zf[:, 2:4, :], k2[:], ALU.subtract), "k1")
                for p in range(2):
                    own(V.tensor_scalar(rrk[:, p, :], zf[:, p, :], par[:, 2, p:p + 1], None, ALU.mult), f"rrk{p}")
                sca.after(dve, n, "knorm")
                own(V.tensor_scalar(ksq[:], ksq[:], 1e-12, None, ALU.max), "kmax")
                own(V.reciprocal(ksq[:], ksq[:]), "krec")
                own(V.tensor_tensor(kk[:], kkr[:], ksq[:], ALU.mult), "kk")
                for d in range(2):
                    sca.after(dve, n, f"ta1.{d}")
                    own(V.tensor_scalar(lw[:], lw[:], 0.5 * DECAY, 0.5 * DECAY, ALU.mult, ALU.add), f"lw{d}")
                    own(V.tensor_scalar(aa[:], aa[:], 0.5, 0.5, ALU.mult, ALU.add), f"aa{d}")
                    own(V.tensor_tensor_scan(flat(L[:]), flat(run1[:]), flat(lw[:]), 0.0, ALU.mult, ALU.add), f"L{d}")
                    own(V.tensor_tensor(Lx[:], L[:], lw[:], ALU.subtract), f"Lx{d}")
                    if d:
                        chunks = lambda a: a.rearrange("p a (c j) -> p (a c) j", j=CH)
                        end = chunks(L[:])[:, :, CH - 1:CH].to_broadcast([P, 8, CH])
                        own(V.tensor_tensor(chunks(inc[:]), end, chunks(Lx[:]), ALU.subtract), "inc1")
                        own(V.tensor_tensor(chunks(exc[:]), end, chunks(L[:]), ALU.subtract), "exc1")
                    own(V.tensor_tensor(kka[:], kk[:], aa[:], ALU.mult), f"kka{d}")
                    own(V.tensor_tensor(kd[:], k2[:], aa[:], ALU.mult), f"kdm{d}")
                    own(V.tensor_tensor(kd[:], kd[:], k1[:], ALU.add), f"kd{d}")
                    own(V.tensor_copy(kds[:], kd[:]) if d == 0 else V.tensor_tensor(kds[:], kds[:], kd[:], ALU.add), f"kds{d}")
                    sca.after(dve, n, f"EN{d}")
                    own(V.tensor_tensor(AR[:, 1, :, :], zf[:, 0:2, :], EI[:], ALU.mult), f"R{d}")
                    own(V.scalar_tensor_tensor(AR[:, 0, :, :], kk[:], -1.0, EX[:], ALU.mult, ALU.mult), f"A{d}")
                    own(V.tensor_tensor(Bh[:], kka[:], EN[:], ALU.mult), f"B{d}")
                    own(V.tensor_tensor(Kh[:], kd[:], EN[:], ALU.mult), f"K{d}")
                    strict = tri[:, d, :, :].rearrange("p m (o t) -> p o m t", o=1).to_broadcast([P, 2, 2, P])
                    heads = lambda m: m.rearrange("p (o t) -> p o t", o=1).to_broadcast([P, 4, P])
                    of_parity = lambda a, q: a.rearrange("p (m h) t -> p m h t", h=2)[:, :, q, :]
                    bank = lambda b: ps[:, b, :].rearrange("p (h m t) -> p h m t", h=2, m=2)
                    per_head = lambda b: ps[:, b, :].rearrange("p (h t) -> p h t", h=4)
                    for g in range(2):
                        pro.after(dve, n, f"SB{g}.{d}")
                        for q in range(2):
                            for m in range(2):
                                ins = V.tensor_tensor(of_parity(MB[:, g, :, m, :], q), bank(2 + q)[:, :, m, :], strict[:, :, m, :], ALU.mult)
                                if m:
                                    own(ins, f"MB{q}.{g}.{d}")
                        pro.after(dve, n, f"SK{g}.{d}")
                        for q in range(2):
                            for m in range(2):
                                ins = V.tensor_tensor(of_parity(MK[:, g, :, m, :], q), bank(4 + q)[:, :, m, :], strict[:, :, m, :], ALU.mult)
                                if m:
                                    own(ins, f"MK{q}.{g}.{d}")
                        pro.after(dve, n, f"SM{g}.{d}")
                        for q in range(2):
                            ab = ps[:, q, g * 256:(g + 1) * 256].rearrange("p (m t) -> p m t", m=2)
                            ins = V.tensor_tensor(of_parity(X[:, g, :, :], q), ab, heads(lev[:, d, 0, :])[:, 0:2, :], ALU.mult)
                        own(ins, f"Xa.{g}.{d}")
                        own(V.tensor_tensor(X[:, g, :, :], X[:, g, :, :], heads(s["ident"][:, :]), ALU.add), f"Xb.{g}.{d}")
                        own(V.tensor_tensor(Z[:, g, :, :], MB[:, g, :, 0, :], heads(lev[:, 1 - d, 0, :]), ALU.mult), f"Za.{g}.{d}")
                        own(V.tensor_tensor(Z[:, g, :, :], Z[:, g, :, :], heads(s["ident"][:, :]), ALU.add), f"Zb.{g}.{d}")
                    for v in range(1, 6):
                        for g in range(2):
                            pro.after(dve, n, f"G{v}.{g}.{d}")
                            own(V.tensor_tensor(G[:, g, :, :], per_head(g), heads(lev[:, d, v, :]), ALU.mult), f"G{v}.{g}.{d}")
                        for g in range(2):
                            pro.after(dve, n, f"XZ{v}.{g}.{d}")
                            if v < 5:
                                own(V.tensor_tensor(X[:, g, :, :], X[:, g, :, :], per_head(2 + g), ALU.add), f"X{v}.{g}.{d}")
                            own(V.tensor_tensor(Z[:, g, :, :], Z[:, g, :, :], per_head(4 + g), ALU.add), f"Z{v}.{g}.{d}")
                    pro.after(dve, n, f"PQ{d}")
                    sca.after(dve, n, f"tot{d}")
                    for c in range(2):
                        pq = ps[:, 2 + c, :].rearrange("p (g q m j) -> p g q m j", g=2, q=2, m=2)
                        to = lambda st: st[:, d, bass.ds(n * 4, 4), :, :].rearrange("p (g c) m j -> p g c m j", c=2)[:, :, c, :, :]
                        tt = tot[:, d, bass.ds(n * 4, 4), :].rearrange("p (g c) (m o) -> p g c m o", c=2, o=1)[:, :, c, :, :]
                        eye = i64[:, :].rearrange("p (a b j) -> p a b j", a=1, b=1).to_broadcast([P, 2, 2, CH])
                        own(V.tensor_tensor(to(Pst), pq[:, :, 0, :, :], eye, ALU.add), f"P{c}.{d}")
                        own(V.tensor_tensor(to(Qst), pq[:, :, 1, :, :], tt.to_broadcast([P, 2, 2, CH]), ALU.mult), f"Q{c}.{d}")
                    for g in range(2):
                        sca.after(dve, n, f"Y{g}.{d}")
                        if not isinstance(n, int):
                            dve.wait_ge(g_stored, (n * 4 + 2 * d - 4) * 16)
                        gy = ps[:, 4 + g, :].rearrange("p (q m t) -> p q m t", q=2, m=2)
                        own(V.tensor_tensor(gst[:, g, :, :], gy[:, 0, :, :], AR[:, 1, :, g * P:(g + 1) * P], ALU.add), f"Gs{g}.{d}")
                own(V.tensor_tensor(kds[:], kds[:], rrk[:], ALU.mult), "bt")
                pro.after(dve, n, "bonus")
                if not isinstance(n, int):
                    dve.wait_ge(b_stored, (n - 1) * 16)
                own(V.tensor_tensor(bst[:], ps[:, 6, :].rearrange("p (m t) -> p m t", m=2), zf[:, 4:6, :], ALU.mult), "bonus")
            turns(dve, turn)

        @block.scalar
        def _(act):
            act.wait_ge(consts_set.sem, 5)

            def turn(n):
                own = lambda ins, name: sca.own(act, n, ins, name)
                act.wait_ge(z_in, n * 16 + 16)
                vec.earlier(act, n, "bonus")
                pro.earlier(act, n, "bonus")
                for j in range(7):
                    own(A.activation(zf[:, j, :], zin[:, j, 1:RB + 1], ACT.Copy, scale=omu[:, j:j + 1]), f"scaled{j}")
                vec.after(act, n, "mix6")
                own(A.activation(th[:], zf[0:CH, 6, :], ACT.Tanh), "th")
                pro.after(act, n, "V")
                for g in range(2):
                    own(A.copy(Vt[:, g, :], ps[:, 7, g * 256:(g + 1) * 256]), f"V{g}")
                pro.after(act, n, "ksum")
                own(A.activation(flat(ksq[:]), ps[:, 6, :], ACT.Sqrt), "knorm")
                for d in range(2):
                    pro.after(act, n, f"lora{d}")
                    for m in range(2):
                        own(A.activation(lw[:, m, :], ps[:, 7, m * RB:(m + 1) * RB], ACT.Tanh, scale=0.5, bias=hpar[:, d, m:m + 1]), f"tw{m}.{d}")
                    for m in range(2):
                        own(A.activation(aa[:, m, :], ps[:, 6, m * RB:(m + 1) * RB], ACT.Tanh, scale=0.5, bias=hpar[:, 2 + d, m:m + 1]), f"ta{m}.{d}")
                    vec.after(act, n, "exc1" if d else "Lx0")
                    own(A.activation(EI[:], (inc if d else L)[:], ACT.Exp), f"EI{d}")
                    own(A.activation(EX[:], (exc if d else Lx)[:], ACT.Exp), f"EX{d}")
                    own(A.activation(EN[:], (inc if d else L)[:], ACT.Exp, scale=-1.0), f"EN{d}")
                    edge = 0 if d else CH - 1
                    whole = EI[:].rearrange("p m (c j) -> p c m j", j=CH)[:, :, :, edge:edge + 1]
                    own(A.copy(tot[:, d, bass.ds(n * 4, 4), :].rearrange("p c (m o) -> p c m o", o=1), whole), f"tot{d}")
                    for g in range(2):
                        pro.after(act, n, f"Kt{g}.{d}")
                        own(A.copy(WI[:, g, :, 0:CH], ps[:, 6, 0:256].rearrange("p (h j) -> p h j", h=4)), f"At{g}.{d}")
                        own(A.copy(Bt[:, g, :], ps[:, 6, 256:512]), f"Bt{g}.{d}")
                        own(A.copy(Kt[:, g, :], ps[:, 7, 0:256]), f"Kt{g}.{d}")
                    for g in range(2):
                        pro.after(act, n, f"MV{g}.{d}")
                        for q in range(2):
                            mv = ps[:, g, :].rearrange("p (m h t) -> p m h t", m=2, h=2)[:, :, q, q * CH:(q + 1) * CH]
                            own(A.copy(WI[:, g, :, :].rearrange("p (m h) t -> p m h t", h=2)[:, :, q, CH:P], mv), f"MV{q}.{g}.{d}")
                    for g in range(2):
                        pro.after(act, n, f"W{g}.{d}")
                        own(A.copy(W[:, g, :, :], ps[:, 6 + g, :].rearrange("p (h t) -> p h t", h=4)), f"W{g}.{d}")
                    for g in range(2):
                        pro.after(act, n, f"GY{g}.{d}")
                        if not isinstance(n, int):
                            act.wait_ge(y_stored, (n * 4 + 2 * d - 4) * 16)
                        own(A.copy(yst[:, g, :, :], ps[:, 4 + g, 256:512].rearrange("p (m t) -> p m t", m=2)), f"Y{g}.{d}")
            turns(act, turn)

        @block.tensor
        def _(pe):
            mm = lambda o, l, r, start=True, stop=True: T.matmul(o, l, r, start=start, stop=stop)
            half = lambda h: slice((h % 2) * CH, (h % 2 + 1) * CH)

            def turn(n):
                vec.after(pe, n, "mix6")
                vec.earlier(pe, n, "bonus")
                sca.earlier(pe, n, "Y1.1")
                for g in range(2):
                    for p in range(2):
                        last = T.transpose(ps[:, 7, g * 256 + p * P:g * 256 + (p + 1) * P], zf[:, 4 + p, g * P:(g + 1) * P], s["ident"][:])
                pro.done(last, "V")
                vec.after(pe, n, "ksq")
                pro.done(mm(ps[:, 6, :], J[:], flat(ksq[:])), "ksum")
                for d in range(2):
                    sca.after(pe, n, "knorm")
                    if d:
                        sca.after(pe, n, "W1.0")
                    for p in range(2):
                        mm(ps[:, 7, p * RB:(p + 1) * RB], lora[0:CH, d, p * P:(p + 1) * P], th[:])
                    for p in range(2):
                        last = mm(ps[:, 6, p * RB:(p + 1) * RB], lora[CH:P, d, p * P:(p + 1) * P], zf[CH:P, 6, :])
                    pro.done(last, f"lora{d}")
                    vec.after(pe, n, f"K{d}")
                    sca.after(pe, n, f"ta1.{d}")
                    for g in range(2):
                        tok = slice(g * P, (g + 1) * P)
                        if g:
                            sca.after(pe, n, f"Kt0.{d}")
                        for p in range(2):
                            T.transpose(ps[:, 6, p * P:(p + 1) * P], AR[:, 0, p, tok], s["ident"][:])
                            last = T.transpose(ps[:, 6, 256 + p * P:256 + (p + 1) * P], Bh[:, p, tok], s["ident"][:])
                        pro.done(last, f"At{g}.{d}")
                        for p in range(2):
                            last = T.transpose(ps[:, 7, p * P:(p + 1) * P], Kh[:, p, tok], s["ident"][:])
                        pro.done(last, f"Kt{g}.{d}")
                        if g:
                            vec.after(pe, n, f"MB1.0.{d}")
                        elif d:
                            vec.after(pe, n, "Gs1.0")
                            sca.after(pe, n, "Y1.0")
                        for p in range(2):
                            for h in (2 * p, 2 * p + 1):
                                q = h % 2
                                last = mm(ps[:, 2 + q, p * 256:(p + 1) * 256], Bh[half(h), p, tok], AR[half(h), :, p, tok])
                        pro.done(last, f"SB{g}.{d}")
                        if g:
                            vec.after(pe, n, f"MK1.0.{d}")
                        for p in range(2):
                            for h in (2 * p, 2 * p + 1):
                                q = h % 2
                                last = mm(ps[:, 4 + q, p * 256:(p + 1) * 256], Kh[half(h), p, tok], AR[half(h), :, p, tok])
                        pro.done(last, f"SK{g}.{d}")
                        if g:
                            vec.after(pe, n, f"Xa.0.{d}")
                        for h in range(4):
                            p = h // 2
                            last = mm(ps[:, h % 2, g * 256 + p * P:g * 256 + (p + 1) * P], AR[half(h), 0, p, tok], Bh[half(h), p, tok])
                        pro.done(last, f"SM{g}.{d}")
                    for v in range(1, 6):
                        for g in range(2):
                            vec.after(pe, n, f"Zb.1.{d}" if v == 1 else f"Z{v - 1}.{g}.{d}")
                            for h in range(4):
                                last = mm(ps[:, g, h * P:(h + 1) * P], MB[:, g, h, 0, :], X[:, g, h, :])
                            pro.done(last, f"G{v}.{g}.{d}")
                        for g in range(2):
                            vec.after(pe, n, f"G{v}.{g}.{d}")
                            for h in range(4):
                                if v < 5:
                                    mm(ps[:, 2 + g, h * P:(h + 1) * P], Z[:, g, h, :], G[:, g, h, :])
                                last = mm(ps[:, 4 + g, h * P:(h + 1) * P], G[:, g, h, :], Z[:, g, h, :])
                            pro.done(last, f"XZ{v}.{g}.{d}")
                    for g in range(2):
                        for h in range(4):
                            last = mm(ps[:, g, h * P:(h + 1) * P], MK[:, g, h, 0, :], Vt[:, g, (h // 2) * P:(h // 2 + 1) * P])
                        pro.done(last, f"MV{g}.{d}")
                    for g in range(2):
                        vec.after(pe, n, f"Z5.{g}.{d}")
                        sca.after(pe, n, f"MV1.{g}.{d}")
                        for h in range(4):
                            last = mm(ps[:, 6 + g, h * P:(h + 1) * P], Z[:, g, h, :], WI[:, g, h, :])
                        pro.done(last, f"W{g}.{d}")
                    for g in range(2):
                        sca.after(pe, n, f"W{g}.{d}")
                        for h in range(4):
                            p = h // 2
                            mm(ps[half(h), 4 + g, p * P:(p + 1) * P], W[:, g, h, 0:CH], MB[:, g, h, 1, :])
                            o = ps[half(h), 4 + g, 256 + p * P:256 + (p + 1) * P]
                            mm(o, W[:, g, h, CH:P], MB[:, g, h, 1, :], stop=False)
                            last = mm(o, Vt[:, g, h * CH:(h + 1) * CH], MK[:, g, h, 1, :], start=False)
                        pro.done(last, f"GY{g}.{d}")
                    for g in range(2):
                        for h in range(4):
                            for c in range(2):
                                rows = slice(c * CH, (c + 1) * CH)
                                at = g * 256 + (h // 2) * CH
                                bh = Bt[rows, g, h * CH:(h + 1) * CH]
                                mm(ps[half(h), 2 + c, at:at + CH], W[rows, g, h, 0:CH], bh)
                                mm(ps[half(h), 2 + c, at + P:at + P + CH], bh, W[rows, g, h, CH:P], stop=False)
                                last = mm(ps[half(h), 2 + c, at + P:at + P + CH], Kt[rows, g, h * CH:(h + 1) * CH],
                                          Vt[rows, g, h * CH:(h + 1) * CH], start=False)
                    pro.done(last, f"PQ{d}")
                vec.after(pe, n, "bt")
                pro.done(mm(ps[:, 6, :], J[:], flat(kds[:])), "bonus")
            turns(pe, turn)


def recurrence_stage(nc, t, s):
    with ExitStack() as ctx:
        chain = {"P": ctx.enter_context(nc.sbuf_tensor("chunk_p", [P, 2, NC_ALL, 2, CH], F32)),
                 "Q": ctx.enter_context(nc.sbuf_tensor("chunk_q", [P, 2, NC_ALL, 2, CH], F32)),
                 "tot": ctx.enter_context(nc.sbuf_tensor("chunk_decay", [P, 2, NC_ALL, 2], F32))}
        recurrence_local_stage(nc, t, s, chain)
        recurrence_chain_stage(nc, t, s, chain)


def recurrence_chain_stage(nc, t, s, chain):
    with ExitStack() as ctx:
        sb = lambda name, shape, dt=F32: ctx.enter_context(nc.sbuf_tensor(name, shape, dt))
        sem = lambda name: ctx.enter_context(nc.semaphore(name))
        CL, CC = SEQ // CH, CTX // CH
        S = sb("states", [P, CL + 1, 2, 2, CH])
        Sc = sb("ctx_states", [P, CC, 2, 2, CH])
        gt, yt = sb("g_in", [P, 2, 2, 2, BLK]), sb("y_in", [P, 2, 2, BLK])
        rg, bon = sb("rw_gate", [P, 2, BLK]), sb("bonus_in", [P, 2, BLK])
        o, sq, mean, rstd, sg = (sb(n, [P, 2, BLK]) for n in ("o_sum", "o_sq", "o_mean", "o_rstd", "silu_g"))
        gn = sb("gn_params", [P, 2, 2])
        jm = s["head_mean"]
        ps = ctx.enter_context(nc.psum_tensor("chain_ps", [P, 8, BLK], F32))
        p_done, s_done = sem("state_products"), sem("states_done")
        gn_in, g_in, y_in, step = sem("gn_in"), [sem(f"g_in{i}") for i in range(2)], sem("chain_y_in"), Signal(ctx, nc, "chain_step")
        o_ps, mean_ps, var_ps, o_ready, dev_ready, act_done, stored, out_ready = (sem(n) for n in (
            "o_ps", "mean_ps", "var_ps", "o_ready", "dev_ready", "chain_act", "rw_stored", "rw_out_ready"))
        block = ctx.enter_context(nc.Block())
        V, T = nc.vector, nc.tensor
        half = lambda h: slice(h * CH, (h + 1) * CH)

        @block.sync
        def _(sp):
            sp.dma_start(gn[:, 0, :], t["rw_gn_g"].rearrange("l (m p) -> p (l m)", p=P)).then_inc(gn_in, 16)
            sp.dma_start(gn[:, 1, :], t["rw_gn_b"].rearrange("l (m p) -> p (l m)", p=P)).then_inc(gn_in, 16)
            for b in range(NB):
                cols = slice(b * BLK, (b + 1) * BLK)
                if b >= 2:
                    sp.wait_ge(o_ps, b - 1)
                sp.dma_start(gt[:, b % 2, :, :, :], t["gT"][:, :, :, cols].rearrange("d m p t -> p d m t")).then_inc(g_in[b % 2], 16)
                if b >= 1:
                    sp.wait_ge(out_ready, b)
                for d in range(2):
                    sp.dma_start(yt[:, d, :, :], t["yT"][d, :, :, cols].rearrange("m p t -> p m t")).then_inc(y_in, 16)
                sp.dma_start(bon[:], t["bonusT"][:, :, cols].rearrange("m p t -> p m t")).then_inc(y_in, 16)
                sp.dma_start(rg[:], t["zT"][T_RG:T_PP, :, Z_LAT + b * BLK:Z_LAT + (b + 1) * BLK].rearrange("m p t -> p m t")).then_inc(y_in, 16)
                if b >= 1:
                    sp.dma_start(t["branchT"][4:6, :, (b - 1) * BLK:b * BLK].rearrange("m p t -> p m t"), sq[:]).then_inc(stored, 16)
            sp.wait_ge(out_ready, NB)
            sp.dma_start(t["branchT"][4:6, :, SEQ - BLK:SEQ].rearrange("m p t -> p m t"), sq[:]).then_inc(stored, 16)
            sp.wait_ge(stored, 16 * NB)

        def chunk(d, i):
            if i < CC:
                return i if d == 0 else CC - 1 - i
            return i if d == 0 else NC_ALL - 1 - (i - CC)

        def state(d, p, i):
            return (Sc[:, i, d, p, :] if i < CC else S[:, i - CC, d, p, :])

        @block.tensor
        def _(pe):
            n = 0
            for i in range(1, NC_ALL - 1):
                for d in range(2):
                    pe.wait_ge(s_done, 4 * (i - 1) + 2 * d + 2)
                    for p in range(2):
                        for h in range(2):
                            bank = (i % 2) * 4 + d * 2 + p
                            last = T.matmul(ps[half(h), bank, 0:CH], chain["P"][half(h), d, chunk(d, i), p, :],
                                            state(d, p, i)[half(h), :], start=True, stop=True)
                        last.then_inc(p_done, 1)
            pe.wait_ge(s_done, 4 * (NC_ALL - 1))
            for b in range(NB):
                pe.wait_ge(g_in[b % 2], 16 * (b // 2) + 16)
                if b >= 1:
                    pe.wait_ge(o_ready, b)
                for c in range(8):
                    for p in range(2):
                        for h in range(2):
                            for d in range(2):
                                ch = CC + b * 8 + c
                                i = ch if d == 0 else NC_ALL - 1 - ch + CC
                                last = T.matmul(ps[half(h), p, c * CH:(c + 1) * CH], state(d, p, i)[half(h), :],
                                                gt[half(h), b % 2, d, p, c * CH:(c + 1) * CH], start=(d == 0), stop=(d == 1))
                last.then_inc(o_ps, 1)
                pe.wait_ge(o_ready, b + 1)
                for p in range(2):
                    last = T.matmul(ps[:, 2 + p, :], jm[:], o[:, p, :], start=True, stop=True)
                last.then_inc(mean_ps, 1)
                pe.wait_ge(dev_ready, b + 1)
                for p in range(2):
                    last = T.matmul(ps[:, 4 + p, :], jm[:], sq[:, p, :], start=True, stop=True)
                last.then_inc(var_ps, 1)

        @block.scalar
        def _(act):
            for b in range(NB):
                act.wait_ge(var_ps, b + 1)
                nc.scalar.activation(rstd[:], ps[:, 4:6, :], ACT.Sqrt, bias=s["gn_eps"][:]).then_inc(act_done, 1)
                act.wait_ge(y_in, 64 * (b + 1))
                nc.scalar.activation(sg[:], rg[:], ACT.Silu).then_inc(act_done, 1)

        @block.vector
        def _(dve):
            own = lambda ins: step.step(dve, ins)
            for d in range(2):
                for p in range(2):
                    V.tensor_copy(state(d, p, 1), chain["Q"][:, d, chunk(d, 0), p, :]).then_inc(s_done, 1)
            for i in range(1, NC_ALL - 1):
                for d in range(2):
                    for p in range(2):
                        dve.wait_ge(p_done, 4 * (i - 1) + 2 * d + p + 1)
                        V.scalar_tensor_tensor(state(d, p, i + 1), ps[:, (i % 2) * 4 + d * 2 + p, 0:CH],
                                               chain["tot"][:, d, chunk(d, i), p:p + 1], chain["Q"][:, d, chunk(d, i), p, :],
                                               ALU.mult, ALU.add).then_inc(s_done, 1)
            dve.wait_ge(gn_in, 32)
            for b in range(NB):
                dve.wait_ge(y_in, 64 * (b + 1))
                own(V.tensor_tensor(yt[:, 0, :, :], yt[:, 0, :, :], yt[:, 1, :, :], ALU.add))
                dve.wait_ge(o_ps, b + 1)
                V.tensor_tensor(o[:], ps[:, 0:2, :], yt[:, 0, :, :], ALU.add).then_inc(o_ready, 1)
                dve.wait_ge(o_ready, b + 1)
                dve.wait_ge(mean_ps, b + 1)
                own(V.tensor_tensor(o[:], o[:], ps[:, 2:4, :], ALU.subtract))
                if b >= 1:
                    dve.wait_ge(stored, 16 * b)
                V.tensor_tensor(sq[:], o[:], o[:], ALU.mult).then_inc(dev_ready, 1)
                dve.wait_ge(act_done, 2 * b + 1)
                own(V.reciprocal(rstd[:], rstd[:]))
                own(V.tensor_tensor(o[:], o[:], rstd[:], ALU.mult))
                for p in range(2):
                    last = V.tensor_scalar(o[:, p, :], o[:, p, :], gn[:, 0, p:p + 1], gn[:, 1, p:p + 1], ALU.mult, ALU.add)
                own(last)
                own(V.tensor_tensor(o[:], o[:], bon[:], ALU.add))
                dve.wait_ge(act_done, 2 * b + 2)
                V.tensor_tensor(sq[:], o[:], sg[:], ALU.mult).then_inc(out_ready, 1)


def attention_stage(nc, t, s):
    ROWS, KR, BAND = SEQ // GRID, 8, 8 * GRID
    NDR, NDC = 15, 31
    PADW = 2 * GRID - 1
    KEYS = BAND + CTX
    with ExitStack() as ctx:
        sb = lambda name, shape, dt=F32: ctx.enter_context(nc.sbuf_tensor(name, shape, dt))
        sem = lambda name: ctx.enter_context(nc.semaphore(name))
        q, k, v = sb("q_t", [P, 2, SEQ]), sb("k_t", [P, 2, NT]), sb("v_t", [P, 2, NT])
        ng = sb("na_gate", [P, 2, SEQ])
        ve, vo = sb("v_even", [P, NT // P, BR]), sb("v_odd", [P, SEQ // P - 1, BR])
        bias = sb("na_bias", [P, 2, NDR * GRID])
        pad = sb("rpb_padded", [4 * NDR, PADW])
        qs = sb("q_heads", [P, 2, 2, P])
        sband = sb("band_scores", [P, 2, BAND])
        pr = sb("probs", [P, 2, 2, KEYS])
        prt = sb("probs_t", [P, 2, KEYS])
        on = sb("o_rows", [P, 2, P])
        st = sb("softmax_stats", [P, 2, 2, 5])
        rsum = sb("softmax_rsum", [P, 2, 2, 2])
        ps = ctx.enter_context(nc.psum_tensor("na_ps", [P, 8, BLK], F32))
        loads = {n: sem("na_in_" + n) for n in ("q", "k", "v", "g", "rpb")}
        pad_set, pad_out, bias_in, bias_set = sem("pad_set"), sem("pad_out"), sem("bias_in"), Signal(ctx, nc, "bias_set")
        silu_done, v_turned, v_copied = sem("na_silu"), sem("v_turned"), sem("v_copied")
        qz = sem("q_zeroed")
        front = lambda name, r: Results(ctx, nc, name, r)
        fs = front("front_scalar", ["q0", "q1"] + [f"{n}{p}" for p in range(2) for n in ("e", "c")])
        fp = front("front_products", ["S0", "S1"])
        fv = front("front_vector", [f"{n}{p}" for p in range(2) for n in ("m", "b", "n")])
        bv = front("back_vector", ["s0", "r0", "P0", "o0", "s1", "r1", "P1", "g0", "o1", "g1"])
        bs = front("back_scalar", ["P0", "P1"])
        bp = front("back_products", ["T0", "O0", "T1", "OT0", "O1", "OT1"])
        stored = sem("na_stored")
        block = ctx.enter_context(nc.Block())
        V, A, T = nc.vector, nc.scalar, nc.tensor
        half = lambda h: slice(h * CH, (h + 1) * CH)

        def ago(res, eng, row, n, result):
            if not isinstance(row, int) or row >= n:
                res.after(eng, row - n, result)

        def rows(eng, one_front, one_back):
            def place(r):
                start = min(max(r - 4, 0), ROWS - KR)
                return start, start % 2, (start - r + KR - 1) * GRID
            def step(r):
                if r < ROWS:
                    one_front(r, r % 2, *place(r))
                if r > 0:
                    one_back(r - 1, (r - 1) % 2, *place(r - 1))
            for r in range(5):
                step(r)
            with eng.Fori(0, 12) as n:
                for u in range(2):
                    one_front(n * 2 + (5 + u), (5 + u) % 2, n * 2 + (1 + u), (1 + u) % 2, (KR - 5) * GRID)
                    one_back(n * 2 + (4 + u), (4 + u) % 2, n * 2 + u, u % 2, (KR - 5) * GRID)
            for r in range(29, ROWS + 1):
                step(r)

        @block.sync
        def _(sp):
            lat = slice(Z_LAT, Z_LAT + SEQ)
            z = lambda a, c: t["zT"][a:a + 2, :, c].rearrange("m p t -> p m t")
            sp.wait_ge(pad_set, 1)
            sp.dma_start(pad[:, GRID - 16:GRID + 15], t["na_rpb"].rearrange("l h r c -> (l h r) c")).then_inc(loads["rpb"], 16)
            sp.dma_start(v[:, :, 0:CTX], z(T_V, slice(Z_CTX, Z_CTX + CTX))).then_inc(loads["v"], 16)
            sp.dma_start(v[:, :, CTX:NT], z(T_V, lat)).then_inc(loads["v"], 16)
            sp.dma_start(k[:, :, 0:CTX], z(T_K, slice(Z_CTX, Z_CTX + CTX))).then_inc(loads["k"], 16)
            sp.dma_start(k[:, :, CTX:NT], z(T_K, lat)).then_inc(loads["k"], 16)
            sp.dma_start(q[:], z(T_Q, lat)).then_inc(loads["q"], 16)
            sp.dma_start(ng[:], z(T_NG, lat)).then_inc(loads["g"], 16)
            sp.wait_ge(loads["rpb"], 16)
            src = pad[:].rearrange("r (a c) -> r a c", a=1).to_broadcast([4 * NDR, GRID, PADW])
            sp.dma_start(t["rpbPad"][:, :, 0:PADW], src).then_inc(pad_out, 16)
            sp.wait_ge(pad_out, 16)
            for p in range(2):
                for h in range(2):
                    src = bass.AP(tensor=t["rpbPad"].tensor, offset=(2 * p + h) * NDR * GRID * 2 * GRID + GRID - 1,
                                  ap=[[PADW, GRID], [GRID * 2 * GRID, NDR], [1, GRID]])
                    sp.dma_start(bias[half(h), p, :].rearrange("q (r c) -> q r c", c=GRID), src).then_inc(bias_in, 16)
            bv.after(sp, ROWS - 1, "g1")
            sp.dma_start(t["branchT"][2:4, :, :].rearrange("m p t -> p m t"), ng[:]).then_inc(stored, 16)
            sp.wait_ge(stored, 16)

        @block.gpsimd
        def _(pool):
            nc.gpsimd.memset(pad[:], 0.0).then_inc(pad_set, 1)
            nc.gpsimd.memset(qs[:], 0.0).then_inc(qz, 1)
            pool.wait_ge(bias_in, 16 * 4)
            for h in range(2):
                w = bias[half(h), :, :].rearrange("p m (r c) -> p (m r) c", c=GRID)
                bias_set.step(pool, nc.gpsimd.affine_select(out=w[:, :, 0:GRID - 16], in_=w[:, :, 0:GRID - 16], compare_op=ALU.is_ge,
                                                            fill=-1e30, base=8, pattern=[[0, 2 * NDR], [1, GRID - 16]], channel_multiplier=-1))
                bias_set.step(pool, nc.gpsimd.affine_select(out=w[:, :, 16:GRID], in_=w[:, :, 16:GRID], compare_op=ALU.is_gt,
                                                            fill=-1e30, base=8 - 16, pattern=[[0, 2 * NDR], [-1, GRID - 16]], channel_multiplier=1))

        @block.scalar
        def _(act):
            act.wait_ge(loads["g"], 16)
            A.activation(ng[:], ng[:], ACT.Silu).then_inc(silu_done, 1)
            for n in range(17):
                act.wait_ge(v_turned, n + 1)
                dst = ve[:, 2 * n:2 * n + 2, :] if n < 9 else vo[:, 2 * (n - 9):min(2 * (n - 9) + 2, 15), :]
                w = dst.shape[1]
                A.copy(dst, ps[:, n % 4, 0:w * BR].rearrange("p (a c) -> p a c", c=BR)).then_inc(v_copied, 1)
            act.wait_ge(loads["q"], 16)
            act.wait_ge(qz, 1)

            def one_front(r, par, start, vpar, win):
                ago(fp, act, r, 2, "S1")
                for h in range(2):
                    fs.own(act, r, A.activation(qs[half(h), par, :, half(h)], q[half(h), :, bass.ds(r * GRID, GRID)],
                                                ACT.Copy, scale=CH ** -0.5), f"q{h}")
                for p in range(2):
                    ago(bp, act, r, 2, f"T{p}")
                    fv.after(act, r, f"n{p}")
                    fs.own(act, r, A.activation(pr[:, par, p, 0:BAND], sband[:, p, :], ACT.Exp, bias=st[:, par, p, 2:3],
                                                accum_out=st[:, par, p, 3:4]), f"e{p}")
                    fs.own(act, r, A.activation(pr[:, par, p, BAND:KEYS], ps[:, 2 + p, 0:CTX], ACT.Exp, bias=st[:, par, p, 2:3],
                                                accum_out=st[:, par, p, 4:5]), f"c{p}")

            def one_back(r, par, start, vpar, win):
                for p in range(2):
                    bp.after(act, r, f"T{p}")
                    bs.own(act, r, A.copy(prt[:, p, 0:BAND], ps[:, 4, :]), f"P{p}")
            rows(act, one_front, one_back)

        @block.vector
        def _(dve):
            dve.wait_ge(bias_set.sem, 4)
            dve.wait_ge(silu_done, 1)

            def one_front(r, par, start, vpar, win):
                for p in range(2):
                    fp.after(dve, r, f"S{p}")
                    ago(fs, dve, r, 1, f"c{p}")
                    fv.done(V.reduce_max(st[:, par, p, 1:2], ps[:, 2 + p, 0:CTX], AX.X), f"m{p}")
                    fv.own(dve, r, V.tensor_tensor_reduce(out=sband[:, p, :], in0=ps[:, p, :], in1=bias[:, p, win:win + BAND], scale=1.0,
                                                          scalar=-3e38, op0=ALU.add, op1=ALU.max, accum_out=st[:, par, p, 0:1]), f"b{p}")
                    fv.own(dve, r, V.tensor_scalar(st[:, par, p, 2:3], st[:, par, p, 0:1], st[:, par, p, 1:2], -1.0, ALU.max, ALU.mult), f"n{p}")

            def one_back(r, par, start, vpar, win):
                def sums(p):
                    fs.after(dve, r, f"c{p}")
                    bv.own(dve, r, V.tensor_tensor(rsum[:, par, p, 0:1], st[:, par, p, 3:4], st[:, par, p, 4:5], ALU.add), f"s{p}")
                    bv.own(dve, r, V.reciprocal(rsum[:, par, p, 1:2], rsum[:, par, p, 0:1]), f"r{p}")
                    bp.after(dve, r, f"T{p}")
                    bv.own(dve, r, V.tensor_copy(prt[:, p, BAND:KEYS], ps[:, 5, 0:CTX]), f"P{p}")

                def out_rows(p):
                    bp.after(dve, r, f"O{p}")
                    bv.own(dve, r, V.tensor_scalar(on[:, p, :], ps[:, 6, 0:P], rsum[:, par, p, 1:2], None, ALU.mult), f"o{p}")

                def gate(p):
                    bp.after(dve, r, f"OT{p}")
                    for h in range(2):
                        cols = ng[half(h), p, bass.ds(r * GRID, GRID)]
                        ins = V.tensor_tensor(cols, ps[half(h), 7, half(h)], cols, ALU.mult)
                    bv.own(dve, r, ins, f"g{p}")
                sums(0)
                out_rows(0)
                sums(1)
                gate(0)
                out_rows(1)
                gate(1)
            rows(dve, one_front, one_back)

        @block.tensor
        def _(pe):
            pe.wait_ge(loads["v"], 32)
            for n in range(17):
                if n >= 4:
                    pe.wait_ge(v_copied, n - 3)
                tiles = [CTX * 0 + P * a for a in (2 * n, 2 * n + 1)] if n < 9 else [CTX + CH + P * a for a in range(2 * (n - 9), min(2 * (n - 9) + 2, 15))]
                for a, c0 in enumerate(tiles):
                    for p in range(2):
                        last = T.transpose(ps[:, n % 4, a * BR + p * P:a * BR + (p + 1) * P], v[:, p, c0:c0 + P], s["ident"][:])
                last.then_inc(v_turned, 1)
            pe.wait_ge(v_copied, 17)
            pe.wait_ge(loads["k"], 32)

            def scores(r, par, p, start):
                if p == 0:
                    fs.after(pe, r, "q1")
                T.matmul(ps[:, p, :], qs[:, par, p, :], k[:, p, bass.ds(start * GRID + CTX, BAND)], start=True, stop=True)
                fp.done(T.matmul(ps[:, 2 + p, 0:CTX], qs[:, par, p, :], k[:, p, 0:CTX], start=True, stop=True), f"S{p}")

            def turn_probs(r, par, p):
                fs.after(pe, r, f"c{p}")
                if p:
                    bs.after(pe, r, "P0")
                    bv.after(pe, r, "P0")
                else:
                    ago(bs, pe, r, 1, "P1")
                    ago(bv, pe, r, 1, "P1")
                for j in range(6):
                    last = T.transpose(ps[:, 4 + j // 4, (j % 4) * P:(j % 4 + 1) * P], pr[:, par, p, j * P:(j + 1) * P], s["ident"][:])
                bp.done(last, f"T{p}")

            def values(r, p, start, vpar):
                bs.after(pe, r, f"P{p}")
                bv.after(pe, r, f"P{p}")
                for j in range(6):
                    if j >= 4:
                        rhs = ve[:, j - 4, p * P:(p + 1) * P]
                    elif isinstance(start, int):
                        rhs = (vo[:, start // 2 + j, p * P:(p + 1) * P] if vpar else ve[:, 2 + start // 2 + j, p * P:(p + 1) * P])
                    else:
                        tile = half_start[0]
                        rhs = (vo if vpar else ve)[:, bass.ds(tile + (j if vpar else 2 + j), 1), p * P:(p + 1) * P]
                        rhs = rhs.rearrange("p a c -> p (a c)")
                    last = T.matmul(ps[:, 6, 0:P], prt[:, p, j * P:(j + 1) * P], rhs, start=(j == 0), stop=(j == 5))
                bp.done(last, f"O{p}")

            def turn_out(r, p):
                bv.after(pe, r, f"o{p}")
                bp.done(T.transpose(ps[:, 7, 0:P], on[:, p, :], s["ident"][:]), f"OT{p}")

            half_start = [None]

            def one_front(r, par, start, vpar, win):
                scores(r, par, 0, start)
                scores(r, par, 1, start)

            def one_back(r, par, start, vpar, win):
                turn_probs(r, par, 0)
                values(r, 0, start, vpar)
                turn_probs(r, par, 1)
                turn_out(r, 0)
                values(r, 1, start, vpar)
                turn_out(r, 1)

            def place(r):
                start = min(max(r - 4, 0), ROWS - KR)
                return start, start % 2, (start - r + KR - 1) * GRID
            for r in range(5):
                one_front(r, r % 2, *place(r))
                if r:
                    one_back(r - 1, (r - 1) % 2, *place(r - 1))
            with pe.Fori(0, 12) as n:
                half_start[0] = n
                for u in range(2):
                    one_front(n * 2 + (5 + u), (5 + u) % 2, n * 2 + (1 + u), (1 + u) % 2, 0)
                    one_back(n * 2 + (4 + u), (4 + u) % 2, n * 2 + u, u % 2, 0)
            for r in range(29, ROWS + 1):
                if r < ROWS:
                    one_front(r, r % 2, *place(r))
                one_back(r - 1, (r - 1) % 2, *place(r - 1))


def local_branches_stage(nc, t, s):
    with ExitStack() as ctx:
        sb = lambda name, shape, dt=F32: ctx.enter_context(nc.sbuf_tensor(name, shape, dt))
        sem = lambda name: ctx.enter_context(nc.semaphore(name))
        NCK = BLK // P
        gin = sb("gm_in", [P, 2, 6, BLK])
        sq, rstd, vn, gout = sb("gm_sq", [P, 2, BLK]), sb("gm_rstd", [P, 2, BLK]), sb("gm_vn", [P, 2, BLK]), sb("gm_out", [P, 2, BLK])
        vrow = sb("gm_v_rows", [P, NCK, BR])
        wraw, wt = sb("gm_w", [P, 4, P]), sb("gm_w_t", [P, 4, P])
        lnp, bs = sb("gm_ln", [P, 2, 2]), sb("gm_bias", [P, 2, P])
        jm = s["head_mean"]
        EDGE = 8
        pp, s2, s4, s8 = (sb(n, [P, 2, SEQ + 2 * EDGE]) for n in ("pool_in", "pool_2", "pool_4", "pool_8"))
        dd, pg = sb("pool_diff", [P, 2, SEQ]), sb("pool_gate", [P, 2, SEQ])
        edge = sb("pool_edge", [P, 2, 2, EDGE])
        plw, pls = sb("pool_w", [P, 2, P]), sb("pool_scale", [P, 2])
        pout = sb("pool_out", [P, 2, BLK])
        ps = ctx.enter_context(nc.psum_tensor("local_ps", [P, 8, BLK], F32))
        g_in = [sem(f"gm_in{i}") for i in range(2)]
        w_in, bias_in, pool_in, plw_in, plw_set, edge_set = (sem(n) for n in ("gm_w_in", "gm_bias_in", "pool_in", "pool_w_in", "pool_w_set", "pool_edge_set"))
        gm_stored, pl_stored = sem("gm_stored"), sem("pool_stored")
        act_r = Results(ctx, nc, "gm_scalar", ["v", "u", "g", "sqrt", "rows0", "rows1"])
        vec_r = Results(ctx, nc, "gm_vector", ["dev", "sq", "rec", "n1", "ln", "m", "mu", "mg"])
        pe_r = Results(ctx, nc, "gm_products", ["mean", "var", "rows", "mixed"])
        wt_ps, wt_set, pstep = sem("gm_w_turned"), sem("gm_w_set"), Signal(ctx, nc, "pool_step")
        estep = Signal(ctx, nc, "pool_edge_step")
        pl_ps, pl_out, pl_silu = sem("pool_ps"), sem("pool_out_ready"), sem("pool_silu")
        block = ctx.enter_context(nc.Block())
        V, A, T = nc.vector, nc.scalar, nc.tensor
        half = lambda h: slice(h * CH, (h + 1) * CH)
        z = lambda a, c: t["zT"][a:a + 2, :, c].rearrange("m p t -> p m t")

        @block.sync
        def _(sp):
            sp.wait_ge(plw_set, 1)
            sp.dma_start(wraw[:], t["gm_ws"].rearrange("l g p q -> p (l g) q")).then_inc(w_in, 16)
            for n, name in enumerate(("gm_ln_g", "gm_ln_b")):
                sp.dma_start(lnp[:, n, :], t[name].rearrange("l (m h) n -> (h n) (l m)", h=2)).then_inc(bias_in, 16)
            for g in range(4):
                sp.dma_start(bs[half(g % 2), g // 2, :], t["gm_bs"][0, g:g + 1, :].to_broadcast([CH, P])).then_inc(bias_in, 16)
                sp.dma_start(plw[half(g % 2), g // 2, half(g % 2)], t["pl_w"][0, g, :, :]).then_inc(plw_in, 16)
            sp.dma_start(pls[:], t["pl_scale"].rearrange("l (m p) -> p (l m)", p=P)).then_inc(plw_in, 16)
            def load(b):
                c = slice(Z_LAT + b * BLK, Z_LAT + (b + 1) * BLK)
                for n, a in enumerate((T_GU, T_GV, T_GG)):
                    sp.dma_start(gin[:, b % 2, 2 * n:2 * n + 2, :], z(a, c)).then_inc(g_in[b % 2], 16)
            load(0)
            load(1)
            sp.dma_start(pp[:, :, EDGE:EDGE + SEQ], z(T_PP, slice(Z_LAT, Z_LAT + SEQ))).then_inc(pool_in, 16)
            sp.dma_start(pg[:], z(T_PG, slice(Z_LAT, Z_LAT + SEQ))).then_inc(pool_in, 16)
            for b in range(NB):
                vec_r.after(sp, b, "mg")
                sp.dma_start(t["branchT"][0:2, :, b * BLK:(b + 1) * BLK].rearrange("m p t -> p m t"), gout[:]).then_inc(gm_stored, 16)
                if b + 2 < NB:
                    load(b + 2)
            for b in range(NB):
                sp.wait_ge(pl_out, b + 1)
                sp.dma_start(t["branchT"][6:8, :, b * BLK:(b + 1) * BLK].rearrange("m p t -> p m t"), pout[:]).then_inc(pl_stored, 16)
            sp.wait_ge(gm_stored, 16 * NB)
            sp.wait_ge(pl_stored, 16 * NB)

        @block.gpsimd
        def _(pool):
            nc.gpsimd.memset(plw[:], 0.0).then_inc(plw_set, 1)
            last = nc.gpsimd.memset(edge[:], 1.0)
            last.then_inc(edge_set, 1)
            pool.wait_ge(edge_set, 1)
            for g, w in enumerate((2, 4, 8, 16)):
                r = w // 2
                for i in range(r):
                    estep.step(pool, nc.gpsimd.memset(edge[half(g % 2), g // 2, 0, i:i + 1], w / (i + r)))
                for i in range(EDGE - (r - 1), EDGE):
                    estep.step(pool, nc.gpsimd.memset(edge[half(g % 2), g // 2, 1, i:i + 1], w / (r + EDGE - i)))
            for side in (0, SEQ + EDGE):
                last = nc.gpsimd.memset(pp[:, :, side:side + EDGE], 0.0)
            last.then_inc(edge_set, 1)

        @block.scalar
        def _(act):
            act.wait_ge(wt_ps, 1)
            A.copy(wt[:], ps[:, 7, :].rearrange("p (g t) -> p g t", g=4)).then_inc(wt_set, 1)
            for b in range(NB):
                gi = gin[:, b % 2, :, :]
                act.wait_ge(g_in[b % 2], 48 * (b // 2 + 1))
                act_r.own(act, b, A.activation(gi[:, 2:4, :], gi[:, 2:4, :], ACT.Gelu_apprx_tanh), "v")
                act_r.own(act, b, A.activation(gi[:, 0:2, :], gi[:, 0:2, :], ACT.Gelu_apprx_tanh), "u")
                act_r.own(act, b, A.activation(gi[:, 4:6, :], gi[:, 4:6, :], ACT.Silu), "g")
                pe_r.after(act, b, "var")
                vec_r.earlier(act, b, "rec")
                act_r.own(act, b, A.activation(rstd[:], ps[:, 2:4, :], ACT.Sqrt, bias=s["eps"][:]), "sqrt")
                pe_r.after(act, b, "rows")
                for n in range(2):
                    act_r.own(act, b, A.copy(vrow[:, 2 * n:2 * n + 2, :], ps[:, 4 + n, :].rearrange("p (c m) -> p c m", c=2)), f"rows{n}")
            act.wait_ge(pool_in, 32)
            A.activation(pg[:], pg[:], ACT.Silu).then_inc(pl_silu, 1)

        @block.vector
        def _(dve):
            dve.wait_ge(bias_in, 16 * 6)
            for b in range(NB):
                own = lambda ins, name: vec_r.own(dve, b, ins, name)
                gi = gin[:, b % 2, :, :]
                pe_r.after(dve, b, "mean")
                own(V.tensor_tensor(vn[:], gi[:, 2:4, :], ps[:, 0:2, :], ALU.subtract), "dev")
                own(V.tensor_tensor(sq[:], vn[:], vn[:], ALU.mult), "sq")
                act_r.after(dve, b, "sqrt")
                own(V.reciprocal(rstd[:], rstd[:]), "rec")
                own(V.tensor_tensor(vn[:], vn[:], rstd[:], ALU.mult), "n1")
                for p in range(2):
                    last = V.tensor_scalar(vn[:, p, :], vn[:, p, :], lnp[:, 0, p:p + 1], lnp[:, 1, p:p + 1], ALU.mult, ALU.add)
                own(last, "ln")
                pe_r.after(dve, b, "mixed")
                if b:
                    dve.wait_ge(gm_stored, 16 * b)
                for p in range(2):
                    last = V.tensor_tensor(gout[:, p, :].rearrange("p (c t) -> p c t", t=P), ps[:, 6 + p, :].rearrange("p (c t) -> p c t", t=P),
                                           bs[:, p:p + 1, :].to_broadcast([P, NCK, P]), ALU.add)
                own(last, "m")
                own(V.tensor_tensor(gout[:], gout[:], gi[:, 0:2, :], ALU.mult), "mu")
                own(V.tensor_tensor(gout[:], gout[:], gi[:, 4:6, :], ALU.mult), "mg")
            step = lambda ins: pstep.step(dve, ins)
            W = SEQ + 2 * EDGE
            dve.wait_ge(pool_in, 32)
            dve.wait_ge(edge_set, 2)
            step(V.tensor_tensor(s2[:, :, 1:W], pp[:, :, 0:W - 1], pp[:, :, 1:W], ALU.add))
            step(V.tensor_tensor(s4[:, :, 2:W - 1], s2[:, :, 1:W - 2], s2[:, :, 3:W], ALU.add))
            step(V.tensor_tensor(s8[:, 1, 4:W - 3], s4[:, 1, 2:W - 5], s4[:, 1, 6:W - 1], ALU.add))
            step(V.tensor_tensor(s2[half(1), 1, 8:W - 7], s8[half(1), 1, 4:W - 11], s8[half(1), 1, 12:W - 3], ALU.add))
            mid = slice(EDGE, EDGE + SEQ)
            for g, src in enumerate((s2, s4, s8, s2)):
                c, p, w = half(g % 2), g // 2, 2 << g
                for side, cols in ((0, slice(EDGE, 2 * EDGE)), (1, slice(SEQ, SEQ + EDGE))):
                    last = V.tensor_tensor(src[c, p, cols], src[c, p, cols], edge[c, p, side, :], ALU.mult)
                step(last)
                step(V.scalar_tensor_tensor(dd[c, p, :], src[c, p, mid], 1.0 / w, pp[c, p, mid], ALU.mult, ALU.subtract))
            dve.wait_ge(pl_silu, 1)
            for b in range(NB):
                dve.wait_ge(pl_ps, b + 1)
                if b:
                    dve.wait_ge(pl_stored, 16 * b)
                for p in range(2):
                    last = V.scalar_tensor_tensor(pout[:, p, :], ps[:, 2 * (b % 2) + p, :], pls[:, p:p + 1], pg[:, p, b * BLK:(b + 1) * BLK],
                                                  ALU.mult, ALU.mult)
                last.then_inc(pl_out, 1)

        @block.tensor
        def _(pe):
            pe.wait_ge(w_in, 16)
            for g in range(4):
                last = T.transpose(ps[:, 7, g * P:(g + 1) * P], wraw[:, g, :], s["ident"][:])
            last.then_inc(wt_ps, 1)
            pe.wait_ge(wt_set, 1)
            for b in range(NB):
                act_r.after(pe, b, "v")
                for p in range(2):
                    last = T.matmul(ps[:, p, :], jm[:], gin[:, b % 2, 2 + p, :], start=True, stop=True)
                pe_r.done(last, "mean")
                vec_r.after(pe, b, "sq")
                for p in range(2):
                    last = T.matmul(ps[:, 2 + p, :], jm[:], sq[:, p, :], start=True, stop=True)
                pe_r.done(last, "var")
                vec_r.after(pe, b, "ln")
                for c in range(NCK):
                    for p in range(2):
                        last = T.transpose(ps[:, 4 + c // 2, (c % 2) * BR + p * P:(c % 2) * BR + (p + 1) * P], vn[:, p, c * P:(c + 1) * P], s["ident"][:])
                pe_r.done(last, "rows")
                act_r.after(pe, b, "rows1")
                for c in range(NCK):
                    for g in range(4):
                        last = T.matmul(ps[half(g % 2), 6 + g // 2, c * P:(c + 1) * P], vrow[:, c, g * CH:(g + 1) * CH], wt[:, g, :],
                                        start=True, stop=True)
                pe_r.done(last, "mixed")
            pe.wait_ge(pstep.sem, 12)
            pe.wait_ge(plw_in, 16 * 5)
            for b in range(NB):
                if b >= 2:
                    pe.wait_ge(pl_out, b - 1)
                for p in range(2):
                    last = T.matmul(ps[:, 2 * (b % 2) + p, :], plw[:, p, :], dd[:, p, b * BLK:(b + 1) * BLK], start=True, stop=True)
                last.then_inc(pl_ps, 1)


def merge_stage(nc, t, s):
    HALF = SEQ // 2
    HB = HALF // BLK
    with ExitStack() as ctx:
        sb = lambda name, shape, dt=F32: ctx.enter_context(nc.sbuf_tensor(name, shape, dt))
        sem = lambda name: ctx.enter_context(nc.semaphore(name))
        h_hi, h_lo = sb("mh_hi", [P, KT, HALF], F32R), sb("mh_lo", [P, KT, HALF], F32R)
        b_hi, b_lo = sb("mb_hi", [P, 8, HALF], F32R), sb("mb_lo", [P, 8, HALF], F32R)
        y = sb("y_t", [P, KT, HALF])
        NKW = KT + 2
        w_raw, w_hi, w_lo = sb("mw_raw", [P, NKW, P]), sb("mw_hi", [P, NKW, P], F32R), sb("mw_lo", [P, NKW, P], F32R)
        raw = sb("m_raw", [P, 2, BLK])
        gate = sb("m_gate", [P, HB, BLK])
        prod = sb("m_prod", [P, HB, BLK])
        ps = ctx.enter_context(nc.psum_tensor("merge_ps", [P, 8, BLK], F32))
        raw_in = [sem("raw_in0"), sem("raw_in1")]
        raw_hi, raw_lo = sem("raw_hi"), sem("raw_lo")
        w_loaded, w_hi_ready, w_lo_ready, w_used = sem("mw_loaded"), sem("mw_hi_ready"), sem("mw_lo_ready"), sem("mw_used")
        gates_ps, proj_ps, gate_ready, y_step, y_done = sem("gates_ps"), sem("proj_ps"), sem("gate_ready"), sem("y_step"), sem("y_done")
        block = ctx.enter_context(nc.Block())
        V, A, T = nc.vector, nc.scalar, nc.tensor
        TURNS = KT * 4
        NR = 32

        w_cols = t["w_in"].rearrange("l (k p) n -> p (l k) n", p=P)
        w_brs = t["w_br"].rearrange("l i (k p) n -> (l i) p k n", p=P)

        def over_turns(eng, half, body):
            with eng.Fori(0, KT) as j:
                for i in range(4):
                    body(j, i, j * 4 + (half * TURNS + i))

        @block.sync
        def _(sp):
            for half in range(2):
                for n in range(NR):
                    m, b = n // HB, n % HB
                    src = t["hT"] if m < KT else t["branchT"]
                    if half or n >= 2:
                        sp.wait_ge(raw_lo, half * NR + n - 1)
                    sp.dma_start(raw[:, n % 2, :], src[m % KT, :, half * HALF + b * BLK:half * HALF + (b + 1) * BLK]).then_inc(raw_in[n % 2], 16)

                def load(j, i, turn):
                    gates_at, proj_at = sp.snap(j * P + (MERGE0 + i * D)), sp.snap(j * P)
                    sp.wait_ge(w_lo_ready, turn * NKW)
                    sp.dma_start(w_raw[:, 0:KT, :], w_cols[:, :, bass.ds(gates_at, P)]).then_inc(w_loaded, 16)
                    sp.dma_start(w_raw[:, KT:NKW, :], w_brs[i, :, :, bass.ds(proj_at, P)]).then_inc(w_loaded, 16)
                over_turns(sp, half, load)
                sp.wait_ge(y_step, (half + 1) * TURNS * 2)
                sp.dma_start(t["mergedT"][:, :, half * HALF:(half + 1) * HALF].rearrange("k p t -> p k t"), y[:]).then_inc(y_done, 16)
            sp.wait_ge(y_done, 32)

        @block.gpsimd
        def _(pool):
            for half in range(2):
                for n in range(NR):
                    m, b = n // HB, n % HB
                    cols = slice(b * BLK, (b + 1) * BLK)
                    pool.wait_ge(raw_hi, half * NR + n + 1)
                    hi, lo = (h_hi, h_lo) if m < KT else (b_hi, b_lo)
                    nc.gpsimd.tensor_tensor(lo[:, m % KT, cols], raw[:, n % 2, :], hi[:, m % KT, cols].bitcast(F32), ALU.subtract).then_inc(raw_lo, 1)

        @block.scalar
        def _(act):
            for half in range(2):
                if half:
                    act.wait_ge(proj_ps, TURNS)
                for n in range(NR):
                    m, b = n // HB, n % HB
                    act.wait_ge(raw_in[n % 2], 16 * (half * NR // 2 + n // 2 + 1))
                    A.copy((h_hi if m < KT else b_hi)[:, m % KT, b * BLK:(b + 1) * BLK], raw[:, n % 2, :]).then_inc(raw_hi, 1)

                def turn(j, i, turn):
                    act.wait_ge(w_loaded, turn * 32 + 32)
                    for k in range(NKW):
                        if k == KT - 1:
                            act.wait_ge(gates_ps, turn)
                        elif k == NKW - 1:
                            act.wait_ge(proj_ps, turn)
                        else:
                            act.wait_ge(w_used, turn * (NKW - 2) + (k + 1 - (k > KT - 1)))
                        A.copy(w_hi[:, k, :], w_raw[:, k, :]).then_inc(w_hi_ready, 1)
                    act.wait_ge(gates_ps, turn + 1)
                    act.wait_ge(y_step, turn * 2)
                    A.activation(gate[:], ps[:, 0:HB, :], ACT.Sigmoid).then_inc(gate_ready, 1)
                over_turns(act, half, turn)

        @block.vector
        def _(dve):
            for half in range(2):
                def turn(j, i, turn):
                    for k in range(NKW):
                        dve.wait_ge(w_hi_ready, turn * NKW + (k + 1))
                        V.tensor_tensor(w_lo[:, k, :], w_raw[:, k, :], w_hi[:, k, :].bitcast(F32), ALU.subtract).then_inc(w_lo_ready, 1)
                    dve.wait_ge(gate_ready, turn + 1)
                    dve.wait_ge(proj_ps, turn + 1)
                    yj = y[:, bass.ds(j, 1), :].rearrange("p a (b t) -> p (a b) t", b=HB)
                    if i == 0 and half:
                        dve.wait_ge(y_done, 16)
                    V.tensor_tensor(yj if i == 0 else prod[:], gate[:], ps[:, 2:2 + HB, :], ALU.mult).then_inc(y_step, 1)
                    dve.wait_ge(y_step, turn * 2 + 1)
                    if i:
                        V.tensor_tensor(yj, yj, prod[:], ALU.add).then_inc(y_step, 1)
                    else:
                        dve.sem_inc(y_step, 1)
                    dve.wait_ge(y_step, turn * 2 + 2)
                over_turns(dve, half, turn)

        @block.tensor
        def _(pe):
            pe.sem_inc(w_used, NKW - 2)
            for half in range(2):
                pe.wait_ge(raw_lo, (half + 1) * NR)

                def turn(j, i, turn):
                    for k in range(NKW):
                        gates = k < KT
                        first, last_k = k in (0, KT), k in (KT - 1, NKW - 1)
                        hi, lo = (h_hi, h_lo) if gates else (b_hi, b_lo)
                        m = k if gates else 2 * i + k - KT
                        pe.wait_ge(w_hi_ready, turn * NKW + (k + 1))
                        pe.wait_ge(w_lo_ready, turn * NKW + (k + 1))
                        if k == 0:
                            pe.wait_ge(gate_ready, turn)
                        if k == KT:
                            pe.wait_ge(y_step, turn * 2)
                        for b in range(HB):
                            bank = ps[:, b if gates else 2 + b, :]
                            cols = slice(b * BLK, (b + 1) * BLK)
                            T.matmul(bank, w_hi[:, k, :], hi[:, m, cols], start=first, stop=False)
                            T.matmul(bank, w_hi[:, k, :], lo[:, m, cols], start=False, stop=False)
                            last = T.matmul(bank, w_lo[:, k, :], hi[:, m, cols], start=False, stop=last_k)
                        if k == KT - 1:
                            last.then_inc(gates_ps, 1)
                        elif k == NKW - 1:
                            last.then_inc(proj_ps, 1)
                        else:
                            last.then_inc(w_used, 1)
                over_turns(pe, half, turn)


def output_stage(nc, t, s):
    with ExitStack() as ctx:
        sb = lambda name, shape, dt=F32: ctx.enter_context(nc.sbuf_tensor(name, shape, dt))
        sem = lambda name: ctx.enter_context(nc.semaphore(name))
        wo_raw = sb("wo_raw", [P, 2, D])
        wo_hi, wo_lo = sb("wo_hi", [P, KT, D], F32R), sb("wo_lo", [P, KT, D], F32R)
        yr = sb("y_raw", [P, 2, KT, P])
        yh, yl = sb("y_hi", [P, 2, KT, P], F32R), sb("y_lo", [P, 2, KT, P], F32R)
        xr = sb("x_res", [P, 2, D])
        gb, fg = sb("gate_rows", [P, D]), sb("final_g_rows", [P, D])
        gcol = sb("gate_cols", [P, P])
        junk = sb("out_junk", [P, D])
        ss, rt, rs = sb("out_ss", [P, 2]), sb("out_rt", [P, 2]), sb("out_rs", [P, 2])
        ps = ctx.enter_context(nc.psum_tensor("out_ps", [P, 4, BLK], F32))
        gps = ctx.enter_context(nc.psum_tensor("gate_ps", [P, 2, BLK], F32))
        wo_in = [sem("wo_in0"), sem("wo_in1")]
        wo_h, wo_l, fg_in = sem("wo_hi_ready"), sem("wo_lo_ready"), sem("final_g_in")
        y_in, x_in = [sem("y_in0"), sem("y_in1")], [sem("xr_in0"), sem("xr_in1")]
        y_h, y_l, prod = sem("y_hi_ready"), sem("y_lo_ready"), sem("out_products")
        gcol_set, gate_mm = sem("gate_cols_set"), sem("gate_turned")
        vec = Results(ctx, nc, "out_vector", ["gated", "res", "rec", "norm"])
        sca = Results(ctx, nc, "out_scalar", ["ss", "rt"])
        gstep = Signal(ctx, nc, "gate_rows_set")
        stored = [sem("out_stored0"), sem("out_stored1")]
        block = ctx.enter_context(nc.Block())
        V, A, T = nc.vector, nc.scalar, nc.tensor
        NTT = SEQ // P
        x_rows = t["x"].rearrange("a (n p) d -> (a n) p d", p=P)
        o_rows = t["out"].rearrange("a (n p) d -> (a n) p d", p=P)

        def over_tiles(eng, body):
            body(0, 0, 0)
            body(1, 1, 0)
            with eng.Fori(1, NTT // 2) as n:
                body(n * 2, 0, n)
                body(n * 2 + 1, 1, n)

        @block.sync
        def _(sp):
            w = t["w_out"].rearrange("l (k p) n -> (l k) p n", p=P)
            sp.dma_start(fg[:], t["final_g"].rearrange("(a d) -> a d", a=1).to_broadcast([P, D])).then_inc(fg_in, 16)
            for k in range(KT):
                if k >= 2:
                    sp.wait_ge(wo_l, k - 1)
                sp.dma_start(wo_raw[:, k % 2, :], w[k]).then_inc(wo_in[k % 2], 16)

            def load(n, par, m):
                if not isinstance(n, int):
                    sp.wait_ge(stored[par], m * 16)
                sp.dma_start(yr[:, par, :, :], t["mergedT"][:, :, bass.ds(n * P, P)].rearrange("k p t -> p k t")).then_inc(y_in[par], 16)
                sp.dma_start(xr[:, par, :], x_rows[bass.ds(n, 1), :, :].rearrange("a p d -> p (a d)")).then_inc(x_in[par], 16)
            over_tiles(sp, load)

        @block.gpsimd
        def _(pool):
            for k in range(KT):
                pool.wait_ge(wo_h, k + 1)
                nc.gpsimd.tensor_tensor(wo_lo[:, k, :], wo_raw[:, k % 2, :], wo_hi[:, k, :].bitcast(F32), ALU.subtract).then_inc(wo_l, 1)

            def split(n, par, m):
                pool.wait_ge(y_h, n + 1)
                nc.gpsimd.tensor_tensor(yl[:, par, :, :], yr[:, par, :, :], yh[:, par, :, :].bitcast(F32), ALU.subtract).then_inc(y_l, 1)
            over_tiles(pool, split)

        @block.scalar
        def _(act):
            for k in range(KT):
                act.wait_ge(wo_in[k % 2], 16 * (k // 2 + 1))
                A.copy(wo_hi[:, k, :], wo_raw[:, k % 2, :]).then_inc(wo_h, 1)

            def hi(n, par, m):
                act.wait_ge(y_in[par], m * 16 + 16)
                if not isinstance(n, int):
                    act.wait_ge(prod, n - 1)
                A.copy(yh[:, par, :, :], yr[:, par, :, :]).then_inc(y_h, 1)

            def norm(n, par, m):
                vec.after(act, n, "res")
                sca.own(act, n, A.activation(junk[:], xr[:, par, :], ACT.Square, accum_out=ss[:, par:par + 1]), "ss")
                sca.own(act, n, A.activation(rt[:, par:par + 1], ss[:, par:par + 1], ACT.Sqrt, bias=s["eps"][:], scale=1.0 / D), "rt")
                vec.after(act, n, "norm")
                act.dma_start(o_rows[bass.ds(n, 1), :, :].rearrange("a p d -> p (a d)"), xr[:, par, :]).then_inc(stored[par], 16)
            hi(0, 0, 0)
            hi(1, 1, 0)
            norm(0, 0, 0)
            with act.Fori(1, NTT // 2) as n:
                hi(n * 2, 0, n)
                norm(n * 2 - 1, 1, n - 1)
                hi(n * 2 + 1, 1, n)
                norm(n * 2, 0, n)
            norm(NTT - 1, 1, NTT // 2 - 1)
            for par in range(2):
                act.wait_ge(stored[par], 16 * NTT // 2)

        @block.vector
        def _(dve):
            for k in range(KT):
                gstep.step(dve, V.tensor_copy(gcol[:], s["mod"][:, 0, 2 * KT + k:2 * KT + k + 1].to_broadcast([P, P])))
                dve.wait_ge(gate_mm, k + 1)
            V.tensor_copy(gb[:].rearrange("p (b d) -> p b d", b=2), gps[:]).then_inc(gcol_set, 1)
            dve.wait_ge(gcol_set, 1)
            dve.wait_ge(fg_in, 16)

            def tile(n, par, m):
                dve.wait_ge(prod, n + 1)
                dve.wait_ge(x_in[par], m * 16 + 16)
                gated = ps[:, 2 * par:2 * par + 2, :]
                vec.own(dve, n, V.tensor_tensor(gated, gated, gb[:].rearrange("p (b d) -> p b d", b=2), ALU.mult), "gated")
                xv = xr[:, par, :].rearrange("p (b d) -> p b d", b=2)
                vec.own(dve, n, V.tensor_tensor(xv, xv, gated, ALU.add), "res")
                sca.after(dve, n, "rt")
                vec.own(dve, n, V.reciprocal(rs[:, par:par + 1], rt[:, par:par + 1]), "rec")
                vec.own(dve, n, V.scalar_tensor_tensor(xr[:, par, :], xr[:, par, :], rs[:, par:par + 1], fg[:], ALU.mult, ALU.mult), "norm")
            over_tiles(dve, tile)

        @block.tensor
        def _(pe):
            for k in range(KT):
                pe.wait_ge(gstep.sem, k + 1)
                T.matmul(gps[:, k // 4, (k % 4) * P:(k % 4 + 1) * P], gcol[:], s["ident"][:], start=True, stop=True).then_inc(gate_mm, 1)

            def tile(n, par, m):
                pe.wait_ge(y_l, n + 1)
                if isinstance(n, int) and n == 0:
                    pe.wait_ge(wo_l, KT)
                if not isinstance(n, int):
                    vec.after(pe, n - 2, "res")
                for k in range(KT):
                    for b in range(2):
                        o = ps[:, 2 * par + b, :]
                        cols = slice(b * BLK, (b + 1) * BLK)
                        T.matmul(o, yh[:, par, k, :], wo_hi[:, k, cols], start=(k == 0), stop=False)
                        T.matmul(o, yh[:, par, k, :], wo_lo[:, k, cols], start=False, stop=False)
                        last = T.matmul(o, yl[:, par, k, :], wo_hi[:, k, cols], start=False, stop=(k == KT - 1))
                last.then_inc(prod, 1)
            over_tiles(pe, tile)


STAGES = (modulation_stage, projection_stage, recurrence_stage, attention_stage, local_branches_stage, merge_stage, output_stage)


_INS = ["x", "c", "ctx", "c_ctx", "ada_w", "ada_b", "norm_g", "w_in", "gm_ln_g", "gm_ln_b", "gm_ws", "gm_bs", "na_rpb",
        "rw_mu", "rw_w0", "rw_w2", "rw_a0", "rw_a2", "rw_kk", "rw_ka", "rw_rk", "rw_gn_g", "rw_gn_b", "pl_w", "pl_scale",
        "w_br", "w_out", "final_g"]


def hybrid_layer_kernel(nc, t, stages=None):
    with ExitStack() as ctx:
        ctx.enter_context(nc.allow_non_contiguous_dma(reason="parameters as columns"))
        s = {name: ctx.enter_context(nc.sbuf_tensor(name, shape, F32)) for name, shape in (
            ("ident", [P, P]), ("ones", [P, P]), ("heads", [P, P]), ("head_mean", [P, P]), ("eps", [P, 1]), ("gn_eps", [P, 1]),
            ("mod", [P, 2, 24]), ("gscale", [P, 2, KT]))}
        for stage in (stages or STAGES):
            stage(nc, t, s)


SCRATCH = {"zT": (T_END, P, ZPAD), "hT": (KT, P, SEQ), "gT": (2, 2, P, SEQ), "yT": (2, 2, P, SEQ),
           "bonusT": (2, P, SEQ), "branchT": (8, P, SEQ), "rpbPad": (60, GRID, 2 * GRID), "mergedT": (KT, P, SEQ)}


def kernel(**inputs):
    import numpy as _np
    import concourse.bacc as _bacc
    from concourse import mybir as _mybir
    from concourse.bass_utils import run_bass_kernel_spmd as _run

    nc = _bacc.Bacc("TRN2", target_bir_lowering=False, num_devices=1)
    arrays, t = {}, {}
    for name in _INS:
        a = _np.ascontiguousarray(inputs[name])
        arrays[f"in_{name}"] = a
        t[name] = nc.dram_tensor(f"in_{name}", a.shape, _mybir.dt.from_np(a.dtype), kind="ExternalInput").ap()
    for name, shape in SCRATCH.items():
        t[name] = nc.dram_tensor(f"scratch_{name}", shape, F32, kind="Internal").ap()
    t["out"] = nc.dram_tensor("out", (1, SEQ, D), F32, kind="ExternalOutput").ap()
    hybrid_layer_kernel(nc, t)
    r = _run(nc, [arrays], core_ids=[0])
    return r.results[0]["out"]
```

```python
import numpy as np
import concourse.bass as bass
from concourse import mybir
from contextlib import ExitStack

F32 = mybir.dt.float32
F32R = mybir.dt.float32r
ALU = mybir.AluOpType
ACT = mybir.ActivationFunctionType
AX = mybir.AxisListType

P = 128
D = 1024
KT = D // P
CTX = 256
SEQ = 2048
NT = CTX + SEQ
BLK = 512
NB = SEQ // BLK
BR = 256
CH = 64
EPS = 1e-6
GN_EPS = 64e-5
ZPAD = NT + 3
Z_CTX, Z_LAT = 1, CTX + 2
GRID = 64

T_GU, T_GV, T_GG, T_Q, T_K, T_V, T_NG, T_RW, T_RG, T_PP, T_PG, T_END = 0, 2, 4, 6, 8, 10, 12, 14, 21, 23, 25, 27
T_ALL = T_END + 32


class Signal:

    def __init__(self, ctx, nc, name):
        self.sem = ctx.enter_context(nc.semaphore(name))
        self.n = 0
        self.base = 0

    def mark(self, ins, inc=1):
        ins.then_inc(self.sem, inc)
        self.n += inc
        return self.n

    def step(self, eng, ins):
        self.mark(ins)
        eng.wait_ge(self.sem, self.base + self.n)


def modulation_stage(nc, t, s):
    with ExitStack() as ctx:
        ada = ctx.enter_context(nc.sbuf_tensor("ada", [P, 6, KT, 512], F32))
        cc = ctx.enter_context(nc.sbuf_tensor("cc", [P, 2, KT], F32))
        sc = ctx.enter_context(nc.sbuf_tensor("sc", [P, KT, 2], F32))
        bias = ctx.enter_context(nc.sbuf_tensor("ada_bias", [P, 24], F32))
        ng = ctx.enter_context(nc.sbuf_tensor("norm_g_cols", [P, KT], F32))
        mp = ctx.enter_context(nc.psum_tensor("mod_ps", [P, 24, 2], F32))
        c_in = ctx.enter_context(nc.semaphore("c_in"))
        ada_in = [ctx.enter_context(nc.semaphore(f"ada_in{j}")) for j in range(6)]
        small_in = ctx.enter_context(nc.semaphore("mod_small_in"))
        silu_c = ctx.enter_context(nc.semaphore("silu_c"))
        mod_done = ctx.enter_context(nc.semaphore("mod_done"))
        ones_ready = ctx.enter_context(nc.semaphore("ones_ready"))
        step = Signal(ctx, nc, "mod_step")
        mod, gs = s["mod"], s["gscale"]
        block = ctx.enter_context(nc.Block())

        @block.sync
        def _(sp):
            sp.dma_start(cc[:, 0, :], t["c"].rearrange("a (k p) -> p (a k)", p=P)).then_inc(c_in, 16)
            sp.dma_start(cc[:, 1, :], t["c_ctx"].rearrange("(k p) -> p k", p=P)).then_inc(c_in, 16)
            w = t["ada_w"].rearrange("l (k p) n -> p (l k) n", p=P)
            for j in range(6):
                sp.dma_start(ada[:, j, :, :], w[:, :, j * 512:(j + 1) * 512]).then_inc(ada_in[j], 16)
            sp.dma_start(bias[:], t["ada_b"].rearrange("l (m p) -> p (l m)", p=P)).then_inc(small_in, 16)
            sp.dma_start(ng[:], t["norm_g"].rearrange("l (m p) -> p (l m)", p=P)).then_inc(small_in, 16)

        @block.scalar
        def _(act):
            act.wait_ge(c_in, 32)
            nc.scalar.activation(sc[:, :, :].rearrange("p k s -> p s k"), cc[:], ACT.Silu).then_inc(silu_c, 1)

        @block.tensor
        def _(pe):
            pe.wait_ge(silu_c, 1)
            for m in range(24):
                if m % 4 == 0:
                    pe.wait_ge(ada_in[m // 4], 16)
                for k in range(KT):
                    last = nc.tensor.matmul(mp[:, m, :], ada[:, m // 4, k, (m % 4) * P:(m % 4 + 1) * P],
                                            sc[:, k, :], start=(k == 0), stop=(k == KT - 1))
            last.then_inc(mod_done, 1)

        @block.vector
        def _(dve):
            nc.vector.memset(s["eps"][:], EPS)
            nc.vector.memset(s["gn_eps"][:], GN_EPS)
            step.step(dve, nc.vector.memset(s["heads"][:], 0.0))
            for h in range(2):
                step.mark(nc.vector.memset(s["heads"][h * CH:(h + 1) * CH, h * CH:(h + 1) * CH], 1.0))
            dve.wait_ge(step.sem, step.n)
            nc.vector.tensor_scalar(s["head_mean"][:], s["heads"][:], 1.0 / CH, None, ALU.mult)
            dve.wait_ge(small_in, 32)
            dve.wait_ge(mod_done, 1)
            for v in range(2):
                step.mark(nc.vector.tensor_tensor(mod[:, v, :], mp[:, :, v], bias[:], ALU.add))
            dve.wait_ge(step.sem, step.n)
            for v in range(2):
                nc.vector.scalar_tensor_tensor(gs[:, v, :], mod[:, v, KT:2 * KT], 1.0, ng[:], ALU.add, ALU.mult)

        @block.gpsimd
        def _(pool):
            nc.gpsimd.memset(s["ones"][:], 1.0).then_inc(ones_ready, 1)
            pool.wait_ge(ones_ready, 1)
            nc.gpsimd.affine_select(out=s["ident"][:], in_=s["ones"][:], compare_op=ALU.is_equal, fill=0.0,
                                    base=0, pattern=[[-1, P]], channel_multiplier=1)


def projection_stage(nc, t, s):
    with ExitStack() as ctx:
        sb = lambda name, shape, dt=F32: ctx.enter_context(nc.sbuf_tensor(name, shape, dt))
        sem = lambda name: ctx.enter_context(nc.semaphore(name))
        h_hi, h_lo = sb("h_hi", [P, KT, NT], F32R), sb("h_lo", [P, KT, NT], F32R)
        x_in = sb("x_rows", [P, 4, D])
        h_st = sb("h_stage", [P, KT, BLK])
        z_st = sb("z_stage", [P, ZPAD])
        w_raw = sb("w_raw", [P, KT, P])
        w_hi, w_lo = sb("w_hi", [P, KT, P], F32R), sb("w_lo", [P, KT, P], F32R)
        ss, rt, rs = sb("sum_sq", [P, 4]), sb("rms", [P, 4]), sb("rstd", [P, 4])
        ps = ctx.enter_context(nc.psum_tensor("proj_ps", [P, 8, BLK], F32))
        x_loaded, rms_done, x_normed = sem("x_loaded"), sem("rms_done"), sem("x_normed")
        sq_done, rs_done = sem("sq_done"), sem("rs_done")
        turned, h_ready, hi_ready, lo_ready, h_stored = (sem("turned"), sem("h_ready"), sem("hi_ready"),
                                                         sem("lo_ready"), sem("h_stored"))
        w_loaded, w_hi_ready, w_lo_ready, w_free = sem("w_loaded"), sem("w_hi_ready"), sem("w_lo_ready"), sem("w_free")
        z_ps_ready, z_act, z_dve, z_stored = sem("z_ps_ready"), sem("z_act"), sem("z_dve"), sem("z_stored")
        block = ctx.enter_context(nc.Block())
        x_rows = t["x"].rearrange("a (n p) d -> p (a n) d", p=P)
        ctx_rows = t["ctx"].rearrange("a (n p) d -> p (a n) d", p=P)
        w_cols = t["w_in"].rearrange("l (k p) n -> p (l k) n", p=P)
        zT, hT = t["zT"], t["hT"]
        RUNS = [(T_RW, T_RG, True), (T_K, T_NG, True), (T_GU, T_K, False), (T_NG, T_RW, False), (T_RG, T_END, False),
                (T_END, T_ALL, False)]
        TURNS = T_ALL

        def over_blocks(eng, body):
            body(0, 2)
            with eng.Fori(1, NB + 1) as b:
                body(b, 4)

        def over_tiles(eng, body):
            turn = 0
            for a, e, with_ctx in RUNS:
                if turn == 0:
                    body(a, 0, with_ctx, False)
                    a, turn = a + 1, 1
                with eng.Fori(a, e) as tile:
                    body(tile, tile + (turn - a), with_ctx, a == T_END)
                turn += e - a

        @block.sync
        def _(sp):
            def load_x(b, n):
                if n == 4:
                    sp.wait_ge(turned, b * 8)
                src = ctx_rows if n == 2 else x_rows[:, bass.ds((b - 1) * 4, 4), :]
                sp.dma_start(x_in[:, 0:n, :], src).then_inc(x_loaded, 16)

            def store_h(b, n):
                if n == 4:
                    sp.wait_ge(h_ready, b * 8 + 8)
                    sp.dma_start(hT[:, :, bass.ds((b - 1) * BLK, BLK)].rearrange("k p t -> p k t"),
                                 h_st[:]).then_inc(h_stored, 16)

            load_x(0, 2)
            sp.dma_start(w_raw[:], w_cols[:, :, T_RW * P:(T_RW + 1) * P]).then_inc(w_loaded, 16)
            with sp.Fori(1, NB + 1) as b:
                load_x(b, 4)
                store_h(b, 4)

            def tile(col, turn, with_ctx, then, gates):
                if then is not None:
                    sp.wait_ge(w_hi_ready, turn * 8 + 8)
                    sp.wait_ge(w_lo_ready, turn * 8 + 8)
                    sp.dma_start(w_raw[:], w_cols[:, :, bass.ds(then * P, P)]).then_inc(w_loaded, 16)
                sp.wait_ge(z_act, turn * 2 + 3)
                sp.wait_ge(z_dve, turn * 2 + 3)
                lo = 0 if with_ctx else Z_LAT
                if gates:
                    sp.dma_start(t["gatesT"][bass.ds(col - T_END, 1), :, :].rearrange("a p t -> p (a t)"),
                                 z_st[:, Z_LAT:Z_LAT + SEQ]).then_inc(z_stored, 16)
                else:
                    sp.dma_start(zT[bass.ds(col, 1), :, lo:ZPAD].rearrange("a p t -> p (a t)"),
                                 z_st[:, lo:ZPAD]).then_inc(z_stored, 16)

            turn = 0
            for n, (a, e, with_ctx) in enumerate(RUNS):
                with sp.Fori(a, e - 1) as col:
                    tile(col, col + (turn - a), with_ctx, col + 1, a == T_END)
                turn += e - a
                tile(e - 1, turn - 1, with_ctx, RUNS[n + 1][0] if n + 1 < len(RUNS) else None, a == T_END)
            sp.wait_ge(z_stored, 16 * TURNS)
            sp.wait_ge(h_stored, 16 * NB)

        @block.gpsimd
        def _(pool):
            def split_lo(b, n):
                w = n * P
                lo = 0 if n == 2 else (b - 1) * BLK + CTX
                for k in range(KT):
                    pool.wait_ge(hi_ready, b * 8 + k + 1)
                    nc.gpsimd.tensor_tensor(h_lo[:, k, bass.ds(lo, w)], h_st[:, k, 0:w],
                                            h_hi[:, k, bass.ds(lo, w)].bitcast(F32),
                                            ALU.subtract).then_inc(lo_ready, 1)
            over_blocks(pool, split_lo)

        @block.scalar
        def _(act):
            def norm(b, n):
                act.wait_ge(x_loaded, b * 16 + 16)
                before = 0 if n == 2 else b * 4 - 2
                for j in range(n):
                    nc.scalar.activation(z_st[:, 0:D], x_in[:, j, :], ACT.Square,
                                         accum_out=ss[:, j:j + 1]).then_inc(sq_done, 1)
                    act.wait_ge(sq_done, before + j + 1)
                act.wait_ge(x_normed, b)
                nc.scalar.activation(rt[:, 0:n], ss[:, 0:n], ACT.Sqrt, bias=s["eps"][:], scale=1.0 / D).then_inc(rms_done, 1)
                lo = 0 if n == 2 else (b - 1) * BLK + CTX
                w = n * P
                for k in range(KT):
                    act.wait_ge(h_ready, b * 8 + k + 1)
                    nc.scalar.copy(h_hi[:, k, bass.ds(lo, w)], h_st[:, k, 0:w]).then_inc(hi_ready, 1)
            over_blocks(act, norm)

            def tile(col, turn, with_ctx, gates):
                first = isinstance(turn, int)
                act.wait_ge(w_loaded, turn * 16 + 16)
                for k in range(KT):
                    if k < KT - 1:
                        act.wait_ge(w_free, turn * 7 + k + 1)
                    elif not first:
                        act.wait_ge(z_ps_ready, turn * 5)
                    nc.scalar.copy(w_hi[:, k, :], w_raw[:, k, :]).then_inc(w_hi_ready, 1)
                if gates:
                    act.wait_ge(z_stored, turn * 16)
                    for m in range(NB):
                        act.wait_ge(z_ps_ready, turn * 5 + m + 1)
                        nc.scalar.activation(z_st[:, Z_LAT + m * BLK:Z_LAT + (m + 1) * BLK], ps[:, m, :],
                                             ACT.Sigmoid).then_inc(z_dve if m % 2 else z_act, 1)
                    return
                if not first:
                    act.wait_ge(z_stored, turn * 16)
                for m in (0, 2):
                    act.wait_ge(z_ps_ready, turn * 5 + m + 1)
                    nc.scalar.copy(z_st[:, Z_LAT + m * BLK:Z_LAT + (m + 1) * BLK], ps[:, m, :]).then_inc(z_act, 1)
            act.sem_inc(z_act, 1)
            over_tiles(act, tile)

        @block.vector
        def _(dve):
            def norm(b, n):
                dve.wait_ge(rms_done, b + 1)
                nc.vector.reciprocal(rs[:, 0:n], rt[:, 0:n]).then_inc(rs_done, 1)
                dve.wait_ge(rs_done, b + 1)
                for j in range(n):
                    last = nc.vector.tensor_scalar(x_in[:, j, :], x_in[:, j, :], rs[:, j:j + 1], None, ALU.mult)
                last.then_inc(x_normed, 1)
                v = 1 if n == 2 else 0
                w = n * P
                dve.wait_ge(lo_ready, b * 8)
                if n == 4:
                    dve.wait_ge(h_stored, b * 16 - 16)
                for k in range(KT):
                    dve.wait_ge(turned, b * 8 + k + 1)
                    nc.vector.tensor_scalar(h_st[:, k, 0:w], ps[:, k, 0:w], s["gscale"][:, v, k:k + 1],
                                            s["mod"][:, v, k:k + 1], ALU.mult, ALU.add).then_inc(h_ready, 1)
            over_blocks(dve, norm)

            def tile(col, turn, with_ctx, gates):
                first = isinstance(turn, int)
                for k in range(KT):
                    dve.wait_ge(w_hi_ready, turn * 8 + k + 1)
                    nc.vector.tensor_tensor(w_lo[:, k, :], w_raw[:, k, :], w_hi[:, k, :].bitcast(F32),
                                            ALU.subtract).then_inc(w_lo_ready, 1)
                if gates:
                    return
                if not first:
                    dve.wait_ge(z_stored, turn * 16)
                for m in (1, 3):
                    dve.wait_ge(z_ps_ready, turn * 5 + m + 1)
                    ins = nc.vector.tensor_copy(z_st[:, Z_LAT + m * BLK:Z_LAT + (m + 1) * BLK], ps[:, m, :])
                    if m == 1 or not with_ctx:
                        ins.then_inc(z_dve, 1)
                if with_ctx:
                    dve.wait_ge(z_ps_ready, turn * 5 + 5)
                    nc.vector.tensor_copy(z_st[:, Z_CTX:Z_CTX + CTX], ps[:, 4, 0:CTX]).then_inc(z_dve, 1)
            for col in (0, Z_CTX + CTX, ZPAD - 1):
                last = nc.vector.memset(z_st[:, col:col + 1], 0.0)
            last.then_inc(z_dve, 1)
            over_tiles(dve, tile)

        @block.tensor
        def _(pe):
            def turn_rows(b, n):
                pe.wait_ge(x_normed, b + 1)
                for k in range(KT):
                    if n == 4:
                        pe.wait_ge(h_ready, b * 8 + k - 7)
                    for j in range(n):
                        last = nc.tensor.transpose(ps[:, k, j * P:(j + 1) * P], x_in[:, j, k * P:(k + 1) * P],
                                                   s["ident"][:])
                    last.then_inc(turned, 1)
            over_blocks(pe, turn_rows)
            pe.wait_ge(lo_ready, 8 * (NB + 1))
            pe.sem_inc(w_free, 7)

            def product(m, k, w, h, first, last):
                cols = slice(CTX + m * BLK, CTX + (m + 1) * BLK) if m < NB else slice(0, CTX)
                out = ps[:, m, :] if m < NB else ps[:, m, 0:CTX]
                return nc.tensor.matmul(out, w[:, k, :], h[:, k, cols], start=first, stop=last)

            def tile(col, turn, with_ctx, gates):
                first = isinstance(turn, int)
                ms = range(NB + 1) if with_ctx else range(NB)
                for k in range(KT):
                    pe.wait_ge(w_hi_ready, turn * 8 + k + 1)
                    pe.wait_ge(w_lo_ready, turn * 8 + k + 1)
                    if 0 < k < KT - 1:
                        for m in ms:
                            product(m, k, w_hi, h_hi, False, False)
                            product(m, k, w_hi, h_lo, False, False)
                        for m in ms:
                            last = product(m, k, w_lo, h_hi, False, False)
                        last.then_inc(w_free, 1)
                        continue
                    for m in ms:
                        if k == 0:
                            if not first or m > 1:
                                pe.wait_ge(z_dve if m % 2 or m == NB else z_act, turn * 2 + (m > 1))
                        product(m, k, w_hi, h_hi, k == 0, False)
                        product(m, k, w_hi, h_lo, False, False)
                        last = product(m, k, w_lo, h_hi, False, k == KT - 1)
                        if k == KT - 1:
                            last.then_inc(z_ps_ready, 2 if m == NB - 1 and not with_ctx else 1)
                    if k == 0:
                        last.then_inc(w_free, 1)
            over_tiles(pe, tile)


class Results:

    def __init__(self, ctx, nc, name, results):
        self.sem = ctx.enter_context(nc.semaphore(name))
        self.at = {r: n + 1 for n, r in enumerate(results)}
        self.each = len(results)
        assert len(self.at) == self.each
        self.names, self.n = results, 0

    def done(self, ins, result):
        assert self.names[self.n % self.each] == result, (self.names[self.n % self.each], result)
        self.n += 1
        ins.then_inc(self.sem, 1)

    def after(self, eng, turn, result):
        eng.wait_ge(self.sem, turn * self.each + self.at[result])

    def earlier(self, eng, turn, result):
        if not isinstance(turn, int) or turn > 0:
            self.after(eng, turn - 1, result)

    def own(self, eng, turn, ins, result):
        self.done(ins, result)
        self.after(eng, turn, result)


NC_ALL = NT // CH
RB = 256
LEVELS = (1, 2, 4, 8, 16, 32)
DECAY = -float(np.exp(-0.5))


def recurrence_local_stage(nc, t, s, chain):
    with ExitStack() as ctx:
        sb = lambda name, shape, dt=F32: ctx.enter_context(nc.sbuf_tensor(name, shape, dt))
        sem = lambda name: ctx.enter_context(nc.semaphore(name))
        zin, zf, nbr = sb("z_halo", [P, 7, RB + 2]), sb("z_mixed", [P, 7, RB]), sb("neighbours", [P, 7, RB])
        th = sb("tanh_w_lo", [CH, RB])
        kkr, ksq, kk, k1, k2, rrk, kds = (sb(n, [P, 2, RB]) for n in
                                          ("kk_raw", "kk_sq", "kk_unit", "k_1", "k_2", "r_rk", "kd_sum"))
        lw, aa, L, Lx, exc = (sb(n, [P, 2, RB]) for n in ("log_w", "a_rate", "log_run", "log_before", "log_exc"))
        inc = lw
        EI, EX, EN = (sb(n, [P, 2, RB]) for n in ("e_inc", "e_exc", "e_neg"))
        kka, kd = sb("kk_a", [P, 2, RB]), sb("k_d", [P, 2, RB])
        AR = sb("a_r_hat", [P, 2, 2, 2, RB])
        Bh, Kh = sb("b_hat", [P, 2, 2, RB]), sb("k_hat", [P, 2, 2, RB])
        Vt = sb("v_rows", [P, 2, 2 * P])
        Bt, Kt = sb("b_rows", [P, 2, 2 * P]), sb("k_rows", [P, 2, 2 * P])
        MB, MK = sb("m_b", [P, 2, 4, 2, P]), sb("m_k", [P, 2, 4, 2, P])
        X, Z, G = sb("inv", [P, 2, 4, P]), sb("inv_t", [P, 2, 4, P]), sb("inv_g", [P, 2, 4, P])
        WI, W = sb("w_in_rows", [P, 2, 4, P]), sb("w_rows", [P, 2, 4, P])
        gst, yst, bst = sb("g_stage", [P, 2, RB]), sb("y_stage", [P, 2, RB]), sb("bonus_stage", [P, 2, RB])
        lev = sb("level_masks", [P, 2, len(LEVELS), P])
        tri = sb("chunk_masks", [P, 2, 2, P])
        run1, i64, J = sb("scan_keep", [P, 2, RB]), sb("ident_64", [P, CH]), s["heads"]
        mu, omu, hmu = sb("mu", [P, 7]), sb("one_less_mu", [P, 7]), sb("half_mu", [P, 7])
        par = sb("rw_params", [P, 7, 2])
        hpar = sb("rw_half_params", [P, 4, 2])
        lora = sb("lora", [P, 2, 2 * P])
        ps = ctx.enter_context(nc.psum_tensor("rw_ps", [P, 8, BLK], F32))
        consts_in, consts_set, masks = sem("rw_params_in"), Signal(ctx, nc, "rw_consts_set"), Signal(ctx, nc, "rw_masks")
        z_in, g_stored, y_stored, b_stored = sem("rw_z_in"), sem("g_stored"), sem("y_stored"), sem("bonus_stored")
        prep_v = Results(ctx, nc, "prep_vector", ["mix6"] + [f"mix{j}" for j in range(6)]
                         + ["kkr0", "kkr1", "ksq", "k20", "k21", "k1", "rrk0", "rrk1"]
                         + sum(([f"{n}{d}" for n in ["lw", "L", "Lx"] + ["inc", "exc"] * d + ["aa", "kdm", "kd", "kds"]]
                                + ["kmax", "krec", "kk"] * (1 - d) + [f"{n}{d}" for n in ["kka", "R", "A", "B", "K"]]
                                for d in range(2)), []) + ["bt", "bonus"])
        main_v = Results(ctx, nc, "main_vector", sum(([f"{n}{d}" for n in
                         sum(([f"MB0.{g}.", f"MB1.{g}.", f"MI.{g}.", f"Xa.{g}.", f"Xb.{g}.", f"Za.{g}.", f"Zb.{g}.", f"MK0.{g}.", f"MK1.{g}."]
                              for g in range(2)), [])
                         + [f"G{v}.{g}." for v in range(1, 6) for g in range(2)]
                         + ["Gs0.", "Gs1.", "P0.", "Q0.", "P1.", "Q1."]] for d in range(2)), []))
        prep_a = Results(ctx, nc, "prep_scalar", [f"scaled{j}" for j in range(7)] + ["th"]
                         + sum(([f"{n}{d}" for n in ["tw0.", "tw1.", "ta0.", "ta1."]] + ["knorm"] * (1 - d)
                                + [f"{n}{d}" for n in ["EI", "EX", "EN", "tot"]] for d in range(2)), []))
        main_a = Results(ctx, nc, "main_scalar", sum(([f"{n}{d}" for n in
                         ["X1.0.", "Z1.0.", "X1.1.", "Z1.1.", "At0.", "Bt0.", "X2.0.", "Z2.0.", "X2.1.", "Z2.1.", "At1.", "Bt1.",
                          "X3.0.", "Z3.0.", "X3.1.", "Z3.1.", "Kt.", "X4.0.", "Z4.0.", "X4.1.", "Z4.1."] + ["V."] * (1 - d)
                         + ["Z5.0.", "MV0.0.", "MV1.0.", "Z5.1.", "MV0.1.", "MV1.1.", "W0.", "W1.", "Y0.", "Y1."]]
                                                      for d in range(2)), []))
        prep_p = Results(ctx, nc, "prep_products", ["tw0", "ta0", "ksum", "tw1", "ta1", "bonus"])
        main_p = Results(ctx, nc, "main_products", sum(([f"{n}{d}" for n in ["SB0.", "SM0.", "SK0.", "SB1.", "SM1.", "SK1."]
                         + sum(([f"G{v}.0.", f"G{v}.1.", f"T{v}."] + [f"{x}{v}.{g}." for g in range(2) for x in "XZ"] for v in range(1, 4)), [])
                         + ["G4.0.", "G4.1."] + ["T4."] * (1 - d) + [f"{x}4.{g}." for g in range(2) for x in "XZ"]
                         + ["G5.0.", "G5.1.", "Z5.0.", "MV0.", "Z5.1.", "MV1.", "W0.", "W1.", "GY0.", "GY1.", "PQ"]]
                                                        for d in range(2)), []))
        nbr_set = sem("neighbours_set")
        Pst, Qst, tot = chain["P"], chain["Q"], chain["tot"]
        block = ctx.enter_context(nc.Block())

        NBLK = NT // RB

        def units(eng, prologue, unit):
            prologue()
            unit(0, 0, (0, 1))
            unit(0, 1, (1, 0))
            with eng.Fori(1, NBLK - 1) as n:
                unit(n, 0, (n, 1))
                unit(n, 1, (n + 1, 0))
            unit(NBLK - 1, 0, (NBLK - 1, 1))
            unit(NBLK - 1, 1, None)

        @block.sync
        def _(sp):
            row = lambda a: a.rearrange("l (m p) -> p (l m)", p=P)
            sp.dma_start(mu[:], row(t["rw_mu"])).then_inc(consts_in, 16)
            sp.dma_start(par[:, 0, :], row(t["rw_kk"])).then_inc(consts_in, 16)
            sp.dma_start(par[:, 1, :], row(t["rw_ka"])).then_inc(consts_in, 16)
            sp.dma_start(par[:, 2, :], t["rw_rk"].rearrange("l (m h) n -> (h n) (l m)", h=2)).then_inc(consts_in, 16)
            for d in range(2):
                sp.dma_start(par[:, 3 + d, :], row(t["rw_w0"][:, d, :])).then_inc(consts_in, 16)
                sp.dma_start(par[:, 5 + d, :], row(t["rw_a0"][:, d, :])).then_inc(consts_in, 16)
                sp.dma_start(lora[0:CH, d, :], t["rw_w2"][0, d, :, :]).then_inc(consts_in, 16)
                sp.dma_start(lora[CH:P, d, :], t["rw_a2"][0, d, :, :]).then_inc(consts_in, 16)

            def load(n):
                if not (isinstance(n, int) and n == 0):
                    sp.wait_ge(nbr_set, n)
                    prep_a.after(sp, n - 1, "scaled6")
                c0 = 0 if isinstance(n, int) and n == 0 else n * RB + 1
                sp.dma_start(zin[:], t["zT"][T_RW:T_RG, :, bass.ds(c0, RB + 2)].rearrange("k p t -> p k t")).then_inc(z_in, 16)

            def turn(n, more):
                for d in range(2):
                    if d and more:
                        load(n + 2)
                    main_v.after(sp, n, f"Gs1.{d}")
                    sp.dma_start(t["gT"][d, :, :, bass.ds(n * RB, RB)].rearrange("m p t -> p m t"), gst[:]).then_inc(g_stored, 16)
                    main_a.after(sp, n, f"Y1.{d}")
                    sp.dma_start(t["yT"][d, :, :, bass.ds(n * RB, RB)].rearrange("m p t -> p m t"), yst[:]).then_inc(y_stored, 16)
                    if d == 0:
                        prep_v.after(sp, n, "bonus")
                        sp.dma_start(t["bonusT"][:, :, bass.ds(n * RB, RB)].rearrange("m p t -> p m t"), bst[:]).then_inc(b_stored, 16)
            load(0)
            load(1)
            turn(0, True)
            with sp.Fori(1, NBLK - 2) as n:
                turn(n, True)
            turn(NBLK - 2, False)
            turn(NBLK - 1, False)
            sp.wait_ge(g_stored, 16 * 2 * NBLK)
            sp.wait_ge(y_stored, 16 * 2 * NBLK)
            sp.wait_ge(b_stored, 16 * NBLK)

        @block.gpsimd
        def _(pool):
            masks.step(pool, nc.gpsimd.memset(lev[:], 0.0))
            one = s["ones"]
            for v, b in enumerate(LEVELS):
                n = P // (2 * b)
                view = lambda m: m.rearrange("p (n h b) -> p n h b", h=2, b=b)
                for d in range(2):
                    o = view(lev[:, d, v, :])[:, :, d, :]
                    masks.step(pool, nc.gpsimd.affine_select(out=o, in_=view(one[:, :])[:, :, 0, :], compare_op=ALU.is_ge, fill=0.0,
                                                             base=-b * (1 - d), pattern=[[-2 * b, n], [0, b]], channel_multiplier=1))
                    masks.step(pool, nc.gpsimd.affine_select(out=o, in_=o, compare_op=ALU.is_ge, fill=0.0, base=b * (2 - d) - 1,
                                                             pattern=[[2 * b, n], [0, b]], channel_multiplier=-1))
            for d in range(2):
                for incl in range(2):
                    o = tri[:, d, incl, :].rearrange("p (c j) -> p c j", c=2)
                    src = one[:, :].rearrange("p (c j) -> p c j", c=2)
                    op = ALU.is_ge if incl else ALU.is_gt
                    sign = 1 - 2 * d
                    masks.step(pool, nc.gpsimd.affine_select(out=o, in_=src, compare_op=op, fill=0.0, base=0,
                                                             pattern=[[CH * sign, 2], [sign, CH]], channel_multiplier=-sign))
                    masks.step(pool, nc.gpsimd.affine_select(out=o, in_=o, compare_op=ALU.is_ge, fill=0.0, base=0,
                                                             pattern=[[-CH, 2], [0, CH]], channel_multiplier=1))
                    masks.step(pool, nc.gpsimd.affine_select(out=o, in_=o, compare_op=ALU.is_ge, fill=0.0, base=CH - 1,
                                                             pattern=[[CH, 2], [0, CH]], channel_multiplier=-1))
            for h in range(2):
                masks.step(pool, nc.gpsimd.affine_select(out=i64[h * CH:(h + 1) * CH, :], in_=one[h * CH:(h + 1) * CH, 0:CH],
                                                         compare_op=ALU.is_equal, fill=0.0, base=0, pattern=[[-1, CH]],
                                                         channel_multiplier=1))

            def neighbours(n):
                pool.wait_ge(z_in, n * 16 + 16)
                if not (isinstance(n, int) and n == 0):
                    prep_v.after(pool, n - 1, "mix5")
                nc.gpsimd.tensor_tensor(nbr[:], zin[:, :, 0:RB], zin[:, :, 2:RB + 2], ALU.add).then_inc(nbr_set, 1)
            neighbours(0)
            with pool.Fori(1, NBLK) as n:
                neighbours(n)

        N_MASKS = 1 + 4 * len(LEVELS) + 12 + 2
        V, A, T = nc.vector, nc.scalar, nc.tensor
        flat = lambda a: a.rearrange("p a b -> p (a b)")

        @block.vector
        def _(dve):
            dve.wait_ge(consts_in, 16 * 12)
            consts_set.mark(V.memset(run1[:], 1.0))
            dve.wait_ge(consts_set.sem, consts_set.n)
            consts_set.mark(V.memset(run1[:].rearrange("p a (c j) -> p a c j", j=CH)[:, :, :, 0:1], 0.0))
            consts_set.mark(V.tensor_scalar(omu[:], mu[:], -1.0, 1.0, ALU.mult, ALU.add))
            consts_set.mark(V.tensor_scalar(hmu[:], mu[:], 0.5, None, ALU.mult))
            consts_set.mark(V.tensor_scalar(hpar[:], par[:, 3:7, :], 0.5, None, ALU.mult))
            dve.wait_ge(consts_set.sem, consts_set.n)
            dve.wait_ge(masks.sem, N_MASKS)
            for d in range(2):
                ident = s["ident"][:, :].rearrange("p (o t) -> p o t", o=1).to_broadcast([P, len(LEVELS) - 1, P])
                consts_set.step(dve, V.tensor_tensor(lev[:, d, 1:, :], lev[:, d, 1:, :], ident, ALU.add))

            def mix(n):
                dve.wait_ge(nbr_set, n + 1)
                for j in (6, 0, 1, 2, 3, 4, 5):
                    prep_a.after(dve, n, f"scaled{j}")
                    prep_v.own(dve, n, V.scalar_tensor_tensor(zf[:, j, :], nbr[:, j, :], hmu[:, j:j + 1], zf[:, j, :], ALU.mult, ALU.add), f"mix{j}")

            def keys(n):
                own = lambda ins, name: prep_v.own(dve, n, ins, name)
                for p in range(2):
                    own(V.tensor_scalar(kkr[:, p, :], zf[:, 2 + p, :], par[:, 0, p:p + 1], None, ALU.mult), f"kkr{p}")
                own(V.tensor_tensor(ksq[:], kkr[:], kkr[:], ALU.mult), "ksq")
                for p in range(2):
                    own(V.tensor_scalar(k2[:, p, :], zf[:, 2 + p, :], par[:, 1, p:p + 1], None, ALU.mult), f"k2{p}")
                own(V.tensor_tensor(k1[:], zf[:, 2:4, :], k2[:], ALU.subtract), "k1")
                for p in range(2):
                    own(V.tensor_scalar(rrk[:, p, :], zf[:, p, :], par[:, 2, p:p + 1], None, ALU.mult), f"rrk{p}")

            def decay(n, d):
                own = lambda ins, name: prep_v.own(dve, n, ins, f"{name}{d}")
                prep_a.after(dve, n, f"tw1.{d}")
                own(V.tensor_scalar(lw[:], lw[:], 0.5 * DECAY, 0.5 * DECAY, ALU.mult, ALU.add), "lw")
                own(V.tensor_tensor_scan(flat(L[:]), flat(run1[:]), flat(lw[:]), 0.0, ALU.mult, ALU.add), "L")
                own(V.tensor_tensor(Lx[:], L[:], lw[:], ALU.subtract), "Lx")
                if d:
                    chunks = lambda a: a.rearrange("p a (c j) -> p (a c) j", j=CH)
                    end = chunks(L[:])[:, :, CH - 1:CH].to_broadcast([P, 8, CH])
                    own(V.tensor_tensor(chunks(inc[:]), end, chunks(Lx[:]), ALU.subtract), "inc")
                    own(V.tensor_tensor(chunks(exc[:]), end, chunks(L[:]), ALU.subtract), "exc")

            def rates(n, d):
                own = lambda ins, name: prep_v.own(dve, n, ins, f"{name}{d}")
                prep_a.after(dve, n, f"ta1.{d}")
                own(V.tensor_scalar(aa[:], aa[:], 0.5, 0.5, ALU.mult, ALU.add), "aa")
                own(V.tensor_tensor(kd[:], k2[:], aa[:], ALU.mult), "kdm")
                own(V.tensor_tensor(kd[:], kd[:], k1[:], ALU.add), "kd")
                own(V.tensor_copy(kds[:], kd[:]) if d == 0 else V.tensor_tensor(kds[:], kds[:], kd[:], ALU.add), "kds")

            def unit_keys(n):
                own = lambda ins, name: prep_v.own(dve, n, ins, name)
                prep_a.after(dve, n, "knorm")
                own(V.tensor_scalar(ksq[:], ksq[:], 1e-12, None, ALU.max), "kmax")
                own(V.reciprocal(ksq[:], ksq[:]), "krec")
                own(V.tensor_tensor(kk[:], kkr[:], ksq[:], ALU.mult), "kk")

            def hats(n, d):
                own = lambda ins, name: prep_v.own(dve, n, ins, f"{name}{d}")
                own(V.tensor_tensor(kka[:], kk[:], aa[:], ALU.mult), "kka")
                prep_a.after(dve, n, f"EN{d}")
                own(V.tensor_tensor(AR[:, d, 1, :, :], zf[:, 0:2, :], EI[:], ALU.mult), "R")
                own(V.scalar_tensor_tensor(AR[:, d, 0, :, :], kk[:], -1.0, EX[:], ALU.mult, ALU.mult), "A")
                own(V.tensor_tensor(Bh[:, d, :, :], kka[:], EN[:], ALU.mult), "B")
                own(V.tensor_tensor(Kh[:, d, :, :], kd[:], EN[:], ALU.mult), "K")

            def prologue():
                mix(0)
                keys(0)
                decay(0, 0)
                rates(0, 0)
                unit_keys(0)
                hats(0, 0)

            heads = lambda m: m.rearrange("p (o t) -> p o t", o=1).to_broadcast([P, 4, P])
            of_parity = lambda a, q: a.rearrange("p (m h) t -> p m h t", h=2)[:, :, q, :]
            bank = lambda b: ps[:, b, :].rearrange("p (h m t) -> p h m t", h=2, m=2)
            per_head = lambda b: ps[:, b, :].rearrange("p (h t) -> p h t", h=4)

            def unit(n, d, nxt):
                own = lambda ins, name: main_v.own(dve, n, ins, name)
                strict = tri[:, d, :, :].rearrange("p m (o t) -> p o m t", o=1).to_broadcast([P, 2, 2, P])
                for g in range(2):
                    main_p.after(dve, n, f"SB{g}.{d}")
                    for q in range(2):
                        for m in range(2):
                            ins = V.tensor_tensor(of_parity(MB[:, g, :, m, :], q), bank(2 + q)[:, :, m, :], strict[:, :, m, :], ALU.mult)
                            if m:
                                own(ins, f"MB{q}.{g}.{d}")
                    own(V.tensor_tensor(MB[:, g, :, 0, :], MB[:, g, :, 0, :], heads(s["ident"][:, :]), ALU.add), f"MI.{g}.{d}")
                    main_p.after(dve, n, f"SM{g}.{d}")
                    for q in range(2):
                        ab = ps[:, q, g * 256:(g + 1) * 256].rearrange("p (m t) -> p m t", m=2)
                        ins = V.tensor_tensor(of_parity(X[:, g, :, :], q), ab, heads(lev[:, d, 0, :])[:, 0:2, :], ALU.mult)
                    own(ins, f"Xa.{g}.{d}")
                    own(V.tensor_tensor(X[:, g, :, :], X[:, g, :, :], heads(s["ident"][:, :]), ALU.add), f"Xb.{g}.{d}")
                    own(V.tensor_tensor(Z[:, g, :, :], MB[:, g, :, 0, :], heads(lev[:, 1 - d, 0, :]), ALU.mult), f"Za.{g}.{d}")
                    own(V.tensor_tensor(Z[:, g, :, :], Z[:, g, :, :], heads(s["ident"][:, :]), ALU.add), f"Zb.{g}.{d}")
                    main_p.after(dve, n, f"SK{g}.{d}")
                    for q in range(2):
                        for m in range(2):
                            ins = V.tensor_tensor(of_parity(MK[:, g, :, m, :], q), bank(4 + q)[:, :, m, :], strict[:, :, m, :], ALU.mult)
                            if m:
                                own(ins, f"MK{q}.{g}.{d}")
                for v in range(1, 6):
                    for g in range(2):
                        main_p.after(dve, n, f"G{v}.{g}.{d}")
                        own(V.tensor_tensor(G[:, g, :, :], per_head(g), heads(lev[:, d, v, :]), ALU.mult), f"G{v}.{g}.{d}")
                    if nxt is None:
                        continue
                    if v == 1 and d:
                        mix(nxt[0])
                    if v == 2 and d:
                        keys(nxt[0])
                    if v == 3:
                        decay(*nxt)
                    if v == 4:
                        rates(*nxt)
                if nxt:
                    if d:
                        unit_keys(nxt[0])
                    hats(*nxt)
                    if d == 0:
                        prep_v.own(dve, n, V.tensor_tensor(kds[:], kds[:], rrk[:], ALU.mult), "bt")
                for g in range(2):
                    main_p.after(dve, n, f"GY{g}.{d}")
                    main_a.after(dve, n, f"Y{g}.{d}")
                    if g == 0 and not (isinstance(n, int) and n == 0 and d == 0):
                        dve.wait_ge(g_stored, (n * 2 + d) * 16)
                    gy = ps[:, 4 + g, :].rearrange("p (q m t) -> p q m t", q=2, m=2)
                    own(V.tensor_tensor(gst[:, :, g * P:(g + 1) * P], gy[:, 0, :, :], AR[:, d, 1, :, g * P:(g + 1) * P], ALU.add), f"Gs{g}.{d}")
                main_p.after(dve, n, f"PQ{d}")
                prep_a.after(dve, n, f"tot{d}")
                for c in range(2):
                    pq = ps[:, c, :].rearrange("p (g q m j) -> p g q m j", g=2, q=2, m=2)
                    to = lambda st: st[:, d, bass.ds(n * 4, 4), :, :].rearrange("p (g c) m j -> p g c m j", c=2)[:, :, c, :, :]
                    tt = tot[:, d, bass.ds(n * 4, 4), :].rearrange("p (g c) (m o) -> p g c m o", c=2, o=1)[:, :, c, :, :]
                    eye = i64[:, :].rearrange("p (a b j) -> p a b j", a=1, b=1).to_broadcast([P, 2, 2, CH])
                    own(V.tensor_tensor(to(Pst), pq[:, :, 0, :, :], eye, ALU.add), f"P{c}.{d}")
                    own(V.tensor_tensor(to(Qst), pq[:, :, 1, :, :], tt.to_broadcast([P, 2, 2, CH]), ALU.mult), f"Q{c}.{d}")
                if d == 0:
                    prep_p.after(dve, n, "bonus")
                    if not (isinstance(n, int) and n == 0):
                        dve.wait_ge(b_stored, n * 16)
                    prep_v.own(dve, n, V.tensor_tensor(bst[:], ps[:, 6, :].rearrange("p (m t) -> p m t", m=2), zf[:, 4:6, :], ALU.mult), "bonus")
            units(dve, prologue, unit)

        @block.scalar
        def _(act):
            act.wait_ge(consts_set.sem, 5)

            def scaled(n):
                act.wait_ge(z_in, n * 16 + 16)
                prep_v.earlier(act, n, "bonus")
                for j in range(7):
                    prep_a.own(act, n, A.activation(zf[:, j, :], zin[:, j, 1:RB + 1], ACT.Copy, scale=omu[:, j:j + 1]), f"scaled{j}")

            def tanh_lo(n):
                prep_v.after(act, n, "mix6")
                prep_a.own(act, n, A.activation(th[:], zf[0:CH, 6, :], ACT.Tanh), "th")

            def rate(n, d, name, to, bias):
                prep_p.after(act, n, f"{name}{d}")
                for m in range(2):
                    prep_a.own(act, n, A.activation(to[:, m, :], ps[:, 6, m * RB:(m + 1) * RB], ACT.Tanh, scale=0.5, bias=hpar[:, bias + d, m:m + 1]),
                               f"{name}{m}.{d}")

            def key_norm(n):
                prep_p.after(act, n, "ksum")
                prep_a.own(act, n, A.activation(flat(ksq[:]), ps[:, 7, :], ACT.Sqrt), "knorm")

            def exps(n, d):
                own = lambda ins, name: prep_a.own(act, n, ins, f"{name}{d}")
                prep_v.after(act, n, "exc1" if d else "Lx0")
                own(A.activation(EI[:], (inc if d else L)[:], ACT.Exp), "EI")
                own(A.activation(EX[:], (exc if d else Lx)[:], ACT.Exp), "EX")
                own(A.activation(EN[:], (inc if d else L)[:], ACT.Exp, scale=-1.0), "EN")
                edge = 0 if d else CH - 1
                whole = EI[:].rearrange("p m (c j) -> p c m j", j=CH)[:, :, :, edge:edge + 1]
                own(A.copy(tot[:, d, bass.ds(n * 4, 4), :].rearrange("p c (m o) -> p c m o", o=1), whole), "tot")

            def prologue():
                scaled(0)
                tanh_lo(0)
                rate(0, 0, "tw", lw, 0)
                rate(0, 0, "ta", aa, 2)
                key_norm(0)
                exps(0, 0)

            per_head = lambda b: ps[:, b, :].rearrange("p (h t) -> p h t", h=4)

            def unit(n, d, nxt):
                own = lambda ins, name: main_a.own(act, n, ins, f"{name}{d}")
                if nxt and d:
                    scaled(nxt[0])

                def level(v, g):
                    for x, to in (("X", X), ("Z", Z)):
                        if v < 5 or x == "Z":
                            main_p.after(act, n, f"{x}{v}.{g}.{d}")
                            own(A.copy(to[:, g, :, :], per_head((2 if x == "X" else 4) + g)), f"{x}{v}.{g}.")

                def kept_rows(v):
                    main_p.after(act, n, f"T{v}.{d}")
                    if v < 3:
                        own(A.copy(WI[:, v - 1, :, 0:CH], ps[:, 7, 0:256].rearrange("p (h j) -> p h j", h=4)), f"At{v - 1}.")
                        own(A.copy(Bt[:, v - 1, :], ps[:, 7, 256:512]), f"Bt{v - 1}.")
                    else:
                        own(A.copy(flat((Kt if v == 3 else Vt)[:]), ps[:, 7, :]), "Kt." if v == 3 else "V.")
                for v in range(1, 5):
                    if v == 2 and nxt and d:
                        tanh_lo(nxt[0])
                    if v == 3 and nxt:
                        rate(*nxt, "tw", lw, 0)
                    if v == 4 and nxt:
                        rate(*nxt, "ta", aa, 2)
                    level(v, 0)
                    level(v, 1)
                    if v < 4 or d == 0:
                        kept_rows(v)
                if nxt:
                    if d:
                        key_norm(nxt[0])
                    exps(*nxt)
                for g in range(2):
                    level(5, g)
                    main_p.after(act, n, f"MV{g}.{d}")
                    for q in range(2):
                        mv = ps[:, g, :].rearrange("p (m h t) -> p m h t", m=2, h=2)[:, :, q, q * CH:(q + 1) * CH]
                        own(A.copy(WI[:, g, :, :].rearrange("p (m h) t -> p m h t", h=2)[:, :, q, CH:P], mv), f"MV{q}.{g}.")
                for g in range(2):
                    main_p.after(act, n, f"W{g}.{d}")
                    own(A.copy(W[:, g, :, :], per_head(2 + g)), f"W{g}.")
                for g in range(2):
                    main_p.after(act, n, f"GY{g}.{d}")
                    if g == 0 and not (isinstance(n, int) and n == 0 and d == 0):
                        act.wait_ge(y_stored, (n * 2 + d) * 16)
                    own(A.copy(yst[:, :, g * P:(g + 1) * P], ps[:, 4 + g, 256:512].rearrange("p (m t) -> p m t", m=2)), f"Y{g}.")
            units(act, prologue, unit)

        @block.tensor
        def _(pe):
            mm = lambda o, l, r, start=True, stop=True: T.matmul(o, l, r, start=start, stop=stop)
            half = lambda h: slice((h % 2) * CH, (h % 2 + 1) * CH)

            def w_lora(n, d):
                prep_a.after(pe, n, "th" if d == 0 else "ta1.0")
                if d == 0:
                    prep_v.earlier(pe, n, "bonus")
                for p in range(2):
                    last = mm(ps[:, 6, p * RB:(p + 1) * RB], lora[0:CH, d, p * P:(p + 1) * P], th[:])
                prep_p.done(last, f"tw{d}")

            def a_lora(n, d):
                prep_a.after(pe, n, f"tw1.{d}")
                for p in range(2):
                    last = mm(ps[:, 6, p * RB:(p + 1) * RB], lora[CH:P, d, p * P:(p + 1) * P], zf[CH:P, 6, :])
                prep_p.done(last, f"ta{d}")

            def key_sums(n):
                prep_v.after(pe, n, "ksq")
                prep_p.done(mm(ps[:, 7, :], J[:], flat(ksq[:])), "ksum")

            def prologue():
                w_lora(0, 0)
                a_lora(0, 0)
                key_sums(0)

            def unit(n, d, nxt):
                done = lambda ins, name: main_p.done(ins, f"{name}{d}")

                def before(results, name):
                    if d:
                        results.after(pe, n, f"{name}.0")
                    else:
                        results.earlier(pe, n, f"{name}.1")
                prep_v.after(pe, n, f"K{d}")
                before(main_a, "W1")
                for g in range(2):
                    tok = slice(g * P, (g + 1) * P)
                    if g:
                        main_v.after(pe, n, f"MB1.0.{d}")
                    for p in range(2):
                        for h in (2 * p, 2 * p + 1):
                            last = mm(ps[:, 2 + h % 2, p * 256:(p + 1) * 256], Bh[half(h), d, p, tok], AR[half(h), d, :, p, tok])
                    done(last, f"SB{g}.")
                    if g:
                        main_v.after(pe, n, f"Xa.0.{d}")
                    else:
                        before(main_v, "Q1")
                    for h in range(4):
                        p = h // 2
                        last = mm(ps[:, h % 2, g * 256 + p * P:g * 256 + (p + 1) * P], AR[half(h), d, 0, p, tok], Bh[half(h), d, p, tok])
                    done(last, f"SM{g}.")
                    if g:
                        main_v.after(pe, n, f"MK1.0.{d}")
                    else:
                        before(main_a, "Y1")
                    for p in range(2):
                        for h in (2 * p, 2 * p + 1):
                            last = mm(ps[:, 4 + h % 2, p * 256:(p + 1) * 256], Kh[half(h), d, p, tok], AR[half(h), d, :, p, tok])
                    done(last, f"SK{g}.")

                def turn_rows(v):
                    if v == 1:
                        if d:
                            main_a.after(pe, n, "V.0")
                        else:
                            prep_a.after(pe, n, "knorm")
                    else:
                        main_a.after(pe, n, f"Bt0.{d}" if v == 2 else f"Bt1.{d}" if v == 3 else f"Kt.{d}")
                    if v < 3:
                        tok = slice((v - 1) * P, v * P)
                        for p in range(2):
                            T.transpose(ps[:, 7, p * P:(p + 1) * P], AR[:, d, 0, p, tok], s["ident"][:])
                        for p in range(2):
                            last = T.transpose(ps[:, 7, 256 + p * P:256 + (p + 1) * P], Bh[:, d, p, tok], s["ident"][:])
                    else:
                        for g in range(2):
                            for p in range(2):
                                src = Kh[:, d, p, g * P:(g + 1) * P] if v == 3 else zf[:, 4 + p, g * P:(g + 1) * P]
                                last = T.transpose(ps[:, 7, g * 256 + p * P:g * 256 + (p + 1) * P], src, s["ident"][:])
                    done(last, f"T{v}.")
                for v in range(1, 6):
                    for g in range(2):
                        if v == 1:
                            main_v.after(pe, n, f"Xb.1.{d}")
                        else:
                            main_a.after(pe, n, f"X{v - 1}.{g}.{d}")
                        for h in range(4):
                            last = mm(ps[:, g, h * P:(h + 1) * P], MB[:, g, h, 0, :], X[:, g, h, :])
                        done(last, f"G{v}.{g}.")
                    if v < 4 or (v == 4 and d == 0):
                        turn_rows(v)
                    if nxt and v == 2:
                        w_lora(*nxt)
                    if nxt and v == 3:
                        a_lora(*nxt)
                    if nxt and v == 4 and d:
                        main_a.after(pe, n, "Kt.1")
                        key_sums(nxt[0])
                    for g in range(2):
                        main_v.after(pe, n, f"G{v}.{g}.{d}")
                        if v > 1:
                            main_a.after(pe, n, f"Z{v - 1}.{g}.{d}")
                        if v < 5:
                            for h in range(4):
                                last = mm(ps[:, 2 + g, h * P:(h + 1) * P], Z[:, g, h, :], G[:, g, h, :])
                            done(last, f"X{v}.{g}.")
                        for h in range(4):
                            last = mm(ps[:, 4 + g, h * P:(h + 1) * P], G[:, g, h, :], Z[:, g, h, :])
                        done(last, f"Z{v}.{g}.")
                        if v == 5:
                            if g == 0:
                                main_a.after(pe, n, f"V.0")
                            for h in range(4):
                                last = mm(ps[:, g, h * P:(h + 1) * P], MK[:, g, h, 0, :], Vt[:, g, (h // 2) * P:(h // 2 + 1) * P])
                            done(last, f"MV{g}.")
                for g in range(2):
                    main_a.after(pe, n, f"MV1.{g}.{d}")
                    for h in range(4):
                        last = mm(ps[:, 2 + g, h * P:(h + 1) * P], Z[:, g, h, :], WI[:, g, h, :])
                    done(last, f"W{g}.")
                for g in range(2):
                    main_a.after(pe, n, f"W{g}.{d}")
                    for h in range(4):
                        p = h // 2
                        mm(ps[half(h), 4 + g, p * P:(p + 1) * P], W[:, g, h, 0:CH], MB[:, g, h, 1, :])
                        o = ps[half(h), 4 + g, 256 + p * P:256 + (p + 1) * P]
                        mm(o, W[:, g, h, CH:P], MB[:, g, h, 1, :], stop=False)
                        last = mm(o, Vt[:, g, h * CH:(h + 1) * CH], MK[:, g, h, 1, :], start=False)
                    done(last, f"GY{g}.")
                if d == 0:
                    prep_v.after(pe, n, "bt")
                    prep_p.done(mm(ps[:, 6, :], J[:], flat(kds[:])), "bonus")
                for g in range(2):
                    for h in range(4):
                        at = g * 256 + (h // 2) * CH
                        for part in range(3):
                            for c in range(2):
                                rows = slice(c * CH, (c + 1) * CH)
                                bh = Bt[rows, g, h * CH:(h + 1) * CH]
                                o_p, o_q = (ps[half(h), c, at + i * P:at + i * P + CH] for i in range(2))
                                if part == 0:
                                    mm(o_p, W[rows, g, h, 0:CH], bh)
                                elif part == 1:
                                    mm(o_q, bh, W[rows, g, h, CH:P], stop=False)
                                else:
                                    last = mm(o_q, Kt[rows, g, h * CH:(h + 1) * CH], Vt[rows, g, h * CH:(h + 1) * CH], start=False)
                done(last, "PQ")
            units(pe, prologue, unit)


def recurrence_stage(nc, t, s):
    with ExitStack() as ctx:
        chain = {"P": ctx.enter_context(nc.sbuf_tensor("chunk_p", [P, 2, NC_ALL, 2, CH], F32)),
                 "Q": ctx.enter_context(nc.sbuf_tensor("chunk_q", [P, 2, NC_ALL, 2, CH], F32)),
                 "tot": ctx.enter_context(nc.sbuf_tensor("chunk_decay", [P, 2, NC_ALL, 2], F32))}
        recurrence_local_stage(nc, t, s, chain)
        recurrence_chain_stage(nc, t, s, chain)


def recurrence_chain_stage(nc, t, s, chain):
    with ExitStack() as ctx:
        sb = lambda name, shape, dt=F32: ctx.enter_context(nc.sbuf_tensor(name, shape, dt))
        sem = lambda name: ctx.enter_context(nc.semaphore(name))
        CL, CC = SEQ // CH, CTX // CH
        S = sb("states", [P, CL + 1, 2, 2, CH])
        Sc = sb("ctx_states", [P, CC, 2, 2, CH])
        gt, yt = sb("g_in", [P, 2, 2, 2, BLK]), sb("y_in", [P, 2, 2, BLK])
        rg, bon = sb("rw_gate", [P, 2, BLK]), sb("bonus_in", [P, 2, BLK])
        o, sq, mean, rstd, sg = (sb(n, [P, 2, BLK]) for n in ("o_sum", "o_sq", "o_mean", "o_rstd", "silu_g"))
        gn = sb("gn_params", [P, 2, 2])
        jm = s["head_mean"]
        ps = ctx.enter_context(nc.psum_tensor("chain_ps", [P, 8, BLK], F32))
        p_done, s_done = sem("state_products"), sem("states_done")
        gn_in, g_in, y_in, step = sem("gn_in"), [sem(f"g_in{i}") for i in range(2)], sem("chain_y_in"), Signal(ctx, nc, "chain_step")
        o_ps, mean_ps, var_ps, o_ready, dev_ready, act_done, stored, out_ready = (sem(n) for n in (
            "o_ps", "mean_ps", "var_ps", "o_ready", "dev_ready", "chain_act", "rw_stored", "rw_out_ready"))
        block = ctx.enter_context(nc.Block())
        V, T = nc.vector, nc.tensor
        half = lambda h: slice(h * CH, (h + 1) * CH)

        @block.sync
        def _(sp):
            sp.dma_start(gn[:, 0, :], t["rw_gn_g"].rearrange("l (m p) -> p (l m)", p=P)).then_inc(gn_in, 16)
            sp.dma_start(gn[:, 1, :], t["rw_gn_b"].rearrange("l (m p) -> p (l m)", p=P)).then_inc(gn_in, 16)
            for b in range(NB):
                lat = slice(CTX + b * BLK, CTX + (b + 1) * BLK)
                if b >= 2:
                    sp.wait_ge(o_ps, b - 1)
                sp.dma_start(gt[:, b % 2, :, :, :], t["gT"][:, :, :, lat].rearrange("d m p t -> p d m t")).then_inc(g_in[b % 2], 16)
                if b >= 1:
                    sp.wait_ge(out_ready, b)
                for d in range(2):
                    sp.dma_start(yt[:, d, :, :], t["yT"][d, :, :, lat].rearrange("m p t -> p m t")).then_inc(y_in, 16)
                sp.dma_start(bon[:], t["bonusT"][:, :, lat].rearrange("m p t -> p m t")).then_inc(y_in, 16)
                sp.dma_start(rg[:], t["zT"][T_RG:T_PP, :, Z_LAT + b * BLK:Z_LAT + (b + 1) * BLK].rearrange("m p t -> p m t")).then_inc(y_in, 16)
                if b >= 1:
                    sp.dma_start(t["branchT"][4:6, :, (b - 1) * BLK:b * BLK].rearrange("m p t -> p m t"), sq[:]).then_inc(stored, 16)
            sp.wait_ge(out_ready, NB)
            sp.dma_start(t["branchT"][4:6, :, SEQ - BLK:SEQ].rearrange("m p t -> p m t"), sq[:]).then_inc(stored, 16)
            sp.wait_ge(stored, 16 * NB)

        def chunk(d, i):
            if i < CC:
                return i if d == 0 else CC - 1 - i
            return i if d == 0 else NC_ALL - 1 - (i - CC)

        def state(d, p, i):
            return (Sc[:, i, d, p, :] if i < CC else S[:, i - CC, d, p, :])

        @block.tensor
        def _(pe):
            n = 0
            for i in range(1, NC_ALL - 1):
                for d in range(2):
                    pe.wait_ge(s_done, 4 * (i - 1) + 2 * d + 2)
                    for p in range(2):
                        for h in range(2):
                            bank = (i % 2) * 4 + d * 2 + p
                            last = T.matmul(ps[half(h), bank, 0:CH], chain["P"][half(h), d, chunk(d, i), p, :],
                                            state(d, p, i)[half(h), :], start=True, stop=True)
                        last.then_inc(p_done, 1)
            pe.wait_ge(s_done, 4 * (NC_ALL - 1))
            for b in range(NB):
                pe.wait_ge(g_in[b % 2], 16 * (b // 2) + 16)
                if b >= 1:
                    pe.wait_ge(o_ready, b)
                for c in range(8):
                    for p in range(2):
                        for h in range(2):
                            for d in range(2):
                                ch = CC + b * 8 + c
                                i = ch if d == 0 else NC_ALL - 1 - ch + CC
                                last = T.matmul(ps[half(h), p, c * CH:(c + 1) * CH], state(d, p, i)[half(h), :],
                                                gt[half(h), b % 2, d, p, c * CH:(c + 1) * CH], start=(d == 0), stop=(d == 1))
                last.then_inc(o_ps, 1)
                pe.wait_ge(o_ready, b + 1)
                for p in range(2):
                    last = T.matmul(ps[:, 2 + p, :], jm[:], o[:, p, :], start=True, stop=True)
                last.then_inc(mean_ps, 1)
                pe.wait_ge(dev_ready, b + 1)
                for p in range(2):
                    last = T.matmul(ps[:, 4 + p, :], jm[:], sq[:, p, :], start=True, stop=True)
                last.then_inc(var_ps, 1)

        @block.scalar
        def _(act):
            for b in range(NB):
                act.wait_ge(var_ps, b + 1)
                nc.scalar.activation(rstd[:], ps[:, 4:6, :], ACT.Sqrt, bias=s["gn_eps"][:]).then_inc(act_done, 1)
                act.wait_ge(y_in, 64 * (b + 1))
                nc.scalar.activation(sg[:], rg[:], ACT.Silu).then_inc(act_done, 1)

        @block.vector
        def _(dve):
            own = lambda ins: step.step(dve, ins)
            for d in range(2):
                for p in range(2):
                    V.tensor_copy(state(d, p, 1), chain["Q"][:, d, chunk(d, 0), p, :]).then_inc(s_done, 1)
            for i in range(1, NC_ALL - 1):
                for d in range(2):
                    for p in range(2):
                        dve.wait_ge(p_done, 4 * (i - 1) + 2 * d + p + 1)
                        V.scalar_tensor_tensor(state(d, p, i + 1), ps[:, (i % 2) * 4 + d * 2 + p, 0:CH],
                                               chain["tot"][:, d, chunk(d, i), p:p + 1], chain["Q"][:, d, chunk(d, i), p, :],
                                               ALU.mult, ALU.add).then_inc(s_done, 1)
            dve.wait_ge(gn_in, 32)
            for b in range(NB):
                dve.wait_ge(y_in, 64 * (b + 1))
                own(V.tensor_tensor(yt[:, 0, :, :], yt[:, 0, :, :], yt[:, 1, :, :], ALU.add))
                dve.wait_ge(o_ps, b + 1)
                V.tensor_tensor(o[:], ps[:, 0:2, :], yt[:, 0, :, :], ALU.add).then_inc(o_ready, 1)
                dve.wait_ge(o_ready, b + 1)
                dve.wait_ge(mean_ps, b + 1)
                own(V.tensor_tensor(o[:], o[:], ps[:, 2:4, :], ALU.subtract))
                if b >= 1:
                    dve.wait_ge(stored, 16 * b)
                V.tensor_tensor(sq[:], o[:], o[:], ALU.mult).then_inc(dev_ready, 1)
                dve.wait_ge(act_done, 2 * b + 1)
                own(V.reciprocal(rstd[:], rstd[:]))
                own(V.tensor_tensor(o[:], o[:], rstd[:], ALU.mult))
                for p in range(2):
                    last = V.tensor_scalar(o[:, p, :], o[:, p, :], gn[:, 0, p:p + 1], gn[:, 1, p:p + 1], ALU.mult, ALU.add)
                own(last)
                own(V.tensor_tensor(o[:], o[:], bon[:], ALU.add))
                dve.wait_ge(act_done, 2 * b + 2)
                V.tensor_tensor(sq[:], o[:], sg[:], ALU.mult).then_inc(out_ready, 1)


def attention_stage(nc, t, s):
    ROWS, KR, BAND = SEQ // GRID, 8, 8 * GRID
    NDR, NDC = 15, 31
    PADW = 2 * GRID - 1
    KEYS = BAND + CTX
    with ExitStack() as ctx:
        sb = lambda name, shape, dt=F32: ctx.enter_context(nc.sbuf_tensor(name, shape, dt))
        sem = lambda name: ctx.enter_context(nc.semaphore(name))
        q, k, v = sb("q_t", [P, 2, SEQ]), sb("k_t", [P, 2, NT]), sb("v_t", [P, 2, NT])
        ng = sb("na_gate", [P, 2, SEQ])
        ve, vo = sb("v_even", [P, NT // P, BR]), sb("v_odd", [P, SEQ // P - 1, BR])
        bias = sb("na_bias", [P, 2, NDR * GRID])
        pad = sb("rpb_padded", [4 * NDR, PADW])
        qs = sb("q_heads", [P, 2, 2, P])
        sband = sb("band_scores", [P, 2, BAND])
        pr = sb("probs", [P, 2, 2, KEYS])
        prt = sb("probs_t", [P, 2, KEYS])
        on = sb("o_rows", [P, 2, P])
        st = sb("softmax_stats", [P, 2, 2, 5])
        rsum = sb("softmax_rsum", [P, 2, 2, 2])
        ps = ctx.enter_context(nc.psum_tensor("na_ps", [P, 8, BLK], F32))
        loads = {n: sem("na_in_" + n) for n in ("q", "k", "v", "g", "rpb")}
        pad_set, pad_out, bias_in, bias_set = sem("pad_set"), sem("pad_out"), sem("bias_in"), Signal(ctx, nc, "bias_set")
        silu_done, v_turned, v_copied = sem("na_silu"), sem("v_turned"), sem("v_copied")
        qz = sem("q_zeroed")
        front = lambda name, r: Results(ctx, nc, name, r)
        fs = front("front_scalar", ["q0", "q1"] + [f"{n}{p}" for p in range(2) for n in ("e", "c")])
        fp = front("front_products", ["S0", "S1"])
        fv = front("front_vector", [f"{n}{p}" for p in range(2) for n in ("m", "b", "n")])
        bv = front("back_vector", ["s0", "r0", "P0", "o0", "s1", "r1", "P1", "g0", "o1", "g1"])
        bs = front("back_scalar", ["P0", "P1"])
        bp = front("back_products", ["T0", "O0", "T1", "OT0", "O1", "OT1"])
        stored = sem("na_stored")
        block = ctx.enter_context(nc.Block())
        V, A, T = nc.vector, nc.scalar, nc.tensor
        half = lambda h: slice(h * CH, (h + 1) * CH)

        def ago(res, eng, row, n, result):
            if not isinstance(row, int) or row >= n:
                res.after(eng, row - n, result)

        def rows(eng, one_front, one_back):
            def place(r):
                start = min(max(r - 4, 0), ROWS - KR)
                return start, start % 2, (start - r + KR - 1) * GRID
            def step(r):
                if r < ROWS:
                    one_front(r, r % 2, *place(r))
                if r > 0:
                    one_back(r - 1, (r - 1) % 2, *place(r - 1))
            for r in range(5):
                step(r)
            with eng.Fori(0, 12) as n:
                for u in range(2):
                    one_front(n * 2 + (5 + u), (5 + u) % 2, n * 2 + (1 + u), (1 + u) % 2, (KR - 5) * GRID)
                    one_back(n * 2 + (4 + u), (4 + u) % 2, n * 2 + u, u % 2, (KR - 5) * GRID)
            for r in range(29, ROWS + 1):
                step(r)

        @block.sync
        def _(sp):
            lat = slice(Z_LAT, Z_LAT + SEQ)
            z = lambda a, c: t["zT"][a:a + 2, :, c].rearrange("m p t -> p m t")
            sp.wait_ge(pad_set, 1)
            sp.dma_start(pad[:, GRID - 16:GRID + 15], t["na_rpb"].rearrange("l h r c -> (l h r) c")).then_inc(loads["rpb"], 16)
            sp.dma_start(v[:, :, 0:CTX], z(T_V, slice(Z_CTX, Z_CTX + CTX))).then_inc(loads["v"], 16)
            sp.dma_start(v[:, :, CTX:NT], z(T_V, lat)).then_inc(loads["v"], 16)
            sp.dma_start(k[:, :, 0:CTX], z(T_K, slice(Z_CTX, Z_CTX + CTX))).then_inc(loads["k"], 16)
            sp.dma_start(k[:, :, CTX:NT], z(T_K, lat)).then_inc(loads["k"], 16)
            sp.dma_start(q[:], z(T_Q, lat)).then_inc(loads["q"], 16)
            sp.dma_start(ng[:], z(T_NG, lat)).then_inc(loads["g"], 16)
            sp.wait_ge(loads["rpb"], 16)
            src = pad[:].rearrange("r (a c) -> r a c", a=1).to_broadcast([4 * NDR, GRID, PADW])
            sp.dma_start(t["rpbPad"][:, :, 0:PADW], src).then_inc(pad_out, 16)
            sp.wait_ge(pad_out, 16)
            for p in range(2):
                for h in range(2):
                    src = bass.AP(tensor=t["rpbPad"].tensor, offset=(2 * p + h) * NDR * GRID * 2 * GRID + GRID - 1,
                                  ap=[[PADW, GRID], [GRID * 2 * GRID, NDR], [1, GRID]])
                    sp.dma_start(bias[half(h), p, :].rearrange("q (r c) -> q r c", c=GRID), src).then_inc(bias_in, 16)
            bv.after(sp, ROWS - 1, "g1")
            sp.dma_start(t["branchT"][2:4, :, :].rearrange("m p t -> p m t"), ng[:]).then_inc(stored, 16)
            sp.wait_ge(stored, 16)

        @block.gpsimd
        def _(pool):
            nc.gpsimd.memset(pad[:], 0.0).then_inc(pad_set, 1)
            nc.gpsimd.memset(qs[:], 0.0).then_inc(qz, 1)
            pool.wait_ge(bias_in, 16 * 4)
            for h in range(2):
                w = bias[half(h), :, :].rearrange("p m (r c) -> p (m r) c", c=GRID)
                bias_set.step(pool, nc.gpsimd.affine_select(out=w[:, :, 0:GRID - 16], in_=w[:, :, 0:GRID - 16], compare_op=ALU.is_ge,
                                                            fill=-1e30, base=8, pattern=[[0, 2 * NDR], [1, GRID - 16]], channel_multiplier=-1))
                bias_set.step(pool, nc.gpsimd.affine_select(out=w[:, :, 16:GRID], in_=w[:, :, 16:GRID], compare_op=ALU.is_gt,
                                                            fill=-1e30, base=8 - 16, pattern=[[0, 2 * NDR], [-1, GRID - 16]], channel_multiplier=1))

        @block.scalar
        def _(act):
            act.wait_ge(loads["g"], 16)
            A.activation(ng[:], ng[:], ACT.Silu).then_inc(silu_done, 1)
            for n in range(17):
                act.wait_ge(v_turned, n + 1)
                dst = ve[:, 2 * n:2 * n + 2, :] if n < 9 else vo[:, 2 * (n - 9):min(2 * (n - 9) + 2, 15), :]
                w = dst.shape[1]
                A.copy(dst, ps[:, n % 4, 0:w * BR].rearrange("p (a c) -> p a c", c=BR)).then_inc(v_copied, 1)
            act.wait_ge(loads["q"], 16)
            act.wait_ge(qz, 1)

            def one_front(r, par, start, vpar, win):
                ago(fp, act, r, 2, "S1")
                for h in range(2):
                    fs.own(act, r, A.activation(qs[half(h), par, :, half(h)], q[half(h), :, bass.ds(r * GRID, GRID)],
                                                ACT.Copy, scale=CH ** -0.5), f"q{h}")
                for p in range(2):
                    ago(bp, act, r, 2, f"T{p}")
                    fv.after(act, r, f"n{p}")
                    fs.own(act, r, A.activation(pr[:, par, p, 0:BAND], sband[:, p, :], ACT.Exp, bias=st[:, par, p, 2:3],
                                                accum_out=st[:, par, p, 3:4]), f"e{p}")
                    fs.own(act, r, A.activation(pr[:, par, p, BAND:KEYS], ps[:, 2 + p, 0:CTX], ACT.Exp, bias=st[:, par, p, 2:3],
                                                accum_out=st[:, par, p, 4:5]), f"c{p}")

            def one_back(r, par, start, vpar, win):
                for p in range(2):
                    bp.after(act, r, f"T{p}")
                    bs.own(act, r, A.copy(prt[:, p, 0:BAND], ps[:, 4, :]), f"P{p}")
            rows(act, one_front, one_back)

        @block.vector
        def _(dve):
            dve.wait_ge(bias_set.sem, 4)
            dve.wait_ge(silu_done, 1)

            def one_front(r, par, start, vpar, win):
                for p in range(2):
                    fp.after(dve, r, f"S{p}")
                    ago(fs, dve, r, 1, f"c{p}")
                    fv.done(V.reduce_max(st[:, par, p, 1:2], ps[:, 2 + p, 0:CTX], AX.X), f"m{p}")
                    fv.own(dve, r, V.tensor_tensor_reduce(out=sband[:, p, :], in0=ps[:, p, :], in1=bias[:, p, win:win + BAND], scale=1.0,
                                                          scalar=-3e38, op0=ALU.add, op1=ALU.max, accum_out=st[:, par, p, 0:1]), f"b{p}")
                    fv.own(dve, r, V.tensor_scalar(st[:, par, p, 2:3], st[:, par, p, 0:1], st[:, par, p, 1:2], -1.0, ALU.max, ALU.mult), f"n{p}")

            def one_back(r, par, start, vpar, win):
                def sums(p):
                    fs.after(dve, r, f"c{p}")
                    bv.own(dve, r, V.tensor_tensor(rsum[:, par, p, 0:1], st[:, par, p, 3:4], st[:, par, p, 4:5], ALU.add), f"s{p}")
                    bv.own(dve, r, V.reciprocal(rsum[:, par, p, 1:2], rsum[:, par, p, 0:1]), f"r{p}")
                    bp.after(dve, r, f"T{p}")
                    bv.own(dve, r, V.tensor_copy(prt[:, p, BAND:KEYS], ps[:, 5, 0:CTX]), f"P{p}")

                def out_rows(p):
                    bp.after(dve, r, f"O{p}")
                    bv.own(dve, r, V.tensor_scalar(on[:, p, :], ps[:, 6, 0:P], rsum[:, par, p, 1:2], None, ALU.mult), f"o{p}")

                def gate(p):
                    bp.after(dve, r, f"OT{p}")
                    for h in range(2):
                        cols = ng[half(h), p, bass.ds(r * GRID, GRID)]
                        ins = V.tensor_tensor(cols, ps[half(h), 7, half(h)], cols, ALU.mult)
                    bv.own(dve, r, ins, f"g{p}")
                sums(0)
                out_rows(0)
                sums(1)
                gate(0)
                out_rows(1)
                gate(1)
            rows(dve, one_front, one_back)

        @block.tensor
        def _(pe):
            pe.wait_ge(loads["v"], 32)
            for n in range(17):
                if n >= 4:
                    pe.wait_ge(v_copied, n - 3)
                tiles = [CTX * 0 + P * a for a in (2 * n, 2 * n + 1)] if n < 9 else [CTX + CH + P * a for a in range(2 * (n - 9), min(2 * (n - 9) + 2, 15))]
                for a, c0 in enumerate(tiles):
                    for p in range(2):
                        last = T.transpose(ps[:, n % 4, a * BR + p * P:a * BR + (p + 1) * P], v[:, p, c0:c0 + P], s["ident"][:])
                last.then_inc(v_turned, 1)
            pe.wait_ge(v_copied, 17)
            pe.wait_ge(loads["k"], 32)

            def scores(r, par, p, start):
                if p == 0:
                    fs.after(pe, r, "q1")
                T.matmul(ps[:, p, :], qs[:, par, p, :], k[:, p, bass.ds(start * GRID + CTX, BAND)], start=True, stop=True)
                fp.done(T.matmul(ps[:, 2 + p, 0:CTX], qs[:, par, p, :], k[:, p, 0:CTX], start=True, stop=True), f"S{p}")

            def turn_probs(r, par, p):
                fs.after(pe, r, f"c{p}")
                if p:
                    bs.after(pe, r, "P0")
                    bv.after(pe, r, "P0")
                else:
                    ago(bs, pe, r, 1, "P1")
                    ago(bv, pe, r, 1, "P1")
                for j in range(6):
                    last = T.transpose(ps[:, 4 + j // 4, (j % 4) * P:(j % 4 + 1) * P], pr[:, par, p, j * P:(j + 1) * P], s["ident"][:])
                bp.done(last, f"T{p}")

            def values(r, p, start, vpar):
                bs.after(pe, r, f"P{p}")
                bv.after(pe, r, f"P{p}")
                for j in range(6):
                    if j >= 4:
                        rhs = ve[:, j - 4, p * P:(p + 1) * P]
                    elif isinstance(start, int):
                        rhs = (vo[:, start // 2 + j, p * P:(p + 1) * P] if vpar else ve[:, 2 + start // 2 + j, p * P:(p + 1) * P])
                    else:
                        tile = half_start[0]
                        rhs = (vo if vpar else ve)[:, bass.ds(tile + (j if vpar else 2 + j), 1), p * P:(p + 1) * P]
                        rhs = rhs.rearrange("p a c -> p (a c)")
                    last = T.matmul(ps[:, 6, 0:P], prt[:, p, j * P:(j + 1) * P], rhs, start=(j == 0), stop=(j == 5))
                bp.done(last, f"O{p}")

            def turn_out(r, p):
                bv.after(pe, r, f"o{p}")
                bp.done(T.transpose(ps[:, 7, 0:P], on[:, p, :], s["ident"][:]), f"OT{p}")

            half_start = [None]

            def one_front(r, par, start, vpar, win):
                scores(r, par, 0, start)
                scores(r, par, 1, start)

            def one_back(r, par, start, vpar, win):
                turn_probs(r, par, 0)
                values(r, 0, start, vpar)
                turn_probs(r, par, 1)
                turn_out(r, 0)
                values(r, 1, start, vpar)
                turn_out(r, 1)

            def place(r):
                start = min(max(r - 4, 0), ROWS - KR)
                return start, start % 2, (start - r + KR - 1) * GRID
            for r in range(5):
                one_front(r, r % 2, *place(r))
                if r:
                    one_back(r - 1, (r - 1) % 2, *place(r - 1))
            with pe.Fori(0, 12) as n:
                half_start[0] = n
                for u in range(2):
                    one_front(n * 2 + (5 + u), (5 + u) % 2, n * 2 + (1 + u), (1 + u) % 2, 0)
                    one_back(n * 2 + (4 + u), (4 + u) % 2, n * 2 + u, u % 2, 0)
            for r in range(29, ROWS + 1):
                if r < ROWS:
                    one_front(r, r % 2, *place(r))
                one_back(r - 1, (r - 1) % 2, *place(r - 1))


def local_branches_stage(nc, t, s):
    with ExitStack() as ctx:
        sb = lambda name, shape, dt=F32: ctx.enter_context(nc.sbuf_tensor(name, shape, dt))
        sem = lambda name: ctx.enter_context(nc.semaphore(name))
        NCK = BLK // P
        gin = sb("gm_in", [P, 2, 6, BLK])
        sq, rstd, vn, gout = sb("gm_sq", [P, 2, BLK]), sb("gm_rstd", [P, 2, BLK]), sb("gm_vn", [P, 2, BLK]), sb("gm_out", [P, 2, BLK])
        vrow = sb("gm_v_rows", [P, NCK, BR])
        wraw, wt = sb("gm_w", [P, 4, P]), sb("gm_w_t", [P, 4, P])
        lnp, bs = sb("gm_ln", [P, 2, 2]), sb("gm_bias", [P, 2, P])
        jm = s["head_mean"]
        EDGE = 8
        pp, s2, s4, s8 = (sb(n, [P, 2, SEQ + 2 * EDGE]) for n in ("pool_in", "pool_2", "pool_4", "pool_8"))
        dd, pg = sb("pool_diff", [P, 2, SEQ]), sb("pool_gate", [P, 2, SEQ])
        edge = sb("pool_edge", [P, 2, 2, EDGE])
        plw, pls = sb("pool_w", [P, 2, P]), sb("pool_scale", [P, 2])
        pout = sb("pool_out", [P, 2, BLK])
        ps = ctx.enter_context(nc.psum_tensor("local_ps", [P, 8, BLK], F32))
        g_in = [sem(f"gm_in{i}") for i in range(2)]
        w_in, bias_in, pool_in, plw_in, plw_set, edge_set = (sem(n) for n in ("gm_w_in", "gm_bias_in", "pool_in", "pool_w_in", "pool_w_set", "pool_edge_set"))
        gm_stored, pl_stored = sem("gm_stored"), sem("pool_stored")
        act_r = Results(ctx, nc, "gm_scalar", ["v", "u", "g", "sqrt", "rows0", "rows1"])
        vec_r = Results(ctx, nc, "gm_vector", ["dev", "sq", "rec", "n1", "ln", "m", "mu", "mg"])
        pe_r = Results(ctx, nc, "gm_products", ["mean", "var", "rows", "mixed"])
        wt_ps, wt_set, pstep = sem("gm_w_turned"), sem("gm_w_set"), Signal(ctx, nc, "pool_step")
        estep = Signal(ctx, nc, "pool_edge_step")
        pl_ps, pl_out, pl_silu = sem("pool_ps"), sem("pool_out_ready"), sem("pool_silu")
        block = ctx.enter_context(nc.Block())
        V, A, T = nc.vector, nc.scalar, nc.tensor
        half = lambda h: slice(h * CH, (h + 1) * CH)
        z = lambda a, c: t["zT"][a:a + 2, :, c].rearrange("m p t -> p m t")

        @block.sync
        def _(sp):
            sp.wait_ge(plw_set, 1)
            sp.dma_start(wraw[:], t["gm_ws"].rearrange("l g p q -> p (l g) q")).then_inc(w_in, 16)
            for n, name in enumerate(("gm_ln_g", "gm_ln_b")):
                sp.dma_start(lnp[:, n, :], t[name].rearrange("l (m h) n -> (h n) (l m)", h=2)).then_inc(bias_in, 16)
            for g in range(4):
                sp.dma_start(bs[half(g % 2), g // 2, :], t["gm_bs"][0, g:g + 1, :].to_broadcast([CH, P])).then_inc(bias_in, 16)
                sp.dma_start(plw[half(g % 2), g // 2, half(g % 2)], t["pl_w"][0, g, :, :]).then_inc(plw_in, 16)
            sp.dma_start(pls[:], t["pl_scale"].rearrange("l (m p) -> p (l m)", p=P)).then_inc(plw_in, 16)
            def load(b):
                c = slice(Z_LAT + b * BLK, Z_LAT + (b + 1) * BLK)
                for n, a in enumerate((T_GU, T_GV, T_GG)):
                    sp.dma_start(gin[:, b % 2, 2 * n:2 * n + 2, :], z(a, c)).then_inc(g_in[b % 2], 16)
            load(0)
            load(1)
            sp.dma_start(pp[:, :, EDGE:EDGE + SEQ], z(T_PP, slice(Z_LAT, Z_LAT + SEQ))).then_inc(pool_in, 16)
            sp.dma_start(pg[:], z(T_PG, slice(Z_LAT, Z_LAT + SEQ))).then_inc(pool_in, 16)
            for b in range(NB):
                vec_r.after(sp, b, "mg")
                sp.dma_start(t["branchT"][0:2, :, b * BLK:(b + 1) * BLK].rearrange("m p t -> p m t"), gout[:]).then_inc(gm_stored, 16)
                if b + 2 < NB:
                    load(b + 2)
            for b in range(NB):
                sp.wait_ge(pl_out, b + 1)
                sp.dma_start(t["branchT"][6:8, :, b * BLK:(b + 1) * BLK].rearrange("m p t -> p m t"), pout[:]).then_inc(pl_stored, 16)
            sp.wait_ge(gm_stored, 16 * NB)
            sp.wait_ge(pl_stored, 16 * NB)

        @block.gpsimd
        def _(pool):
            nc.gpsimd.memset(plw[:], 0.0).then_inc(plw_set, 1)
            last = nc.gpsimd.memset(edge[:], 1.0)
            last.then_inc(edge_set, 1)
            pool.wait_ge(edge_set, 1)
            for g, w in enumerate((2, 4, 8, 16)):
                r = w // 2
                for i in range(r):
                    estep.step(pool, nc.gpsimd.memset(edge[half(g % 2), g // 2, 0, i:i + 1], w / (i + r)))
                for i in range(EDGE - (r - 1), EDGE):
                    estep.step(pool, nc.gpsimd.memset(edge[half(g % 2), g // 2, 1, i:i + 1], w / (r + EDGE - i)))
            for side in (0, SEQ + EDGE):
                last = nc.gpsimd.memset(pp[:, :, side:side + EDGE], 0.0)
            last.then_inc(edge_set, 1)

        @block.scalar
        def _(act):
            act.wait_ge(wt_ps, 1)
            A.copy(wt[:], ps[:, 7, :].rearrange("p (g t) -> p g t", g=4)).then_inc(wt_set, 1)
            for b in range(NB):
                gi = gin[:, b % 2, :, :]
                act.wait_ge(g_in[b % 2], 48 * (b // 2 + 1))
                act_r.own(act, b, A.activation(gi[:, 2:4, :], gi[:, 2:4, :], ACT.Gelu_apprx_tanh), "v")
                act_r.own(act, b, A.activation(gi[:, 0:2, :], gi[:, 0:2, :], ACT.Gelu_apprx_tanh), "u")
                act_r.own(act, b, A.activation(gi[:, 4:6, :], gi[:, 4:6, :], ACT.Silu), "g")
                pe_r.after(act, b, "var")
                vec_r.earlier(act, b, "rec")
                act_r.own(act, b, A.activation(rstd[:], ps[:, 2:4, :], ACT.Sqrt, bias=s["eps"][:]), "sqrt")
                pe_r.after(act, b, "rows")
                for n in range(2):
                    act_r.own(act, b, A.copy(vrow[:, 2 * n:2 * n + 2, :], ps[:, 4 + n, :].rearrange("p (c m) -> p c m", c=2)), f"rows{n}")
            act.wait_ge(pool_in, 32)
            A.activation(pg[:], pg[:], ACT.Silu).then_inc(pl_silu, 1)

        @block.vector
        def _(dve):
            dve.wait_ge(bias_in, 16 * 6)
            for b in range(NB):
                own = lambda ins, name: vec_r.own(dve, b, ins, name)
                gi = gin[:, b % 2, :, :]
                pe_r.after(dve, b, "mean")
                own(V.tensor_tensor(vn[:], gi[:, 2:4, :], ps[:, 0:2, :], ALU.subtract), "dev")
                own(V.tensor_tensor(sq[:], vn[:], vn[:], ALU.mult), "sq")
                act_r.after(dve, b, "sqrt")
                own(V.reciprocal(rstd[:], rstd[:]), "rec")
                own(V.tensor_tensor(vn[:], vn[:], rstd[:], ALU.mult), "n1")
                for p in range(2):
                    last = V.tensor_scalar(vn[:, p, :], vn[:, p, :], lnp[:, 0, p:p + 1], lnp[:, 1, p:p + 1], ALU.mult, ALU.add)
                own(last, "ln")
                pe_r.after(dve, b, "mixed")
                if b:
                    dve.wait_ge(gm_stored, 16 * b)
                for p in range(2):
                    last = V.tensor_tensor(gout[:, p, :].rearrange("p (c t) -> p c t", t=P), ps[:, 6 + p, :].rearrange("p (c t) -> p c t", t=P),
                                           bs[:, p:p + 1, :].to_broadcast([P, NCK, P]), ALU.add)
                own(last, "m")
                own(V.tensor_tensor(gout[:], gout[:], gi[:, 0:2, :], ALU.mult), "mu")
                own(V.tensor_tensor(gout[:], gout[:], gi[:, 4:6, :], ALU.mult), "mg")
            step = lambda ins: pstep.step(dve, ins)
            W = SEQ + 2 * EDGE
            dve.wait_ge(pool_in, 32)
            dve.wait_ge(edge_set, 2)
            step(V.tensor_tensor(s2[:, :, 1:W], pp[:, :, 0:W - 1], pp[:, :, 1:W], ALU.add))
            step(V.tensor_tensor(s4[:, :, 2:W - 1], s2[:, :, 1:W - 2], s2[:, :, 3:W], ALU.add))
            step(V.tensor_tensor(s8[:, 1, 4:W - 3], s4[:, 1, 2:W - 5], s4[:, 1, 6:W - 1], ALU.add))
            step(V.tensor_tensor(s2[half(1), 1, 8:W - 7], s8[half(1), 1, 4:W - 11], s8[half(1), 1, 12:W - 3], ALU.add))
            mid = slice(EDGE, EDGE + SEQ)
            for g, src in enumerate((s2, s4, s8, s2)):
                c, p, w = half(g % 2), g // 2, 2 << g
                for side, cols in ((0, slice(EDGE, 2 * EDGE)), (1, slice(SEQ, SEQ + EDGE))):
                    last = V.tensor_tensor(src[c, p, cols], src[c, p, cols], edge[c, p, side, :], ALU.mult)
                step(last)
                step(V.scalar_tensor_tensor(dd[c, p, :], src[c, p, mid], 1.0 / w, pp[c, p, mid], ALU.mult, ALU.subtract))
            dve.wait_ge(pl_silu, 1)
            for b in range(NB):
                dve.wait_ge(pl_ps, b + 1)
                if b:
                    dve.wait_ge(pl_stored, 16 * b)
                for p in range(2):
                    last = V.scalar_tensor_tensor(pout[:, p, :], ps[:, 2 * (b % 2) + p, :], pls[:, p:p + 1], pg[:, p, b * BLK:(b + 1) * BLK],
                                                  ALU.mult, ALU.mult)
                last.then_inc(pl_out, 1)

        @block.tensor
        def _(pe):
            pe.wait_ge(w_in, 16)
            for g in range(4):
                last = T.transpose(ps[:, 7, g * P:(g + 1) * P], wraw[:, g, :], s["ident"][:])
            last.then_inc(wt_ps, 1)
            pe.wait_ge(wt_set, 1)
            for b in range(NB):
                act_r.after(pe, b, "v")
                for p in range(2):
                    last = T.matmul(ps[:, p, :], jm[:], gin[:, b % 2, 2 + p, :], start=True, stop=True)
                pe_r.done(last, "mean")
                vec_r.after(pe, b, "sq")
                for p in range(2):
                    last = T.matmul(ps[:, 2 + p, :], jm[:], sq[:, p, :], start=True, stop=True)
                pe_r.done(last, "var")
                vec_r.after(pe, b, "ln")
                for c in range(NCK):
                    for p in range(2):
                        last = T.transpose(ps[:, 4 + c // 2, (c % 2) * BR + p * P:(c % 2) * BR + (p + 1) * P], vn[:, p, c * P:(c + 1) * P], s["ident"][:])
                pe_r.done(last, "rows")
                act_r.after(pe, b, "rows1")
                for c in range(NCK):
                    for g in range(4):
                        last = T.matmul(ps[half(g % 2), 6 + g // 2, c * P:(c + 1) * P], vrow[:, c, g * CH:(g + 1) * CH], wt[:, g, :],
                                        start=True, stop=True)
                pe_r.done(last, "mixed")
            pe.wait_ge(pstep.sem, 12)
            pe.wait_ge(plw_in, 16 * 5)
            for b in range(NB):
                if b >= 2:
                    pe.wait_ge(pl_out, b - 1)
                for p in range(2):
                    last = T.matmul(ps[:, 2 * (b % 2) + p, :], plw[:, p, :], dd[:, p, b * BLK:(b + 1) * BLK], start=True, stop=True)
                last.then_inc(pl_ps, 1)


def merge_stage(nc, t, s):
    with ExitStack() as ctx:
        sb = lambda name, shape, dt=F32: ctx.enter_context(nc.sbuf_tensor(name, shape, dt))
        sem = lambda name: ctx.enter_context(nc.semaphore(name))
        b_hi, b_lo = sb("mb_hi", [P, 8, SEQ], F32R), sb("mb_lo", [P, 8, SEQ], F32R)
        raw = sb("mb_raw", [P, 2, SEQ // 2])
        w_raw, w_hi, w_lo = sb("mw_raw", [P, 4, 2, P]), sb("mw_hi", [P, 2, 4, 2, P], F32R), sb("mw_lo", [P, 2, 4, 2, P], F32R)
        gate, y, prod = sb("m_gate", [P, 2, SEQ]), sb("m_y", [P, SEQ]), sb("m_prod", [P, SEQ])
        ps = ctx.enter_context(nc.psum_tensor("merge_ps", [P, 2, NB, BLK], F32))
        raw_in, gate_in = [sem("raw_in0"), sem("raw_in1")], [sem("gate_in0"), sem("gate_in1")]
        raw_hi, w_loaded, w_hi_ready, w_lo_ready = (sem(n) for n in ("raw_hi", "mw_loaded", "mw_hi_ready", "mw_lo_ready"))
        raw_lo = [sem("raw_lo_even"), sem("raw_lo_odd")]
        proj_ps, gated, y_added, y_stored = sem("proj_ps"), sem("gated"), sem("y_added"), sem("y_stored")
        block = ctx.enter_context(nc.Block())
        V, A, T = nc.vector, nc.scalar, nc.tensor
        NR = 16
        piece = lambda n: (n // 2, slice((n % 2) * (SEQ // 2), (n % 2 + 1) * (SEQ // 2)))
        w_brs = t["w_br"].rearrange("l i (k p) n -> p (l i k) n", p=P)

        def over_columns(eng, body):
            body(0, 0, True)
            body(1, 1, True)
            with eng.Fori(1, KT // 2) as n:
                body(n * 2, 0, False)
                body(n * 2 + 1, 1, False)

        @block.sync
        def _(sp):
            def load_w(j):
                sp.dma_start(w_raw[:].rearrange("p i k n -> p (i k) n"), w_brs[:, :, bass.ds(j * P, P)]).then_inc(w_loaded, 16)

            load_w(0)
            for n in range(NR):
                m, cols = piece(n)
                if n >= 2:
                    sp.wait_ge(raw_lo[n % 2], n // 2)
                sp.dma_start(raw[:, n % 2, :], t["branchT"][m, :, cols]).then_inc(raw_in[n % 2], 16)
                if n == 1:
                    for i in range(2):
                        sp.dma_start(gate[:, i, :], t["gatesT"][8 * i, :, :]).then_inc(gate_in[i], 16)

            def column(j, par, first):
                if isinstance(j, int):
                    if j:
                        sp.wait_ge(y_added, j * 4)
                        sp.dma_start(t["mergedT"][j - 1, :, :], y[:]).then_inc(y_stored, 16)
                else:
                    sp.wait_ge(y_added, j * 4)
                    sp.dma_start(t["mergedT"][bass.ds(j - 1, 1), :, :].rearrange("a p t -> p (a t)"), y[:]).then_inc(y_stored, 16)

            def gates(j, last):
                if not last:
                    sp.wait_ge(w_lo_ready, j + 1)
                    load_w(j + 1)
                for i in range(4):
                    if last and i >= 2:
                        return
                    at = j + (8 * (i + 2) if i < 2 else 8 * (i - 2) + 1)
                    sp.wait_ge(gated, j * 4 + i + 1)
                    sp.dma_start(gate[:, i % 2, :], t["gatesT"][bass.ds(at, 1), :, :].rearrange("a p t -> p (a t)")).then_inc(gate_in[i % 2], 16)
            gates(0, False)
            column(1, 1, True)
            with sp.Fori(1, KT - 1) as j:
                gates(j, False)
                column(j + 1, 0, False)
            gates(KT - 1, True)
            sp.wait_ge(y_added, KT * 4)
            sp.dma_start(t["mergedT"][KT - 1, :, :], y[:]).then_inc(y_stored, 16)
            sp.wait_ge(y_stored, 16 * KT)

        @block.gpsimd
        def _(pool):
            for n in range(0, NR, 2):
                m, cols = piece(n)
                pool.wait_ge(raw_hi, n + 1)
                nc.gpsimd.tensor_tensor(b_lo[:, m, cols], raw[:, n % 2, :], b_hi[:, m, cols].bitcast(F32), ALU.subtract).then_inc(raw_lo[n % 2], 1)

        @block.scalar
        def _(act):
            def split_w(j, par, first):
                act.wait_ge(w_loaded, j * 16 + 16)
                if not first:
                    act.wait_ge(proj_ps, j * 4 - 4)
                A.copy(w_hi[:, par, :, :, :], w_raw[:]).then_inc(w_hi_ready, 1)
            split_w(0, 0, True)
            for n in range(NR):
                m, cols = piece(n)
                act.wait_ge(raw_in[n % 2], 16 * (n // 2) + 16)
                A.copy(b_hi[:, m, cols], raw[:, n % 2, :]).then_inc(raw_hi, 1)
            split_w(1, 1, True)
            with act.Fori(1, KT // 2) as n:
                split_w(n * 2, 0, False)
                split_w(n * 2 + 1, 1, False)

        @block.vector
        def _(dve):
            def split_w(j, par):
                dve.wait_ge(w_hi_ready, j + 1)
                V.tensor_tensor(w_lo[:, par, :, :, :], w_raw[:], w_hi[:, par, :, :, :].bitcast(F32), ALU.subtract).then_inc(w_lo_ready, 1)

            def column(j, par, last):
                for i in range(4):
                    dve.wait_ge(gate_in[i % 2], j * 32 + (16 * (i // 2) + 16))
                    dve.wait_ge(proj_ps, j * 4 + (i + 1))
                    if i == 0 and not (isinstance(j, int) and j == 0):
                        dve.wait_ge(y_stored, j * 16)
                    elif i >= 2:
                        dve.wait_ge(y_added, j * 4 + i)
                    to = y if i == 0 else prod
                    V.tensor_tensor(to[:].rearrange("p (b t) -> p b t", t=BLK), gate[:, i % 2, :].rearrange("p (b t) -> p b t", t=BLK),
                                    ps[:, i % 2, :, :], ALU.mult).then_inc(gated, 1)
                    dve.wait_ge(gated, j * 4 + (i + 1))
                    if i:
                        V.tensor_tensor(y[:], y[:], prod[:], ALU.add).then_inc(y_added, 1)
                    else:
                        dve.sem_inc(y_added, 1)
                    if i == 1 and not last:
                        split_w(j + 1, 1 - par)
            split_w(0, 0)
            for n in range(1, NR, 2):
                m, cols = piece(n)
                dve.wait_ge(raw_hi, n + 1)
                V.tensor_tensor(b_lo[:, m, cols], raw[:, n % 2, :], b_hi[:, m, cols].bitcast(F32), ALU.subtract).then_inc(raw_lo[n % 2], 1)
            column(0, 0, False)
            with dve.Fori(1, KT // 2) as n:
                column(n * 2 - 1, 1, False)
                column(n * 2, 0, False)
            column(KT - 1, 1, True)

        @block.tensor
        def _(pe):
            def column(j, par, first):
                pe.wait_ge(w_lo_ready, j + 1)
                for i in range(4):
                    if j == 0 if isinstance(j, int) else False:
                        for half in range(2):
                            pe.wait_ge(raw_lo[half], 2 * i + 2)
                    if not (isinstance(j, int) and j == 0 and i < 2):
                        pe.wait_ge(gated, j * 4 + (i - 1))
                    for b in range(NB):
                        cols = slice(b * BLK, (b + 1) * BLK)
                        for k in range(2):
                            o, m = ps[:, i % 2, b, :], 2 * i + k
                            T.matmul(o, w_hi[:, par, i, k, :], b_hi[:, m, cols], start=(k == 0), stop=False)
                            T.matmul(o, w_hi[:, par, i, k, :], b_lo[:, m, cols], start=False, stop=False)
                            last = T.matmul(o, w_lo[:, par, i, k, :], b_hi[:, m, cols], start=False, stop=(k == 1))
                    last.then_inc(proj_ps, 1)
            over_columns(pe, column)


def output_stage(nc, t, s):
    with ExitStack() as ctx:
        sb = lambda name, shape, dt=F32: ctx.enter_context(nc.sbuf_tensor(name, shape, dt))
        sem = lambda name: ctx.enter_context(nc.semaphore(name))
        wo_raw = sb("wo_raw", [P, 2, D])
        wo_hi, wo_lo = sb("wo_hi", [P, KT, D], F32R), sb("wo_lo", [P, KT, D], F32R)
        yr = sb("y_raw", [P, 2, KT, P])
        yh, yl = sb("y_hi", [P, 2, KT, P], F32R), sb("y_lo", [P, 2, KT, P], F32R)
        xr = sb("x_res", [P, 2, D])
        gb, fg = sb("gate_rows", [P, D]), sb("final_g_rows", [P, D])
        gcol = sb("gate_cols", [P, P])
        junk = sb("out_junk", [P, D])
        ss, rt, rs = sb("out_ss", [P, 2]), sb("out_rt", [P, 2]), sb("out_rs", [P, 2])
        ps = ctx.enter_context(nc.psum_tensor("out_ps", [P, 4, BLK], F32))
        gps = ctx.enter_context(nc.psum_tensor("gate_ps", [P, 2, BLK], F32))
        wo_in = [sem("wo_in0"), sem("wo_in1")]
        wo_h, wo_l, fg_in = sem("wo_hi_ready"), sem("wo_lo_ready"), sem("final_g_in")
        y_in, x_in = [sem("y_in0"), sem("y_in1")], [sem("xr_in0"), sem("xr_in1")]
        y_h, y_l, prod = sem("y_hi_ready"), sem("y_lo_ready"), sem("out_products")
        gcol_set, gate_mm = sem("gate_cols_set"), sem("gate_turned")
        vec = Results(ctx, nc, "out_vector", ["gated", "res", "rec", "norm"])
        sca = Results(ctx, nc, "out_scalar", ["ss", "rt"])
        gstep = Signal(ctx, nc, "gate_rows_set")
        stored = [sem("out_stored0"), sem("out_stored1")]
        block = ctx.enter_context(nc.Block())
        V, A, T = nc.vector, nc.scalar, nc.tensor
        NTT = SEQ // P
        x_rows = t["x"].rearrange("a (n p) d -> (a n) p d", p=P)
        o_rows = t["out"].rearrange("a (n p) d -> (a n) p d", p=P)

        def over_tiles(eng, body):
            body(0, 0, 0)
            body(1, 1, 0)
            with eng.Fori(1, NTT // 2) as n:
                body(n * 2, 0, n)
                body(n * 2 + 1, 1, n)

        @block.sync
        def _(sp):
            w = t["w_out"].rearrange("l (k p) n -> (l k) p n", p=P)
            sp.dma_start(fg[:], t["final_g"].rearrange("(a d) -> a d", a=1).to_broadcast([P, D])).then_inc(fg_in, 16)
            for k in range(KT):
                if k >= 2:
                    sp.wait_ge(wo_l, k - 1)
                sp.dma_start(wo_raw[:, k % 2, :], w[k]).then_inc(wo_in[k % 2], 16)

            def load(n, par, m):
                if not isinstance(n, int):
                    sp.wait_ge(stored[par], m * 16)
                sp.dma_start(yr[:, par, :, :], t["mergedT"][:, :, bass.ds(n * P, P)].rearrange("k p t -> p k t")).then_inc(y_in[par], 16)
                sp.dma_start(xr[:, par, :], x_rows[bass.ds(n, 1), :, :].rearrange("a p d -> p (a d)")).then_inc(x_in[par], 16)
            over_tiles(sp, load)

        @block.gpsimd
        def _(pool):
            for k in range(KT):
                pool.wait_ge(wo_h, k + 1)
                nc.gpsimd.tensor_tensor(wo_lo[:, k, :], wo_raw[:, k % 2, :], wo_hi[:, k, :].bitcast(F32), ALU.subtract).then_inc(wo_l, 1)

            def split(n, par, m):
                pool.wait_ge(y_h, n + 1)
                nc.gpsimd.tensor_tensor(yl[:, par, :, :], yr[:, par, :, :], yh[:, par, :, :].bitcast(F32), ALU.subtract).then_inc(y_l, 1)
            over_tiles(pool, split)

        @block.scalar
        def _(act):
            for k in range(KT):
                act.wait_ge(wo_in[k % 2], 16 * (k // 2 + 1))
                A.copy(wo_hi[:, k, :], wo_raw[:, k % 2, :]).then_inc(wo_h, 1)

            def hi(n, par, m):
                act.wait_ge(y_in[par], m * 16 + 16)
                if not isinstance(n, int):
                    act.wait_ge(prod, n - 1)
                A.copy(yh[:, par, :, :], yr[:, par, :, :]).then_inc(y_h, 1)

            def norm(n, par, m):
                vec.after(act, n, "res")
                sca.own(act, n, A.activation(junk[:], xr[:, par, :], ACT.Square, accum_out=ss[:, par:par + 1]), "ss")
                sca.own(act, n, A.activation(rt[:, par:par + 1], ss[:, par:par + 1], ACT.Sqrt, bias=s["eps"][:], scale=1.0 / D), "rt")
                vec.after(act, n, "norm")
                act.dma_start(o_rows[bass.ds(n, 1), :, :].rearrange("a p d -> p (a d)"), xr[:, par, :]).then_inc(stored[par], 16)
            hi(0, 0, 0)
            hi(1, 1, 0)
            norm(0, 0, 0)
            with act.Fori(1, NTT // 2) as n:
                hi(n * 2, 0, n)
                norm(n * 2 - 1, 1, n - 1)
                hi(n * 2 + 1, 1, n)
                norm(n * 2, 0, n)
            norm(NTT - 1, 1, NTT // 2 - 1)
            for par in range(2):
                act.wait_ge(stored[par], 16 * NTT // 2)

        @block.vector
        def _(dve):
            for k in range(KT):
                gstep.step(dve, V.tensor_copy(gcol[:], s["mod"][:, 0, 2 * KT + k:2 * KT + k + 1].to_broadcast([P, P])))
                dve.wait_ge(gate_mm, k + 1)
            V.tensor_copy(gb[:].rearrange("p (b d) -> p b d", b=2), gps[:]).then_inc(gcol_set, 1)
            dve.wait_ge(gcol_set, 1)
            dve.wait_ge(fg_in, 16)

            def tile(n, par, m):
                dve.wait_ge(prod, n + 1)
                dve.wait_ge(x_in[par], m * 16 + 16)
                gated = ps[:, 2 * par:2 * par + 2, :]
                vec.own(dve, n, V.tensor_tensor(gated, gated, gb[:].rearrange("p (b d) -> p b d", b=2), ALU.mult), "gated")
                xv = xr[:, par, :].rearrange("p (b d) -> p b d", b=2)
                vec.own(dve, n, V.tensor_tensor(xv, xv, gated, ALU.add), "res")
                sca.after(dve, n, "rt")
                vec.own(dve, n, V.reciprocal(rs[:, par:par + 1], rt[:, par:par + 1]), "rec")
                vec.own(dve, n, V.scalar_tensor_tensor(xr[:, par, :], xr[:, par, :], rs[:, par:par + 1], fg[:], ALU.mult, ALU.mult), "norm")
            over_tiles(dve, tile)

        @block.tensor
        def _(pe):
            for k in range(KT):
                pe.wait_ge(gstep.sem, k + 1)
                T.matmul(gps[:, k // 4, (k % 4) * P:(k % 4 + 1) * P], gcol[:], s["ident"][:], start=True, stop=True).then_inc(gate_mm, 1)

            def tile(n, par, m):
                pe.wait_ge(y_l, n + 1)
                if isinstance(n, int) and n == 0:
                    pe.wait_ge(wo_l, KT)
                if not isinstance(n, int):
                    vec.after(pe, n - 2, "res")
                for k in range(KT):
                    for b in range(2):
                        o = ps[:, 2 * par + b, :]
                        cols = slice(b * BLK, (b + 1) * BLK)
                        T.matmul(o, yh[:, par, k, :], wo_hi[:, k, cols], start=(k == 0), stop=False)
                        T.matmul(o, yh[:, par, k, :], wo_lo[:, k, cols], start=False, stop=False)
                        last = T.matmul(o, yl[:, par, k, :], wo_hi[:, k, cols], start=False, stop=(k == KT - 1))
                last.then_inc(prod, 1)
            over_tiles(pe, tile)


STAGES = (modulation_stage, projection_stage, recurrence_stage, attention_stage, local_branches_stage, merge_stage, output_stage)


_INS = ["x", "c", "ctx", "c_ctx", "ada_w", "ada_b", "norm_g", "w_in", "gm_ln_g", "gm_ln_b", "gm_ws", "gm_bs", "na_rpb",
        "rw_mu", "rw_w0", "rw_w2", "rw_a0", "rw_a2", "rw_kk", "rw_ka", "rw_rk", "rw_gn_g", "rw_gn_b", "pl_w", "pl_scale",
        "w_br", "w_out", "final_g"]


def hybrid_layer_kernel(nc, t, stages=None):
    with ExitStack() as ctx:
        ctx.enter_context(nc.allow_non_contiguous_dma(reason="parameters as columns"))
        s = {name: ctx.enter_context(nc.sbuf_tensor(name, shape, F32)) for name, shape in (
            ("ident", [P, P]), ("ones", [P, P]), ("heads", [P, P]), ("head_mean", [P, P]), ("eps", [P, 1]), ("gn_eps", [P, 1]),
            ("mod", [P, 2, 24]), ("gscale", [P, 2, KT]))}
        for stage in (stages or STAGES):
            stage(nc, t, s)


SCRATCH = {"zT": (T_END, P, ZPAD), "hT": (KT, P, SEQ), "gT": (2, 2, P, NT), "yT": (2, 2, P, NT),
           "bonusT": (2, P, NT), "branchT": (8, P, SEQ), "rpbPad": (60, GRID, 2 * GRID), "mergedT": (KT, P, SEQ), "gatesT": (32, P, SEQ)}


def kernel(**inputs):
    import numpy as _np
    import concourse.bacc as _bacc
    from concourse import mybir as _mybir
    from concourse.bass_utils import run_bass_kernel_spmd as _run

    nc = _bacc.Bacc("TRN2", target_bir_lowering=False, num_devices=1)
    arrays, t = {}, {}
    for name in _INS:
        a = _np.ascontiguousarray(inputs[name])
        arrays[f"in_{name}"] = a
        t[name] = nc.dram_tensor(f"in_{name}", a.shape, _mybir.dt.from_np(a.dtype), kind="ExternalInput").ap()
    for name, shape in SCRATCH.items():
        t[name] = nc.dram_tensor(f"scratch_{name}", shape, F32, kind="Internal").ap()
    t["out"] = nc.dram_tensor("out", (1, SEQ, D), F32, kind="ExternalOutput").ap()
    hybrid_layer_kernel(nc, t)
    r = _run(nc, [arrays], core_ids=[0])
    return r.results[0]["out"]
```

```python
import numpy as np
import concourse.bass as bass
from concourse import mybir
from contextlib import ExitStack

F32 = mybir.dt.float32
F32R = mybir.dt.float32r
ALU = mybir.AluOpType
ACT = mybir.ActivationFunctionType
AX = mybir.AxisListType

P = 128
D = 1024
KT = D // P
CTX = 256
SEQ = 2048
NT = CTX + SEQ
BLK = 512
NB = SEQ // BLK
BR = 256
CH = 64
EPS = 1e-6
GN_EPS = 64e-5
ZPAD = NT + 3
Z_CTX, Z_LAT = 1, CTX + 2
GRID = 64
NDR = 15

T_GU, T_GV, T_GG, T_Q, T_K, T_V, T_NG, T_RW, T_RG, T_PP, T_PG, T_END = 0, 2, 4, 6, 8, 10, 12, 14, 21, 23, 25, 27
T_ALL = T_END + 32


class Signal:

    def __init__(self, ctx, nc, name):
        self.sem = ctx.enter_context(nc.semaphore(name))
        self.n = 0
        self.base = 0

    def mark(self, ins, inc=1):
        ins.then_inc(self.sem, inc)
        self.n += inc
        return self.n

    def step(self, eng, ins):
        self.mark(ins)
        eng.wait_ge(self.sem, self.base + self.n)


def modulation_stage(nc, t, s):
    with ExitStack() as ctx:
        ada = ctx.enter_context(nc.sbuf_tensor("ada", [P, 6, KT, 512], F32))
        cc = ctx.enter_context(nc.sbuf_tensor("cc", [P, 2, KT], F32))
        sc = ctx.enter_context(nc.sbuf_tensor("sc", [P, KT, 2], F32))
        bias = ctx.enter_context(nc.sbuf_tensor("ada_bias", [P, 24], F32))
        ng = ctx.enter_context(nc.sbuf_tensor("norm_g_cols", [P, KT], F32))
        rows = ctx.enter_context(nc.sbuf_tensor("mod_rows", [2, 6, 512], F32))
        row_ps = ctx.enter_context(nc.psum_tensor("mod_row_ps", [P, 6, 512], F32))
        mp = ctx.enter_context(nc.psum_tensor("mod_ps", [P, 24, 2], F32))
        row_done = ctx.enter_context(nc.semaphore("mod_row_done"))
        row_copied = ctx.enter_context(nc.semaphore("mod_row_copied"))
        ident_ready = ctx.enter_context(nc.semaphore("ident_ready"))
        c_in = ctx.enter_context(nc.semaphore("c_in"))
        ada_in = [ctx.enter_context(nc.semaphore(f"ada_in{j}")) for j in range(6)]
        small_in = ctx.enter_context(nc.semaphore("mod_small_in"))
        silu_c = ctx.enter_context(nc.semaphore("silu_c"))
        mod_done = ctx.enter_context(nc.semaphore("mod_done"))
        ones_ready = ctx.enter_context(nc.semaphore("ones_ready"))
        step = Signal(ctx, nc, "mod_step")
        mod, gs = s["mod"], s["gscale"]
        block = ctx.enter_context(nc.Block())

        @block.sync
        def _(sp):
            sp.dma_start(cc[:, 0, :], t["c"].rearrange("a (k p) -> p (a k)", p=P)).then_inc(c_in, 16)
            sp.dma_start(cc[:, 1, :], t["c_ctx"].rearrange("(k p) -> p k", p=P)).then_inc(c_in, 16)
            w = t["ada_w"].rearrange("l (k p) n -> p (l k) n", p=P)
            for j in range(6):
                sp.dma_start(ada[:, j, :, :], w[:, :, j * 512:(j + 1) * 512]).then_inc(ada_in[j], 16)
            sp.dma_start(bias[:], t["ada_b"].rearrange("l (m p) -> p (l m)", p=P)).then_inc(small_in, 16)
            sp.dma_start(ng[:], t["norm_g"].rearrange("l (m p) -> p (l m)", p=P)).then_inc(small_in, 16)

        @block.scalar
        def _(act):
            act.wait_ge(c_in, 32)
            nc.scalar.activation(sc[:, :, :].rearrange("p k s -> p s k"), cc[:], ACT.Silu).then_inc(silu_c, 1)
            for j in range(6):
                act.wait_ge(row_done, j + 1)
                nc.scalar.copy(rows[:, j, :], row_ps[0:2, j, :]).then_inc(row_copied, 1)

        @block.tensor
        def _(pe):
            pe.wait_ge(silu_c, 1)
            for j in range(6):
                pe.wait_ge(ada_in[j], 16)
                for k in range(KT):
                    last = nc.tensor.matmul(row_ps[0:2, j, :], sc[:, k, :], ada[:, j, k, :], start=(k == 0), stop=(k == KT - 1))
                last.then_inc(row_done, 1)
            pe.wait_ge(ident_ready, 1)
            for m in range(24):
                if m % 4 == 0:
                    pe.wait_ge(row_copied, m // 4 + 1)
                last = nc.tensor.transpose(mp[:, m, :], rows[:, m // 4, (m % 4) * P:(m % 4 + 1) * P], s["ident"][0:2, 0:2])
            last.then_inc(mod_done, 1)

        @block.vector
        def _(dve):
            nc.vector.memset(s["eps"][:], EPS)
            nc.vector.memset(s["gn_eps"][:], GN_EPS)
            step.step(dve, nc.vector.memset(s["heads"][:], 0.0))
            for h in range(2):
                step.mark(nc.vector.memset(s["heads"][h * CH:(h + 1) * CH, h * CH:(h + 1) * CH], 1.0))
            dve.wait_ge(step.sem, step.n)
            nc.vector.tensor_scalar(s["head_mean"][:], s["heads"][:], 1.0 / CH, None, ALU.mult)
            dve.wait_ge(small_in, 32)
            dve.wait_ge(mod_done, 1)
            for v in range(2):
                step.mark(nc.vector.tensor_tensor(mod[:, v, :], mp[:, :, v], bias[:], ALU.add))
            dve.wait_ge(step.sem, step.n)
            for v in range(2):
                nc.vector.scalar_tensor_tensor(gs[:, v, :], mod[:, v, KT:2 * KT], 1.0, ng[:], ALU.add, ALU.mult)

        @block.gpsimd
        def _(pool):
            nc.gpsimd.memset(s["ones"][:], 1.0).then_inc(ones_ready, 1)
            pool.wait_ge(ones_ready, 1)
            nc.gpsimd.affine_select(out=s["ident"][:], in_=s["ones"][:], compare_op=ALU.is_equal, fill=0.0,
                                    base=0, pattern=[[-1, P]], channel_multiplier=1).then_inc(ident_ready, 1)


def projection_stage(nc, t, s):
    HB = 2 * P
    with ExitStack() as ctx:
        sb = lambda name, shape, dt=F32: ctx.enter_context(nc.sbuf_tensor(name, shape, dt))
        sem = lambda name: ctx.enter_context(nc.semaphore(name))
        h_hi, h_lo = sb("h_hi", [P, KT, NT], F32R), sb("h_lo", [P, KT, NT], F32R)
        x_in = sb("x_rows", [P, 2, 2, D])
        h_st = sb("h_stage", [P, 2, KT, HB])
        z_st = sb("z_stage", [P, ZPAD])
        w_raw = sb("w_raw", [P, KT, P])
        w_hi, w_lo = sb("w_hi", [P, KT, P], F32R), sb("w_lo", [P, KT, P], F32R)
        ss, rt, rs = sb("sum_sq", [P, 2, 2]), sb("rms", [P, 2, 2]), sb("rstd", [P, 2, 2])
        ps = ctx.enter_context(nc.psum_tensor("proj_ps", [P, 8, BLK], F32))
        x_loaded, rms_done, x_normed = [sem("x_loaded0"), sem("x_loaded1")], sem("rms_done"), sem("x_normed")
        sq_done, rs_done = sem("sq_done"), sem("rs_done")
        turned, h_ready, hi_ready, lo_ready = sem("turned"), sem("h_ready"), sem("hi_ready"), sem("lo_ready")
        w_loaded, w_hi_ready, w_lo_ready, w_free = sem("w_loaded"), sem("w_hi_ready"), sem("w_lo_ready"), sem("w_free")
        z_ps_ready, z_act, z_dve, z_stored = sem("z_ps_ready"), sem("z_act"), sem("z_dve"), sem("z_stored")
        block = ctx.enter_context(nc.Block())
        x_rows = t["x"].rearrange("a (n p) d -> p (a n) d", p=P)
        ctx_rows = t["ctx"].rearrange("a (n p) d -> p (a n) d", p=P)
        w_cols = t["w_in"].rearrange("l (k p) n -> p (l k) n", p=P)
        zT = t["zT"]
        RUNS = [(T_RW, T_RG, True), (T_K, T_NG, True), (T_GU, T_K, False), (T_NG, T_RW, False), (T_RG, T_END, False),
                (T_END, T_ALL, False)]
        TURNS = T_ALL

        NHB = NT // HB

        def over_blocks(eng, ahead, body):
            at = lambda b: (b, b % 2, b // 2)
            ahead(*at(0))
            for b in range(3):
                ahead(*at(b + 1))
                body(*at(b))
            with eng.Fori(1, 3) as m:
                ahead(m * 2 + 2, 0, m + 1)
                body(m * 2 + 1, 1, m)
                ahead(m * 2 + 3, 1, m + 1)
                body(m * 2 + 2, 0, m + 1)
            ahead(*at(8))
            body(*at(7))
            body(*at(8))
        assert NHB == 9
        nothing = lambda b, par, m: None

        def over_tiles(eng, body):
            turn = 0
            for a, e, with_ctx in RUNS:
                first, end = a, e
                if turn == 0:
                    body(a, 0, with_ctx, False, False)
                    first += 1
                if e == T_ALL:
                    end -= 1
                with eng.Fori(first, end) as tile:
                    body(tile, tile + (turn - a), with_ctx, a == T_END, False)
                turn += e - a
            body(end, turn - 1, False, True, True)

        @block.sync
        def _(sp):
            def load_x(b, par, m):
                if not isinstance(b, int) or b >= 2:
                    sp.wait_ge(turned, b * 4 - 4)
                src = ctx_rows if isinstance(b, int) and b == 0 else x_rows[:, bass.ds((b - 1) * 2, 2), :]
                sp.dma_start(x_in[:, par, :, :], src).then_inc(x_loaded[par], 16)

            def load_first_w(b, par, m):
                if isinstance(b, int) and b == 0:
                    sp.dma_start(w_raw[:], w_cols[:, :, T_RW * P:(T_RW + 1) * P]).then_inc(w_loaded, 16)
            over_blocks(sp, load_x, load_first_w)

            def tile(col, turn, with_ctx, then, gates):
                if then is not None:
                    sp.wait_ge(w_hi_ready, turn * 8 + 8)
                    sp.wait_ge(w_lo_ready, turn * 8 + 8)
                    sp.dma_start(w_raw[:], w_cols[:, :, bass.ds(then * P, P)]).then_inc(w_loaded, 16)
                sp.wait_ge(z_act, turn * 2 + 3)
                sp.wait_ge(z_dve, turn * 2 + 3)
                lo = 0 if with_ctx else Z_LAT
                if gates:
                    sp.dma_start(t["gatesT"][bass.ds(col - T_END, 1), :, :].rearrange("a p t -> p (a t)"),
                                 z_st[:, Z_LAT:Z_LAT + SEQ]).then_inc(z_stored, 16)
                else:
                    sp.dma_start(zT[bass.ds(col, 1), :, lo:ZPAD].rearrange("a p t -> p (a t)"),
                                 z_st[:, lo:ZPAD]).then_inc(z_stored, 16)

            turn = 0
            for n, (a, e, with_ctx) in enumerate(RUNS):
                with sp.Fori(a, e - 1) as col:
                    tile(col, col + (turn - a), with_ctx, col + 1, a == T_END)
                turn += e - a
                tile(e - 1, turn - 1, with_ctx, RUNS[n + 1][0] if n + 1 < len(RUNS) else None, a == T_END)
            sp.wait_ge(z_stored, 16 * TURNS)

        @block.gpsimd
        def _(pool):
            def split_lo(b, par, m):
                pool.wait_ge(hi_ready, b + 1)
                cols = bass.ds(b * HB, HB)
                nc.gpsimd.tensor_tensor(h_lo[:, :, cols], h_st[:, par, :, :], h_hi[:, :, cols].bitcast(F32), ALU.subtract).then_inc(lo_ready, 1)
            over_blocks(pool, nothing, split_lo)

        @block.scalar
        def _(act):
            def mean_square(b, par, m):
                act.wait_ge(x_loaded[par], m * 16 + 16)
                for j in range(2):
                    nc.scalar.activation(z_st[:, 0:D], x_in[:, par, j, :], ACT.Square, accum_out=ss[:, par, j:j + 1]).then_inc(sq_done, 1)
                    act.wait_ge(sq_done, b * 2 + (j + 1))
                nc.scalar.activation(rt[:, par, :], ss[:, par, :], ACT.Sqrt, bias=s["eps"][:], scale=1.0 / D).then_inc(rms_done, 1)

            def split_hi(b, par, m):
                act.wait_ge(h_ready, b * 8 + 8)
                nc.scalar.copy(h_hi[:, :, bass.ds(b * HB, HB)], h_st[:, par, :, :]).then_inc(hi_ready, 1)
            over_blocks(act, mean_square, split_hi)

            def split_w(turn, slots):
                for k in slots:
                    if k < KT - 1:
                        act.wait_ge(w_free, turn * 7 + (k + 1))
                    elif not (isinstance(turn, int) and turn == 0):
                        act.wait_ge(z_ps_ready, turn * 5)
                    nc.scalar.copy(w_hi[:, k, :], w_raw[:, k, :]).then_inc(w_hi_ready, 1)

            def tile(col, turn, with_ctx, gates, last):
                if not last:
                    act.wait_ge(w_loaded, turn * 16 + 32)
                    split_w(turn + 1, range(KT - 1))
                if not (isinstance(turn, int) and turn == 0):
                    act.wait_ge(z_stored, turn * 16)
                if gates:
                    for m in range(NB):
                        act.wait_ge(z_ps_ready, turn * 5 + (m + 1))
                        nc.scalar.activation(z_st[:, Z_LAT + m * BLK:Z_LAT + (m + 1) * BLK], ps[:, m, :],
                                             ACT.Sigmoid).then_inc(z_dve if m % 2 else z_act, 1)
                else:
                    for m in (0, 2):
                        act.wait_ge(z_ps_ready, turn * 5 + (m + 1))
                        nc.scalar.copy(z_st[:, Z_LAT + m * BLK:Z_LAT + (m + 1) * BLK], ps[:, m, :]).then_inc(z_act, 1)
                if not last:
                    split_w(turn + 1, (KT - 1,))
            act.sem_inc(z_act, 1)
            act.wait_ge(w_loaded, 16)
            split_w(0, range(KT))
            over_tiles(act, tile)

        @block.vector
        def _(dve):
            def normalise(b, par, m):
                dve.wait_ge(rms_done, b + 1)
                nc.vector.reciprocal(rs[:, par, :], rt[:, par, :]).then_inc(rs_done, 1)
                dve.wait_ge(rs_done, b + 1)
                for j in range(2):
                    last = nc.vector.tensor_scalar(x_in[:, par, j, :], x_in[:, par, j, :], rs[:, par, j:j + 1], None, ALU.mult)
                last.then_inc(x_normed, 1)

            def modulate(b, par, m):
                v = 1 if isinstance(b, int) and b == 0 else 0
                if not isinstance(b, int) or b >= 2:
                    dve.wait_ge(lo_ready, b - 1)
                for k in range(KT):
                    if k % 2 == 0:
                        dve.wait_ge(turned, b * 4 + (k // 2 + 1))
                    nc.vector.tensor_scalar(h_st[:, par, k, :], ps[:, par * 4 + k // 2, (k % 2) * HB:(k % 2 + 1) * HB],
                                            s["gscale"][:, v, k:k + 1], s["mod"][:, v, k:k + 1], ALU.mult, ALU.add).then_inc(h_ready, 1)
            over_blocks(dve, normalise, modulate)

            def split_w(turn, slots):
                for k in slots:
                    dve.wait_ge(w_hi_ready, turn * 8 + (k + 1))
                    nc.vector.tensor_tensor(w_lo[:, k, :], w_raw[:, k, :], w_hi[:, k, :].bitcast(F32),
                                            ALU.subtract).then_inc(w_lo_ready, 1)

            def tile(col, turn, with_ctx, gates, last):
                if not last:
                    split_w(turn + 1, range(KT - 1))
                if not gates:
                    if not (isinstance(turn, int) and turn == 0):
                        dve.wait_ge(z_stored, turn * 16)
                    for m in (1, 3):
                        dve.wait_ge(z_ps_ready, turn * 5 + (m + 1))
                        ins = nc.vector.tensor_copy(z_st[:, Z_LAT + m * BLK:Z_LAT + (m + 1) * BLK], ps[:, m, :])
                        if m == 1 or not with_ctx:
                            ins.then_inc(z_dve, 1)
                    if with_ctx:
                        dve.wait_ge(z_ps_ready, turn * 5 + 5)
                        nc.vector.tensor_copy(z_st[:, Z_CTX:Z_CTX + CTX], ps[:, 4, 0:CTX]).then_inc(z_dve, 1)
                if not last:
                    split_w(turn + 1, (KT - 1,))
            for col in (0, Z_CTX + CTX, ZPAD - 1):
                last = nc.vector.memset(z_st[:, col:col + 1], 0.0)
            last.then_inc(z_dve, 1)
            split_w(0, range(KT))
            over_tiles(dve, tile)

        @block.tensor
        def _(pe):
            def turn_rows(b, par, m):
                pe.wait_ge(x_normed, b + 1)
                for i in range(4):
                    if not isinstance(b, int) or b >= 2:
                        pe.wait_ge(h_ready, b * 8 + (2 * i - 14))
                    for k in (2 * i, 2 * i + 1):
                        for j in range(2):
                            at = (k % 2) * HB + j * P
                            last = nc.tensor.transpose(ps[:, par * 4 + i, at:at + P], x_in[:, par, j, k * P:(k + 1) * P], s["ident"][:])
                    last.then_inc(turned, 1)
            over_blocks(pe, nothing, turn_rows)
            pe.wait_ge(lo_ready, NHB)
            pe.sem_inc(w_free, 7)

            def product(m, k, w, h, first, last):
                cols = slice(CTX + m * BLK, CTX + (m + 1) * BLK) if m < NB else slice(0, CTX)
                out = ps[:, m, :] if m < NB else ps[:, m, 0:CTX]
                return nc.tensor.matmul(out, w[:, k, :], h[:, k, cols], start=first, stop=last)

            def tile(col, turn, with_ctx, gates, last):
                first = isinstance(turn, int) and turn == 0
                ms = range(NB + 1) if with_ctx else range(NB)
                for k in range(KT):
                    pe.wait_ge(w_hi_ready, turn * 8 + k + 1)
                    pe.wait_ge(w_lo_ready, turn * 8 + k + 1)
                    if 0 < k < KT - 1:
                        for m in ms:
                            product(m, k, w_hi, h_hi, False, False)
                            product(m, k, w_hi, h_lo, False, False)
                        for m in ms:
                            last = product(m, k, w_lo, h_hi, False, False)
                        last.then_inc(w_free, 1)
                        continue
                    for m in ms:
                        if k == 0:
                            if not first or m > 1:
                                pe.wait_ge(z_dve if m % 2 or m == NB else z_act, turn * 2 + (m > 1))
                        product(m, k, w_hi, h_hi, k == 0, False)
                        product(m, k, w_hi, h_lo, False, False)
                        last = product(m, k, w_lo, h_hi, False, k == KT - 1)
                        if k == KT - 1:
                            last.then_inc(z_ps_ready, 2 if m == NB - 1 and not with_ctx else 1)
                    if k == 0:
                        last.then_inc(w_free, 1)
            over_tiles(pe, tile)


class Results:

    def __init__(self, ctx, nc, name, results):
        self.sem = ctx.enter_context(nc.semaphore(name))
        self.at = {r: n + 1 for n, r in enumerate(results)}
        self.each = len(results)
        assert len(self.at) == self.each
        self.names, self.n = results, 0

    def done(self, ins, result):
        assert self.names[self.n % self.each] == result, (self.names[self.n % self.each], result)
        self.n += 1
        ins.then_inc(self.sem, 1)

    def after(self, eng, turn, result):
        eng.wait_ge(self.sem, turn * self.each + self.at[result])

    def earlier(self, eng, turn, result):
        if not isinstance(turn, int) or turn > 0:
            self.after(eng, turn - 1, result)

    def own(self, eng, turn, ins, result):
        self.done(ins, result)
        self.after(eng, turn, result)


NC_ALL = NT // CH
RB = 256
LEVELS = (1, 2, 4, 8, 16, 32)
DECAY = -float(np.exp(-0.5))


def recurrence_local_stage(nc, t, s, chain):
    with ExitStack() as ctx:
        sb = lambda name, shape, dt=F32: ctx.enter_context(nc.sbuf_tensor(name, shape, dt))
        sem = lambda name: ctx.enter_context(nc.semaphore(name))
        zin, zf, nbr = sb("z_halo", [P, 7, RB + 2]), sb("z_mixed", [P, 7, RB]), sb("neighbours", [P, 7, RB])
        th = sb("tanh_w_lo", [CH, RB])
        kkr, ksq, kk, k1, k2, rrk, kds = (sb(n, [P, 2, RB]) for n in
                                          ("kk_raw", "kk_sq", "kk_unit", "k_1", "k_2", "r_rk", "kd_sum"))
        lw, aa, L, Lx, exc = (sb(n, [P, 2, RB]) for n in ("log_w", "a_rate", "log_run", "log_before", "log_exc"))
        inc = lw
        EI, EX, EN = (sb(n, [P, 2, RB]) for n in ("e_inc", "e_exc", "e_neg"))
        kka, kd = sb("kk_a", [P, 2, RB]), sb("k_d", [P, 2, RB])
        AR = sb("a_r_hat", [P, 2, 2, 2, RB])
        Bh, Kh = sb("b_hat", [P, 2, 2, RB]), sb("k_hat", [P, 2, 2, RB])
        Vt = sb("v_rows", [P, 2, 2 * P])
        Bt, Kt = sb("b_rows", [P, 2, 2 * P]), sb("k_rows", [P, 2, 2 * P])
        MB, MK = sb("m_b", [P, 2, 4, 2, P]), sb("m_k", [P, 2, 4, 2, P])
        X, Z, G = sb("inv", [P, 2, 4, P]), sb("inv_t", [P, 2, 4, P]), sb("inv_g", [P, 2, 4, P])
        WI, W = sb("w_in_rows", [P, 2, 4, P]), sb("w_rows", [P, 2, 4, P])
        gst, yst, bst = sb("g_stage", [P, 2, RB]), sb("y_stage", [P, 2, RB]), sb("bonus_stage", [P, 2, RB])
        lev = sb("level_masks", [P, 2, len(LEVELS), P])
        tri = sb("chunk_masks", [P, 2, 2, P])
        run1, i64, J = sb("scan_keep", [P, 2, RB]), sb("ident_64", [P, CH]), s["heads"]
        mu, omu, hmu = sb("mu", [P, 7]), sb("one_less_mu", [P, 7]), sb("half_mu", [P, 7])
        par = sb("rw_params", [P, 7, 2])
        hpar = sb("rw_half_params", [P, 4, 2])
        lora = sb("lora", [P, 2, 2 * P])
        ps = ctx.enter_context(nc.psum_tensor("rw_ps", [P, 8, BLK], F32))
        consts_in, consts_set, masks = sem("rw_params_in"), Signal(ctx, nc, "rw_consts_set"), Signal(ctx, nc, "rw_masks")
        z_in, g_stored, y_stored, b_stored = sem("rw_z_in"), sem("g_stored"), sem("y_stored"), sem("bonus_stored")
        prep_v = Results(ctx, nc, "prep_vector", ["mix6"] + [f"mix{j}" for j in range(6)]
                         + ["kkr0", "kkr1", "ksq", "k20", "k21", "k1", "rrk0", "rrk1"]
                         + sum(([f"{n}{d}" for n in ["lw", "L", "Lx"] + ["inc", "exc"] * d + ["aa", "kdm", "kd", "kds"]]
                                + ["kmax", "krec", "kk"] * (1 - d) + [f"{n}{d}" for n in ["kka", "R", "A", "B", "K"]]
                                for d in range(2)), []) + ["bt", "bonus"])
        main_v = Results(ctx, nc, "main_vector", sum(([f"{n}{d}" for n in
                         sum(([f"MB0.{g}.", f"MB1.{g}.", f"MI.{g}.", f"Xa.{g}.", f"Xb.{g}.", f"Za.{g}.", f"Zb.{g}.", f"MK0.{g}.", f"MK1.{g}."]
                              for g in range(2)), [])
                         + [f"G{v}.{g}." for v in range(1, 6) for g in range(2)]
                         + ["Gs0.", "Gs1.", "P0.", "Q0.", "P1.", "Q1."]] for d in range(2)), []))
        prep_a = Results(ctx, nc, "prep_scalar", [f"scaled{j}" for j in range(7)] + ["th"]
                         + sum(([f"{n}{d}" for n in ["tw0.", "tw1.", "ta0.", "ta1."]] + ["knorm"] * (1 - d)
                                + [f"{n}{d}" for n in ["EI", "EX", "EN", "tot"]] for d in range(2)), []))
        main_a = Results(ctx, nc, "main_scalar", sum(([f"{n}{d}" for n in
                         ["X1.0.", "Z1.0.", "X1.1.", "Z1.1.", "At0.", "Bt0.", "X2.0.", "Z2.0.", "X2.1.", "Z2.1.", "At1.", "Bt1.",
                          "X3.0.", "Z3.0.", "X3.1.", "Z3.1.", "Kt.", "X4.0.", "Z4.0.", "X4.1.", "Z4.1."] + ["V."] * (1 - d)
                         + ["Z5.0.", "MV0.0.", "MV1.0.", "Z5.1.", "MV0.1.", "MV1.1.", "W0.", "W1.", "Y0.", "Y1."]]
                                                      for d in range(2)), []))
        prep_p = Results(ctx, nc, "prep_products", ["tw0", "ta0", "ksum", "tw1", "ta1", "bonus"])
        main_p = Results(ctx, nc, "main_products", sum(([f"{n}{d}" for n in ["SB0.", "SM0.", "SK0.", "SB1.", "SM1.", "SK1."]
                         + sum(([f"G{v}.0.", f"G{v}.1.", f"T{v}."] + [f"{x}{v}.{g}." for g in range(2) for x in "XZ"] for v in range(1, 4)), [])
                         + ["G4.0.", "G4.1."] + ["T4."] * (1 - d) + [f"{x}4.{g}." for g in range(2) for x in "XZ"]
                         + ["G5.0.", "G5.1.", "Z5.0.", "MV0.", "Z5.1.", "MV1.", "W0.", "W1.", "GY0.", "GY1.", "PQ"]]
                                                        for d in range(2)), []))
        nbr_set = sem("neighbours_set")
        Pst, Qst, tot = chain["P"], chain["Q"], chain["tot"]
        block = ctx.enter_context(nc.Block())

        NBLK = NT // RB

        def units(eng, prologue, unit):
            prologue()
            unit(0, 0, (0, 1))
            unit(0, 1, (1, 0))
            with eng.Fori(1, NBLK - 1) as n:
                unit(n, 0, (n, 1))
                unit(n, 1, (n + 1, 0))
            unit(NBLK - 1, 0, (NBLK - 1, 1))
            unit(NBLK - 1, 1, None)

        @block.sync
        def _(sp):
            def load(n):
                if not (isinstance(n, int) and n == 0):
                    sp.wait_ge(nbr_set, n)
                    prep_a.after(sp, n - 1, "scaled6")
                c0 = 0 if isinstance(n, int) and n == 0 else n * RB + 1
                sp.dma_start(zin[:], t["zT"][T_RW:T_RG, :, bass.ds(c0, RB + 2)].rearrange("k p t -> p k t")).then_inc(z_in, 16)

            load(0)
            row = lambda a: a.rearrange("l (m p) -> p (l m)", p=P)
            sp.dma_start(mu[:], row(t["rw_mu"])).then_inc(consts_in, 16)
            sp.dma_start(par[:, 0, :], row(t["rw_kk"])).then_inc(consts_in, 16)
            sp.dma_start(par[:, 1, :], row(t["rw_ka"])).then_inc(consts_in, 16)
            sp.dma_start(par[:, 2, :], t["rw_rk"].rearrange("l (m h) n -> (h n) (l m)", h=2)).then_inc(consts_in, 16)
            for d in range(2):
                sp.dma_start(par[:, 3 + d, :], row(t["rw_w0"][:, d, :])).then_inc(consts_in, 16)
                sp.dma_start(par[:, 5 + d, :], row(t["rw_a0"][:, d, :])).then_inc(consts_in, 16)
                sp.dma_start(lora[0:CH, d, :], t["rw_w2"][0, d, :, :]).then_inc(consts_in, 16)
                sp.dma_start(lora[CH:P, d, :], t["rw_a2"][0, d, :, :]).then_inc(consts_in, 16)

            def turn(n, more):
                for d in range(2):
                    if d and more:
                        load(n + 2)
                    main_v.after(sp, n, f"Gs1.{d}")
                    sp.dma_start(t["gT"][d, :, :, bass.ds(n * RB, RB)].rearrange("m p t -> p m t"), gst[:]).then_inc(g_stored, 16)
                    main_a.after(sp, n, f"Y1.{d}")
                    sp.dma_start(t["yT"][d, :, :, bass.ds(n * RB, RB)].rearrange("m p t -> p m t"), yst[:]).then_inc(y_stored, 16)
                    if d == 0:
                        prep_v.after(sp, n, "bonus")
                        sp.dma_start(t["bonusT"][:, :, bass.ds(n * RB, RB)].rearrange("m p t -> p m t"), bst[:]).then_inc(b_stored, 16)
            load(1)
            turn(0, True)
            with sp.Fori(1, NBLK - 2) as n:
                turn(n, True)
            turn(NBLK - 2, False)
            turn(NBLK - 1, False)
            sp.wait_ge(g_stored, 16 * 2 * NBLK)
            sp.wait_ge(y_stored, 16 * 2 * NBLK)
            sp.wait_ge(b_stored, 16 * NBLK)

        @block.gpsimd
        def _(pool):
            def neighbours(n):
                pool.wait_ge(z_in, n * 16 + 16)
                if not (isinstance(n, int) and n == 0):
                    prep_v.after(pool, n - 1, "mix5")
                nc.gpsimd.tensor_tensor(nbr[:], zin[:, :, 0:RB], zin[:, :, 2:RB + 2], ALU.add).then_inc(nbr_set, 1)
            neighbours(0)
            masks.step(pool, nc.gpsimd.memset(lev[:], 0.0))
            one = s["ones"]
            for v, b in enumerate(LEVELS):
                n = P // (2 * b)
                view = lambda m: m.rearrange("p (n h b) -> p n h b", h=2, b=b)
                for d in range(2):
                    o = view(lev[:, d, v, :])[:, :, d, :]
                    masks.step(pool, nc.gpsimd.affine_select(out=o, in_=view(one[:, :])[:, :, 0, :], compare_op=ALU.is_ge, fill=0.0,
                                                             base=-b * (1 - d), pattern=[[-2 * b, n], [0, b]], channel_multiplier=1))
                    masks.step(pool, nc.gpsimd.affine_select(out=o, in_=o, compare_op=ALU.is_ge, fill=0.0, base=b * (2 - d) - 1,
                                                             pattern=[[2 * b, n], [0, b]], channel_multiplier=-1))
            for d in range(2):
                for incl in range(2):
                    o = tri[:, d, incl, :].rearrange("p (c j) -> p c j", c=2)
                    src = one[:, :].rearrange("p (c j) -> p c j", c=2)
                    op = ALU.is_ge if incl else ALU.is_gt
                    sign = 1 - 2 * d
                    masks.step(pool, nc.gpsimd.affine_select(out=o, in_=src, compare_op=op, fill=0.0, base=0,
                                                             pattern=[[CH * sign, 2], [sign, CH]], channel_multiplier=-sign))
                    masks.step(pool, nc.gpsimd.affine_select(out=o, in_=o, compare_op=ALU.is_ge, fill=0.0, base=0,
                                                             pattern=[[-CH, 2], [0, CH]], channel_multiplier=1))
                    masks.step(pool, nc.gpsimd.affine_select(out=o, in_=o, compare_op=ALU.is_ge, fill=0.0, base=CH - 1,
                                                             pattern=[[CH, 2], [0, CH]], channel_multiplier=-1))
            for h in range(2):
                masks.step(pool, nc.gpsimd.affine_select(out=i64[h * CH:(h + 1) * CH, :], in_=one[h * CH:(h + 1) * CH, 0:CH],
                                                         compare_op=ALU.is_equal, fill=0.0, base=0, pattern=[[-1, CH]],
                                                         channel_multiplier=1))

            with pool.Fori(1, NBLK) as n:
                neighbours(n)

        N_MASKS = 1 + 4 * len(LEVELS) + 12 + 2
        V, A, T = nc.vector, nc.scalar, nc.tensor
        flat = lambda a: a.rearrange("p a b -> p (a b)")

        @block.vector
        def _(dve):
            dve.wait_ge(consts_in, 16 * 12)
            consts_set.mark(V.memset(run1[:], 1.0))
            dve.wait_ge(consts_set.sem, consts_set.n)
            consts_set.mark(V.memset(run1[:].rearrange("p a (c j) -> p a c j", j=CH)[:, :, :, 0:1], 0.0))
            consts_set.mark(V.tensor_scalar(omu[:], mu[:], -1.0, 1.0, ALU.mult, ALU.add))
            consts_set.mark(V.tensor_scalar(hmu[:], mu[:], 0.5, None, ALU.mult))
            consts_set.mark(V.tensor_scalar(hpar[:], par[:, 3:7, :], 0.5, None, ALU.mult))
            dve.wait_ge(consts_set.sem, consts_set.n)

            def mix(n):
                dve.wait_ge(nbr_set, n + 1)
                for j in (6, 0, 1, 2, 3, 4, 5):
                    prep_a.after(dve, n, f"scaled{j}")
                    prep_v.own(dve, n, V.scalar_tensor_tensor(zf[:, j, :], nbr[:, j, :], hmu[:, j:j + 1], zf[:, j, :], ALU.mult, ALU.add), f"mix{j}")

            def keys(n):
                own = lambda ins, name: prep_v.own(dve, n, ins, name)
                for p in range(2):
                    own(V.tensor_scalar(kkr[:, p, :], zf[:, 2 + p, :], par[:, 0, p:p + 1], None, ALU.mult), f"kkr{p}")
                own(V.tensor_tensor(ksq[:], kkr[:], kkr[:], ALU.mult), "ksq")
                for p in range(2):
                    own(V.tensor_scalar(k2[:, p, :], zf[:, 2 + p, :], par[:, 1, p:p + 1], None, ALU.mult), f"k2{p}")
                own(V.tensor_tensor(k1[:], zf[:, 2:4, :], k2[:], ALU.subtract), "k1")
                for p in range(2):
                    own(V.tensor_scalar(rrk[:, p, :], zf[:, p, :], par[:, 2, p:p + 1], None, ALU.mult), f"rrk{p}")

            def decay(n, d):
                own = lambda ins, name: prep_v.own(dve, n, ins, f"{name}{d}")
                prep_a.after(dve, n, f"tw1.{d}")
                own(V.tensor_scalar(lw[:], lw[:], 0.5 * DECAY, 0.5 * DECAY, ALU.mult, ALU.add), "lw")
                own(V.tensor_tensor_scan(flat(L[:]), flat(run1[:]), flat(lw[:]), 0.0, ALU.mult, ALU.add), "L")
                own(V.tensor_tensor(Lx[:], L[:], lw[:], ALU.subtract), "Lx")
                if d:
                    chunks = lambda a: a.rearrange("p a (c j) -> p (a c) j", j=CH)
                    end = chunks(L[:])[:, :, CH - 1:CH].to_broadcast([P, 8, CH])
                    own(V.tensor_tensor(chunks(inc[:]), end, chunks(Lx[:]), ALU.subtract), "inc")
                    own(V.tensor_tensor(chunks(exc[:]), end, chunks(L[:]), ALU.subtract), "exc")

            def rates(n, d):
                own = lambda ins, name: prep_v.own(dve, n, ins, f"{name}{d}")
                prep_a.after(dve, n, f"ta1.{d}")
                own(V.tensor_scalar(aa[:], aa[:], 0.5, 0.5, ALU.mult, ALU.add), "aa")
                own(V.tensor_tensor(kd[:], k2[:], aa[:], ALU.mult), "kdm")
                own(V.tensor_tensor(kd[:], kd[:], k1[:], ALU.add), "kd")
                own(V.tensor_copy(kds[:], kd[:]) if d == 0 else V.tensor_tensor(kds[:], kds[:], kd[:], ALU.add), "kds")

            def unit_keys(n):
                own = lambda ins, name: prep_v.own(dve, n, ins, name)
                prep_a.after(dve, n, "knorm")
                own(V.tensor_scalar(ksq[:], ksq[:], 1e-12, None, ALU.max), "kmax")
                own(V.reciprocal(ksq[:], ksq[:]), "krec")
                own(V.tensor_tensor(kk[:], kkr[:], ksq[:], ALU.mult), "kk")

            def hats(n, d):
                own = lambda ins, name: prep_v.own(dve, n, ins, f"{name}{d}")
                own(V.tensor_tensor(kka[:], kk[:], aa[:], ALU.mult), "kka")
                prep_a.after(dve, n, f"EN{d}")
                own(V.tensor_tensor(AR[:, d, 1, :, :], zf[:, 0:2, :], EI[:], ALU.mult), "R")
                own(V.scalar_tensor_tensor(AR[:, d, 0, :, :], kk[:], -1.0, EX[:], ALU.mult, ALU.mult), "A")
                own(V.tensor_tensor(Bh[:, d, :, :], kka[:], EN[:], ALU.mult), "B")
                own(V.tensor_tensor(Kh[:, d, :, :], kd[:], EN[:], ALU.mult), "K")

            def prologue():
                mix(0)
                keys(0)
                decay(0, 0)
                rates(0, 0)
                unit_keys(0)
                hats(0, 0)
                dve.wait_ge(masks.sem, N_MASKS)
                for d in range(2):
                    ident = s["ident"][:, :].rearrange("p (o t) -> p o t", o=1).to_broadcast([P, len(LEVELS) - 1, P])
                    consts_set.step(dve, V.tensor_tensor(lev[:, d, 1:, :], lev[:, d, 1:, :], ident, ALU.add))

            heads = lambda m: m.rearrange("p (o t) -> p o t", o=1).to_broadcast([P, 4, P])
            of_parity = lambda a, q: a.rearrange("p (m h) t -> p m h t", h=2)[:, :, q, :]
            bank = lambda b: ps[:, b, :].rearrange("p (h m t) -> p h m t", h=2, m=2)
            per_head = lambda b: ps[:, b, :].rearrange("p (h t) -> p h t", h=4)

            def unit(n, d, nxt):
                own = lambda ins, name: main_v.own(dve, n, ins, name)
                strict = tri[:, d, :, :].rearrange("p m (o t) -> p o m t", o=1).to_broadcast([P, 2, 2, P])
                for g in range(2):
                    main_p.after(dve, n, f"SB{g}.{d}")
                    for q in range(2):
                        for m in range(2):
                            ins = V.tensor_tensor(of_parity(MB[:, g, :, m, :], q), bank(2 + q)[:, :, m, :], strict[:, :, m, :], ALU.mult)
                            if m:
                                own(ins, f"MB{q}.{g}.{d}")
                    own(V.tensor_tensor(MB[:, g, :, 0, :], MB[:, g, :, 0, :], heads(s["ident"][:, :]), ALU.add), f"MI.{g}.{d}")
                    main_p.after(dve, n, f"SM{g}.{d}")
                    for q in range(2):
                        ab = ps[:, q, g * 256:(g + 1) * 256].rearrange("p (m t) -> p m t", m=2)
                        ins = V.tensor_tensor(of_parity(X[:, g, :, :], q), ab, heads(lev[:, d, 0, :])[:, 0:2, :], ALU.mult)
                    own(ins, f"Xa.{g}.{d}")
                    own(V.tensor_tensor(X[:, g, :, :], X[:, g, :, :], heads(s["ident"][:, :]), ALU.add), f"Xb.{g}.{d}")
                    own(V.tensor_tensor(Z[:, g, :, :], MB[:, g, :, 0, :], heads(lev[:, 1 - d, 0, :]), ALU.mult), f"Za.{g}.{d}")
                    own(V.tensor_tensor(Z[:, g, :, :], Z[:, g, :, :], heads(s["ident"][:, :]), ALU.add), f"Zb.{g}.{d}")
                    main_p.after(dve, n, f"SK{g}.{d}")
                    for q in range(2):
                        for m in range(2):
                            ins = V.tensor_tensor(of_parity(MK[:, g, :, m, :], q), bank(4 + q)[:, :, m, :], strict[:, :, m, :], ALU.mult)
                            if m:
                                own(ins, f"MK{q}.{g}.{d}")
                for v in range(1, 6):
                    for g in range(2):
                        main_p.after(dve, n, f"G{v}.{g}.{d}")
                        own(V.tensor_tensor(G[:, g, :, :], per_head(g), heads(lev[:, d, v, :]), ALU.mult), f"G{v}.{g}.{d}")
                    if nxt is None:
                        continue
                    if v == 1 and d:
                        mix(nxt[0])
                    if v == 2 and d:
                        keys(nxt[0])
                    if v == 3:
                        decay(*nxt)
                    if v == 4:
                        rates(*nxt)
                if nxt:
                    if d:
                        unit_keys(nxt[0])
                    hats(*nxt)
                    if d == 0:
                        prep_v.own(dve, n, V.tensor_tensor(kds[:], kds[:], rrk[:], ALU.mult), "bt")
                for g in range(2):
                    main_p.after(dve, n, f"GY{g}.{d}")
                    main_a.after(dve, n, f"Y{g}.{d}")
                    if g == 0 and not (isinstance(n, int) and n == 0 and d == 0):
                        dve.wait_ge(g_stored, (n * 2 + d) * 16)
                    gy = ps[:, 4 + g, :].rearrange("p (q m t) -> p q m t", q=2, m=2)
                    own(V.tensor_tensor(gst[:, :, g * P:(g + 1) * P], gy[:, 0, :, :], AR[:, d, 1, :, g * P:(g + 1) * P], ALU.add), f"Gs{g}.{d}")
                main_p.after(dve, n, f"PQ{d}")
                prep_a.after(dve, n, f"tot{d}")
                for c in range(2):
                    pq = ps[:, c, :].rearrange("p (g q m j) -> p g q m j", g=2, q=2, m=2)
                    to = lambda st: st[:, d, bass.ds(n * 4, 4), :, :].rearrange("p (g c) m j -> p g c m j", c=2)[:, :, c, :, :]
                    tt = tot[:, d, bass.ds(n * 4, 4), :].rearrange("p (g c) (m o) -> p g c m o", c=2, o=1)[:, :, c, :, :]
                    eye = i64[:, :].rearrange("p (a b j) -> p a b j", a=1, b=1).to_broadcast([P, 2, 2, CH])
                    own(V.tensor_tensor(to(Pst), pq[:, :, 0, :, :], eye, ALU.add), f"P{c}.{d}")
                    own(V.tensor_tensor(to(Qst), pq[:, :, 1, :, :], tt.to_broadcast([P, 2, 2, CH]), ALU.mult), f"Q{c}.{d}")
                if d == 0:
                    prep_p.after(dve, n, "bonus")
                    if not (isinstance(n, int) and n == 0):
                        dve.wait_ge(b_stored, n * 16)
                    prep_v.own(dve, n, V.tensor_tensor(bst[:], ps[:, 6, :].rearrange("p (m t) -> p m t", m=2), zf[:, 4:6, :], ALU.mult), "bonus")
            units(dve, prologue, unit)

        @block.scalar
        def _(act):
            act.wait_ge(consts_set.sem, 5)

            def scaled(n):
                act.wait_ge(z_in, n * 16 + 16)
                prep_v.earlier(act, n, "bonus")
                for j in range(7):
                    prep_a.own(act, n, A.activation(zf[:, j, :], zin[:, j, 1:RB + 1], ACT.Copy, scale=omu[:, j:j + 1]), f"scaled{j}")

            def tanh_lo(n):
                prep_v.after(act, n, "mix6")
                prep_a.own(act, n, A.activation(th[:], zf[0:CH, 6, :], ACT.Tanh), "th")

            def rate(n, d, name, to, bias):
                prep_p.after(act, n, f"{name}{d}")
                for m in range(2):
                    prep_a.own(act, n, A.activation(to[:, m, :], ps[:, 6, m * RB:(m + 1) * RB], ACT.Tanh, scale=0.5, bias=hpar[:, bias + d, m:m + 1]),
                               f"{name}{m}.{d}")

            def key_norm(n):
                prep_p.after(act, n, "ksum")
                prep_a.own(act, n, A.activation(flat(ksq[:]), ps[:, 7, :], ACT.Sqrt), "knorm")

            def exps(n, d):
                own = lambda ins, name: prep_a.own(act, n, ins, f"{name}{d}")
                prep_v.after(act, n, "exc1" if d else "Lx0")
                own(A.activation(EI[:], (inc if d else L)[:], ACT.Exp), "EI")
                own(A.activation(EX[:], (exc if d else Lx)[:], ACT.Exp), "EX")
                own(A.activation(EN[:], (inc if d else L)[:], ACT.Exp, scale=-1.0), "EN")
                edge = 0 if d else CH - 1
                whole = EI[:].rearrange("p m (c j) -> p c m j", j=CH)[:, :, :, edge:edge + 1]
                own(A.copy(tot[:, d, bass.ds(n * 4, 4), :].rearrange("p c (m o) -> p c m o", o=1), whole), "tot")

            def prologue():
                scaled(0)
                tanh_lo(0)
                rate(0, 0, "tw", lw, 0)
                rate(0, 0, "ta", aa, 2)
                key_norm(0)
                exps(0, 0)

            per_head = lambda b: ps[:, b, :].rearrange("p (h t) -> p h t", h=4)

            def unit(n, d, nxt):
                own = lambda ins, name: main_a.own(act, n, ins, f"{name}{d}")
                if nxt and d:
                    scaled(nxt[0])

                def level(v, g):
                    for x, to in (("X", X), ("Z", Z)):
                        if v < 5 or x == "Z":
                            main_p.after(act, n, f"{x}{v}.{g}.{d}")
                            own(A.copy(to[:, g, :, :], per_head((2 if x == "X" else 4) + g)), f"{x}{v}.{g}.")

                def kept_rows(v):
                    main_p.after(act, n, f"T{v}.{d}")
                    if v < 3:
                        own(A.copy(WI[:, v - 1, :, 0:CH], ps[:, 7, 0:256].rearrange("p (h j) -> p h j", h=4)), f"At{v - 1}.")
                        own(A.copy(Bt[:, v - 1, :], ps[:, 7, 256:512]), f"Bt{v - 1}.")
                    else:
                        own(A.copy(flat((Kt if v == 3 else Vt)[:]), ps[:, 7, :]), "Kt." if v == 3 else "V.")
                for v in range(1, 5):
                    if v == 2 and nxt and d:
                        tanh_lo(nxt[0])
                    if v == 3 and nxt:
                        rate(*nxt, "tw", lw, 0)
                    if v == 4 and nxt:
                        rate(*nxt, "ta", aa, 2)
                    level(v, 0)
                    level(v, 1)
                    if v < 4 or d == 0:
                        kept_rows(v)
                if nxt:
                    if d:
                        key_norm(nxt[0])
                    exps(*nxt)
                for g in range(2):
                    level(5, g)
                    main_p.after(act, n, f"MV{g}.{d}")
                    for q in range(2):
                        mv = ps[:, g, :].rearrange("p (m h t) -> p m h t", m=2, h=2)[:, :, q, q * CH:(q + 1) * CH]
                        own(A.copy(WI[:, g, :, :].rearrange("p (m h) t -> p m h t", h=2)[:, :, q, CH:P], mv), f"MV{q}.{g}.")
                for g in range(2):
                    main_p.after(act, n, f"W{g}.{d}")
                    own(A.copy(W[:, g, :, :], per_head(2 + g)), f"W{g}.")
                for g in range(2):
                    main_p.after(act, n, f"GY{g}.{d}")
                    if g == 0 and not (isinstance(n, int) and n == 0 and d == 0):
                        act.wait_ge(y_stored, (n * 2 + d) * 16)
                    own(A.copy(yst[:, :, g * P:(g + 1) * P], ps[:, 4 + g, 256:512].rearrange("p (m t) -> p m t", m=2)), f"Y{g}.")
            units(act, prologue, unit)

        @block.tensor
        def _(pe):
            mm = lambda o, l, r, start=True, stop=True: T.matmul(o, l, r, start=start, stop=stop)
            half = lambda h: slice((h % 2) * CH, (h % 2 + 1) * CH)

            def w_lora(n, d):
                prep_a.after(pe, n, "th" if d == 0 else "ta1.0")
                if d == 0:
                    prep_v.earlier(pe, n, "bonus")
                for p in range(2):
                    last = mm(ps[:, 6, p * RB:(p + 1) * RB], lora[0:CH, d, p * P:(p + 1) * P], th[:])
                prep_p.done(last, f"tw{d}")

            def a_lora(n, d):
                prep_a.after(pe, n, f"tw1.{d}")
                for p in range(2):
                    last = mm(ps[:, 6, p * RB:(p + 1) * RB], lora[CH:P, d, p * P:(p + 1) * P], zf[CH:P, 6, :])
                prep_p.done(last, f"ta{d}")

            def key_sums(n):
                prep_v.after(pe, n, "ksq")
                prep_p.done(mm(ps[:, 7, :], J[:], flat(ksq[:])), "ksum")

            def prologue():
                w_lora(0, 0)
                a_lora(0, 0)
                key_sums(0)

            def unit(n, d, nxt):
                done = lambda ins, name: main_p.done(ins, f"{name}{d}")

                def before(results, name):
                    if d:
                        results.after(pe, n, f"{name}.0")
                    else:
                        results.earlier(pe, n, f"{name}.1")
                prep_v.after(pe, n, f"K{d}")
                before(main_a, "W1")
                for g in range(2):
                    tok = slice(g * P, (g + 1) * P)
                    if g:
                        main_v.after(pe, n, f"MB1.0.{d}")
                    for p in range(2):
                        for h in (2 * p, 2 * p + 1):
                            last = mm(ps[:, 2 + h % 2, p * 256:(p + 1) * 256], Bh[half(h), d, p, tok], AR[half(h), d, :, p, tok])
                    done(last, f"SB{g}.")
                    if g:
                        main_v.after(pe, n, f"Xa.0.{d}")
                    else:
                        before(main_v, "Q1")
                    for h in range(4):
                        p = h // 2
                        last = mm(ps[:, h % 2, g * 256 + p * P:g * 256 + (p + 1) * P], AR[half(h), d, 0, p, tok], Bh[half(h), d, p, tok])
                    done(last, f"SM{g}.")
                    if g:
                        main_v.after(pe, n, f"MK1.0.{d}")
                    else:
                        before(main_a, "Y1")
                    for p in range(2):
                        for h in (2 * p, 2 * p + 1):
                            last = mm(ps[:, 4 + h % 2, p * 256:(p + 1) * 256], Kh[half(h), d, p, tok], AR[half(h), d, :, p, tok])
                    done(last, f"SK{g}.")

                def turn_rows(v):
                    if v == 1:
                        if d:
                            main_a.after(pe, n, "V.0")
                        else:
                            prep_a.after(pe, n, "knorm")
                    else:
                        main_a.after(pe, n, f"Bt0.{d}" if v == 2 else f"Bt1.{d}" if v == 3 else f"Kt.{d}")
                    if v < 3:
                        tok = slice((v - 1) * P, v * P)
                        for p in range(2):
                            T.transpose(ps[:, 7, p * P:(p + 1) * P], AR[:, d, 0, p, tok], s["ident"][:])
                        for p in range(2):
                            last = T.transpose(ps[:, 7, 256 + p * P:256 + (p + 1) * P], Bh[:, d, p, tok], s["ident"][:])
                    else:
                        for g in range(2):
                            for p in range(2):
                                src = Kh[:, d, p, g * P:(g + 1) * P] if v == 3 else zf[:, 4 + p, g * P:(g + 1) * P]
                                last = T.transpose(ps[:, 7, g * 256 + p * P:g * 256 + (p + 1) * P], src, s["ident"][:])
                    done(last, f"T{v}.")
                for v in range(1, 6):
                    for g in range(2):
                        if v == 1:
                            main_v.after(pe, n, f"Xb.1.{d}")
                        else:
                            main_a.after(pe, n, f"X{v - 1}.{g}.{d}")
                        for h in range(4):
                            last = mm(ps[:, g, h * P:(h + 1) * P], MB[:, g, h, 0, :], X[:, g, h, :])
                        done(last, f"G{v}.{g}.")
                    if v < 4 or (v == 4 and d == 0):
                        turn_rows(v)
                    if nxt and v == 2:
                        w_lora(*nxt)
                    if nxt and v == 3:
                        a_lora(*nxt)
                    if nxt and v == 4 and d:
                        main_a.after(pe, n, "Kt.1")
                        key_sums(nxt[0])
                    for g in range(2):
                        main_v.after(pe, n, f"G{v}.{g}.{d}")
                        if v > 1:
                            main_a.after(pe, n, f"Z{v - 1}.{g}.{d}")
                        if v < 5:
                            for h in range(4):
                                last = mm(ps[:, 2 + g, h * P:(h + 1) * P], Z[:, g, h, :], G[:, g, h, :])
                            done(last, f"X{v}.{g}.")
                        for h in range(4):
                            last = mm(ps[:, 4 + g, h * P:(h + 1) * P], G[:, g, h, :], Z[:, g, h, :])
                        done(last, f"Z{v}.{g}.")
                        if v == 5:
                            if g == 0:
                                main_a.after(pe, n, f"V.0")
                            for h in range(4):
                                last = mm(ps[:, g, h * P:(h + 1) * P], MK[:, g, h, 0, :], Vt[:, g, (h // 2) * P:(h // 2 + 1) * P])
                            done(last, f"MV{g}.")
                for g in range(2):
                    main_a.after(pe, n, f"MV1.{g}.{d}")
                    for h in range(4):
                        last = mm(ps[:, 2 + g, h * P:(h + 1) * P], Z[:, g, h, :], WI[:, g, h, :])
                    done(last, f"W{g}.")
                for g in range(2):
                    main_a.after(pe, n, f"W{g}.{d}")
                    for h in range(4):
                        p = h // 2
                        mm(ps[half(h), 4 + g, p * P:(p + 1) * P], W[:, g, h, 0:CH], MB[:, g, h, 1, :])
                        o = ps[half(h), 4 + g, 256 + p * P:256 + (p + 1) * P]
                        mm(o, W[:, g, h, CH:P], MB[:, g, h, 1, :], stop=False)
                        last = mm(o, Vt[:, g, h * CH:(h + 1) * CH], MK[:, g, h, 1, :], start=False)
                    done(last, f"GY{g}.")
                if d == 0:
                    prep_v.after(pe, n, "bt")
                    prep_p.done(mm(ps[:, 6, :], J[:], flat(kds[:])), "bonus")
                for g in range(2):
                    for h in range(4):
                        at = g * 256 + (h // 2) * CH
                        for part in range(3):
                            for c in range(2):
                                rows = slice(c * CH, (c + 1) * CH)
                                bh = Bt[rows, g, h * CH:(h + 1) * CH]
                                o_p, o_q = (ps[half(h), c, at + i * P:at + i * P + CH] for i in range(2))
                                if part == 0:
                                    mm(o_p, W[rows, g, h, 0:CH], bh)
                                elif part == 1:
                                    mm(o_q, bh, W[rows, g, h, CH:P], stop=False)
                                else:
                                    last = mm(o_q, Kt[rows, g, h * CH:(h + 1) * CH], Vt[rows, g, h * CH:(h + 1) * CH], start=False)
                done(last, "PQ")
            units(pe, prologue, unit)


def recurrence_stage(nc, t, s):
    with ExitStack() as ctx:
        chain = {"P": ctx.enter_context(nc.sbuf_tensor("chunk_p", [P, 2, NC_ALL, 2, CH], F32)),
                 "Q": ctx.enter_context(nc.sbuf_tensor("chunk_q", [P, 2, NC_ALL, 2, CH], F32)),
                 "tot": ctx.enter_context(nc.sbuf_tensor("chunk_decay", [P, 2, NC_ALL, 2], F32))}
        recurrence_local_stage(nc, t, s, chain)
        recurrence_chain_stage(nc, t, s, chain)


def recurrence_chain_stage(nc, t, s, chain):
    with ExitStack() as ctx:
        sb = lambda name, shape, dt=F32: ctx.enter_context(nc.sbuf_tensor(name, shape, dt))
        sem = lambda name: ctx.enter_context(nc.semaphore(name))
        CL, CC, NCK = SEQ // CH, CTX // CH, BLK // P
        CHAIN_STEPS = (NC_ALL - 2) // NB
        S = sb("states", [P, CL + 1, 2, 2, CH])
        Sc = sb("ctx_states", [P, CC, 2, 2, CH])
        gt, rg = sb("g_in", [P, 2, 2, 2, BLK]), sb("rw_gate", [P, 2, 2, BLK])
        gn = sb("gn_params", [P, 2, 2])
        gin = sb("gm_in", [P, 2, 6, BLK])
        sq, rstd, dev, gout = sb("norm_sq", [P, 2, BLK]), sb("norm_rstd", [P, 2, BLK]), sb("norm_dev", [P, 2, BLK]), sb("gm_out", [P, 2, BLK])
        vrow = sb("gm_v_rows", [P, NCK, BR])
        wraw, wt = sb("gm_w", [P, 4, P]), sb("gm_w_t", [P, 4, P])
        lnp, bs = sb("gm_ln", [P, 2, 2]), sb("gm_bias", [P, 2, P])
        jm = s["head_mean"]
        pad = sb("rpb_padded", [4 * NDR, 2 * GRID - 1])
        pad_set, rpb_in, pad_out = sem("rpb_pad_set"), sem("rpb_in"), sem("rpb_pad_out")
        ps = ctx.enter_context(nc.psum_tensor("chain_ps", [P, 8, BLK], F32))
        p_done, s_done = sem("state_products"), sem("states_done")
        gn_in, g_in, y_in, step = sem("gn_in"), [sem(f"g_in{i}") for i in range(2)], [sem(f"chain_y_in{i}") for i in range(2)], Signal(ctx, nc, "chain_step")
        o_ps, mean_ps, var_ps, o_ready, dev_ready, root_done, silu_done, stored, out_ready = (sem(n) for n in (
            "o_ps", "mean_ps", "var_ps", "o_ready", "dev_ready", "rw_root_done", "rw_silu_done", "rw_stored", "rw_out_ready"))
        gm_in = [sem(f"gm_in{i}") for i in range(2)]
        w_in, bias_in, gm_stored, wt_ps, wt_set = (sem(n) for n in ("gm_w_in", "gm_bias_in", "gm_stored", "gm_w_turned", "gm_w_set"))
        act_r = Results(ctx, nc, "gm_scalar", ["v", "u", "g", "sqrt", "rows0", "rows1"])
        vec_r = Results(ctx, nc, "gm_vector", ["dev", "sq", "rec", "n1", "ln", "m", "mu", "mg"])
        pe_r = Results(ctx, nc, "gm_products", ["mean", "var", "rows", "mixed"])
        block = ctx.enter_context(nc.Block())
        V, A, T = nc.vector, nc.scalar, nc.tensor
        half = lambda h: slice(h * CH, (h + 1) * CH)
        z = lambda a, c: t["zT"][a:a + 2, :, c].rearrange("m p t -> p m t")

        @block.sync
        def _(sp):
            def load_gm(b):
                c = slice(Z_LAT + b * BLK, Z_LAT + (b + 1) * BLK)
                for n, a in enumerate((T_GV, T_GU, T_GG)):
                    at = (2, 0, 4)[n]
                    sp.dma_start(gin[:, b % 2, at:at + 2, :], z(a, c)).then_inc(gm_in[b % 2], 16)

            def load_rw(b):
                lat = slice(CTX + b * BLK, CTX + (b + 1) * BLK)
                par = b % 2
                sp.dma_start(gt[:, par, :, :, :], t["gT"][:, :, :, lat].rearrange("d m p t -> p d m t")).then_inc(g_in[par], 16)
                for d in range(2):
                    sp.dma_start(gin[:, par, 2 * d:2 * d + 2, :], t["yT"][d, :, :, lat].rearrange("m p t -> p m t")).then_inc(y_in[par], 16)
                sp.dma_start(gin[:, par, 4:6, :], t["bonusT"][:, :, lat].rearrange("m p t -> p m t")).then_inc(y_in[par], 16)
                sp.dma_start(rg[:, par, :, :], z(T_RG, slice(Z_LAT + b * BLK, Z_LAT + (b + 1) * BLK))).then_inc(y_in[par], 16)
            load_gm(0)
            sp.wait_ge(pad_set, 1)
            sp.dma_start(pad[:, GRID - 16:GRID + 15], t["na_rpb"].rearrange("l h r c -> (l h r) c")).then_inc(rpb_in, 16)
            sp.dma_start(wraw[:], t["gm_ws"].rearrange("l g p q -> p (l g) q")).then_inc(w_in, 16)
            for n, name in enumerate(("gm_ln_g", "gm_ln_b")):
                sp.dma_start(lnp[:, n, :], t[name].rearrange("l (m h) n -> (h n) (l m)", h=2)).then_inc(bias_in, 16)
            for g in range(4):
                sp.dma_start(bs[half(g % 2), g // 2, :], t["gm_bs"][0, g:g + 1, :].to_broadcast([CH, P])).then_inc(bias_in, 16)
            load_gm(1)
            sp.dma_start(gn[:, 0, :], t["rw_gn_g"].rearrange("l (m p) -> p (l m)", p=P)).then_inc(gn_in, 16)
            sp.dma_start(gn[:, 1, :], t["rw_gn_b"].rearrange("l (m p) -> p (l m)", p=P)).then_inc(gn_in, 16)
            sp.wait_ge(rpb_in, 16)
            src = pad[:].rearrange("r (a c) -> r a c", a=1).to_broadcast([4 * NDR, GRID, 2 * GRID - 1])
            sp.dma_start(t["rpbPad"][:, :, 0:2 * GRID - 1], src).then_inc(pad_out, 16)
            for b in range(NB):
                vec_r.after(sp, b, "mg")
                sp.dma_start(t["branchT"][0:2, :, b * BLK:(b + 1) * BLK].rearrange("m p t -> p m t"), gout[:]).then_inc(gm_stored, 16)
                if b + 2 < NB:
                    load_gm(b + 2)
                if b >= 2:
                    load_rw(b - 2)
            for b in range(NB):
                sp.wait_ge(out_ready, b + 1)
                sp.dma_start(t["branchT"][4:6, :, b * BLK:(b + 1) * BLK].rearrange("m p t -> p m t"), gout[:]).then_inc(stored, 16)
                if b + 2 < NB:
                    load_rw(b + 2)
            sp.wait_ge(pad_out, 16)
            sp.wait_ge(gm_stored, 16 * NB)
            sp.wait_ge(stored, 16 * NB)

        def chunk(d, i):
            if i < CC:
                return i if d == 0 else CC - 1 - i
            return i if d == 0 else NC_ALL - 1 - (i - CC)

        def state(d, p, i):
            return (Sc[:, i, d, p, :] if i < CC else S[:, i - CC, d, p, :])

        assert CHAIN_STEPS == 8

        @block.gpsimd
        def _(pool):
            nc.gpsimd.memset(pad[:], 0.0).then_inc(pad_set, 1)

        @block.tensor
        def _(pe):
            def chain_steps(b, *parts):
                for q in parts:
                    i = 1 + b * CHAIN_STEPS + q
                    for d in range(2):
                        pe.wait_ge(s_done, 4 * (i - 1) + 2 * d + 2)
                        for p in range(2):
                            for h in range(2):
                                last = T.matmul(ps[half(h), 6 + d, p * CH:(p + 1) * CH], chain["P"][half(h), d, chunk(d, i), p, :],
                                                state(d, p, i)[half(h), :], start=True, stop=True)
                        last.then_inc(p_done, 1)
            pe.wait_ge(w_in, 16)
            for g in range(4):
                last = T.transpose(ps[:, 4, g * P:(g + 1) * P], wraw[:, g, :], s["ident"][:])
            last.then_inc(wt_ps, 1)
            pe.wait_ge(wt_set, 1)
            for b in range(NB):
                act_r.after(pe, b, "v")
                for p in range(2):
                    last = T.matmul(ps[:, p, :], jm[:], gin[:, b % 2, 2 + p, :], start=True, stop=True)
                pe_r.done(last, "mean")
                chain_steps(b, 0, 1)
                vec_r.after(pe, b, "sq")
                for p in range(2):
                    last = T.matmul(ps[:, p, :], jm[:], sq[:, p, :], start=True, stop=True)
                pe_r.done(last, "var")
                chain_steps(b, 2, 3)
                vec_r.after(pe, b, "ln")
                for c in range(NCK):
                    for p in range(2):
                        last = T.transpose(ps[:, 2 + c // 2, (c % 2) * BR + p * P:(c % 2) * BR + (p + 1) * P], dev[:, p, c * P:(c + 1) * P], s["ident"][:])
                pe_r.done(last, "rows")
                chain_steps(b, 4, 5)
                act_r.after(pe, b, "rows1")
                for c in range(NCK):
                    for g in range(4):
                        last = T.matmul(ps[half(g % 2), 4 + g // 2, c * P:(c + 1) * P], vrow[:, c, g * CH:(g + 1) * CH], wt[:, g, :],
                                        start=True, stop=True)
                pe_r.done(last, "mixed")
                chain_steps(b, 6, 7)
            chain_steps(NB, *range((NC_ALL - 2) % NB))
            pe.wait_ge(s_done, 4 * (NC_ALL - 1))
            vec_r.after(pe, NB - 1, "mg")
            for b in range(NB):
                pe.wait_ge(g_in[b % 2], 16 * (b // 2) + 16)
                if b >= 1:
                    pe.wait_ge(o_ready, 2 * b)
                for c in range(8):
                    for p in range(2):
                        for d in range(2):
                            for h in range(2):
                                ch = CC + b * 8 + c
                                i = ch if d == 0 else NC_ALL - 1 - ch + CC
                                last = T.matmul(ps[half(h), p, c * CH:(c + 1) * CH], state(d, p, i)[half(h), :],
                                                gt[half(h), b % 2, d, p, c * CH:(c + 1) * CH], start=(d == 0), stop=(d == 1))
                last.then_inc(o_ps, 1)
                for p in range(2):
                    pe.wait_ge(o_ready, 2 * b + p + 1)
                    T.matmul(ps[:, 2 + p, :], jm[:], dev[:, p, :], start=True, stop=True).then_inc(mean_ps, 1)
                for p in range(2):
                    pe.wait_ge(dev_ready, 2 * b + p + 1)
                    T.matmul(ps[:, 4 + p, :], jm[:], sq[:, p, :], start=True, stop=True).then_inc(var_ps, 1)

        @block.scalar
        def _(act):
            act.wait_ge(wt_ps, 1)
            A.copy(wt[:], ps[:, 4, :].rearrange("p (g t) -> p g t", g=4)).then_inc(wt_set, 1)
            for b in range(NB):
                gi = gin[:, b % 2, :, :]
                act.wait_ge(gm_in[b % 2], 48 * (b // 2 + 1))
                act_r.own(act, b, A.activation(gi[:, 2:4, :], gi[:, 2:4, :], ACT.Gelu_apprx_tanh), "v")
                act_r.own(act, b, A.activation(gi[:, 0:2, :], gi[:, 0:2, :], ACT.Gelu_apprx_tanh), "u")
                act_r.own(act, b, A.activation(gi[:, 4:6, :], gi[:, 4:6, :], ACT.Silu), "g")
                pe_r.after(act, b, "var")
                vec_r.earlier(act, b, "rec")
                act_r.own(act, b, A.activation(rstd[:], ps[:, 0:2, :], ACT.Sqrt, bias=s["eps"][:]), "sqrt")
                pe_r.after(act, b, "rows")
                for n in range(2):
                    act_r.own(act, b, A.copy(vrow[:, 2 * n:2 * n + 2, :], ps[:, 2 + n, :].rearrange("p (c m) -> p c m", c=2)), f"rows{n}")
            for b in range(NB):
                act.wait_ge(y_in[b % 2], 64 * (b // 2 + 1))
                A.activation(rg[:, b % 2, :, :], rg[:, b % 2, :, :], ACT.Silu).then_inc(silu_done, 1)
                for p in range(2):
                    act.wait_ge(var_ps, 2 * b + p + 1)
                    A.activation(rstd[:, p, :], ps[:, 4 + p, :], ACT.Sqrt, bias=s["gn_eps"][:]).then_inc(root_done, 1)

        @block.vector
        def _(dve):
            own = lambda ins: step.step(dve, ins)

            def chain_steps(b, *parts):
                for q in parts:
                    i = 1 + b * CHAIN_STEPS + q
                    for d in range(2):
                        dve.wait_ge(p_done, 2 * (i - 1) + d + 1)
                        for p in range(2):
                            V.scalar_tensor_tensor(state(d, p, i + 1), ps[:, 6 + d, p * CH:(p + 1) * CH],
                                                   chain["tot"][:, d, chunk(d, i), p:p + 1], chain["Q"][:, d, chunk(d, i), p, :],
                                                   ALU.mult, ALU.add).then_inc(s_done, 1)
            for d in range(2):
                for p in range(2):
                    V.tensor_copy(state(d, p, 1), chain["Q"][:, d, chunk(d, 0), p, :]).then_inc(s_done, 1)
            dve.wait_ge(bias_in, 16 * 6)
            for b in range(NB):
                own_gm = lambda ins, name: vec_r.own(dve, b, ins, name)
                gi = gin[:, b % 2, :, :]
                pe_r.after(dve, b, "mean")
                own_gm(V.tensor_tensor(dev[:], gi[:, 2:4, :], ps[:, 0:2, :], ALU.subtract), "dev")
                chain_steps(b, 0)
                own_gm(V.tensor_tensor(sq[:], dev[:], dev[:], ALU.mult), "sq")
                chain_steps(b, 1)
                act_r.after(dve, b, "sqrt")
                own_gm(V.reciprocal(rstd[:], rstd[:]), "rec")
                chain_steps(b, 2)
                own_gm(V.tensor_tensor(dev[:], dev[:], rstd[:], ALU.mult), "n1")
                chain_steps(b, 3)
                for p in range(2):
                    last = V.tensor_scalar(dev[:, p, :], dev[:, p, :], lnp[:, 0, p:p + 1], lnp[:, 1, p:p + 1], ALU.mult, ALU.add)
                own_gm(last, "ln")
                chain_steps(b, 4, 5)
                pe_r.after(dve, b, "mixed")
                if b:
                    dve.wait_ge(gm_stored, 16 * b)
                for p in range(2):
                    last = V.tensor_tensor(gout[:, p, :].rearrange("p (c t) -> p c t", t=P), ps[:, 4 + p, :].rearrange("p (c t) -> p c t", t=P),
                                           bs[:, p:p + 1, :].to_broadcast([P, NCK, P]), ALU.add)
                own_gm(last, "m")
                chain_steps(b, 6)
                act_r.after(dve, b, "g")
                own_gm(V.tensor_tensor(gout[:], gout[:], gi[:, 0:2, :], ALU.mult), "mu")
                chain_steps(b, 7)
                own_gm(V.tensor_tensor(gout[:], gout[:], gi[:, 4:6, :], ALU.mult), "mg")
            chain_steps(NB, *range((NC_ALL - 2) % NB))
            dve.wait_ge(gn_in, 32)
            dve.wait_ge(gm_stored, 16 * NB)
            for b in range(NB):
                y0, y1, bonus = (gin[:, b % 2, 2 * n:2 * n + 2, :] for n in range(3))
                dve.wait_ge(y_in[b % 2], 64 * (b // 2 + 1))
                own(V.tensor_tensor(y0, y0, y1, ALU.add))
                dve.wait_ge(o_ps, b + 1)
                for p in range(2):
                    V.tensor_tensor(dev[:, p, :], ps[:, p, :], y0[:, p, :], ALU.add).then_inc(o_ready, 1)
                for p in range(2):
                    dve.wait_ge(o_ready, 2 * b + p + 1)
                    dve.wait_ge(mean_ps, 2 * b + p + 1)
                    step.mark(V.tensor_tensor(dev[:, p, :], dev[:, p, :], ps[:, 2 + p, :], ALU.subtract))
                for p in range(2):
                    dve.wait_ge(step.sem, step.n - 1 + p)
                    V.tensor_tensor(sq[:, p, :], dev[:, p, :], dev[:, p, :], ALU.mult).then_inc(dev_ready, 1)
                for p in range(2):
                    dve.wait_ge(root_done, 2 * b + p + 1)
                    own(V.reciprocal(rstd[:, p, :], rstd[:, p, :]))
                own(V.tensor_tensor(dev[:], dev[:], rstd[:], ALU.mult))
                for p in range(2):
                    last = V.tensor_scalar(dev[:, p, :], dev[:, p, :], gn[:, 0, p:p + 1], gn[:, 1, p:p + 1], ALU.mult, ALU.add)
                own(last)
                own(V.tensor_tensor(dev[:], dev[:], bonus, ALU.add))
                dve.wait_ge(silu_done, b + 1)
                if b >= 1:
                    dve.wait_ge(stored, 16 * b)
                V.tensor_tensor(gout[:], dev[:], rg[:, b % 2, :, :], ALU.mult).then_inc(out_ready, 1)


def attention_stage(nc, t, s):
    ROWS, KR, BAND = SEQ // GRID, 8, 8 * GRID
    PADW = 2 * GRID - 1
    KEYS = BAND + CTX
    with ExitStack() as ctx:
        sb = lambda name, shape, dt=F32: ctx.enter_context(nc.sbuf_tensor(name, shape, dt))
        sem = lambda name: ctx.enter_context(nc.semaphore(name))
        q, k, v = sb("q_t", [P, 2, SEQ]), sb("k_t", [P, 2, NT]), sb("v_t", [P, 2, NT])
        ng = sb("na_gate", [P, 2, SEQ])
        ve, vo = sb("v_even", [P, NT // P, BR]), sb("v_odd", [P, SEQ // P - 1, BR])
        bias = sb("na_bias", [P, 2, NDR * GRID])
        qs = sb("q_heads", [P, 2, 2, P])
        sband = sb("band_scores", [P, 2, BAND])
        pr = sb("probs", [P, 2, 2, KEYS])
        prt = sb("probs_t", [P, 2, KEYS])
        on = sb("o_rows", [P, 2, P])
        st = sb("softmax_stats", [P, 2, 2, 5])
        rsum = sb("softmax_rsum", [P, 2, 2])
        EDGE = 8
        pp, s2, s4, s8 = (sb(n, [P, SEQ + 2 * EDGE]) for n in ("pool_in", "pool_2", "pool_4", "pool_8"))
        dd, pg = sb("pool_diff", [P, 2, SEQ]), sb("pool_gate", [P, 2, SEQ])
        edge = sb("pool_edge", [P, 2, 2, EDGE])
        plw, pls = sb("pool_w", [P, 2, P]), sb("pool_scale", [P, 2])
        ps = ctx.enter_context(nc.psum_tensor("na_ps", [P, 8, BLK], F32))
        pool_in, pg_in, plw_in, plw_set, diff_set = (sem(n) for n in ("pool_in", "pool_gate_in", "pool_w_in", "pool_w_set", "pool_diff_set"))
        pl_ps, pl_out, pl_silu, pl_stored = sem("pool_products"), sem("pool_out_ready"), sem("pool_silu"), sem("pool_stored")
        estep, pstep = Signal(ctx, nc, "pool_edge_step"), Signal(ctx, nc, "pool_step")
        loads = {n: sem("na_in_" + n) for n in ("q", "k", "v", "g")}
        bias_in, bias_set = sem("bias_in"), Signal(ctx, nc, "bias_set")
        silu_done, v_turned, v_copied = sem("na_silu"), sem("v_turned"), sem("v_copied")
        qz = sem("q_zeroed")
        front = lambda name, r: Results(ctx, nc, name, r)
        fs = front("front_scalar", ["q0", "q1"] + [f"{n}{p}" for p in range(2) for n in ("e", "c")])
        fp = front("front_products", ["S0", "S1"])
        fv = front("front_vector", [f"{n}{p}" for p in range(2) for n in ("m", "b", "n")])
        bv = front("back_vector", ["P0", "P1", "s", "r", "o", "g"])
        bs = front("back_scalar", ["P0", "P1"])
        bp = front("back_products", ["T0", "T1", "O", "OT"])
        stored = sem("na_stored")
        block = ctx.enter_context(nc.Block())
        V, A, T = nc.vector, nc.scalar, nc.tensor
        half = lambda h: slice(h * CH, (h + 1) * CH)

        def place(r):
            start = min(max(r - 4, 0), ROWS - KR)
            return start, start % 2, (start - r + KR - 1) * GRID

        def steps(eng, step):
            def short(r):
                step(r if r < ROWS else None, place(r), r - 1 if 1 <= r <= ROWS else None, place(r - 1), r - 2 if r >= 2 else None, r % 2)
            for r in range(5):
                short(r)
            with eng.Fori(0, 12) as n:
                for u in range(2):
                    step(n * 2 + (5 + u), (n * 2 + (1 + u), (1 + u) % 2, (KR - 5) * GRID),
                         n * 2 + (4 + u), (n * 2 + u, u % 2, (KR - 5) * GRID, n), n * 2 + (3 + u), (5 + u) % 2)
            for r in range(29, ROWS + 2):
                short(r)

        @block.sync
        def _(sp):
            lat = slice(Z_LAT, Z_LAT + SEQ)
            z = lambda a, c: t["zT"][a:a + 2, :, c].rearrange("m p t -> p m t")
            sp.dma_start(v[:, :, 0:CTX], z(T_V, slice(Z_CTX, Z_CTX + CTX))).then_inc(loads["v"], 16)
            sp.dma_start(v[:, :, CTX:NT], z(T_V, lat)).then_inc(loads["v"], 16)
            for p in range(2):
                for h in range(2):
                    src = bass.AP(tensor=t["rpbPad"].tensor, offset=(2 * p + h) * NDR * GRID * 2 * GRID + GRID - 1,
                                  ap=[[PADW, GRID], [GRID * 2 * GRID, NDR], [1, GRID]])
                    sp.dma_start(bias[half(h), p, :].rearrange("q (r c) -> q r c", c=GRID), src).then_inc(bias_in, 16)
            sp.dma_start(k[:, :, 0:CTX], z(T_K, slice(Z_CTX, Z_CTX + CTX))).then_inc(loads["k"], 16)
            sp.dma_start(k[:, :, CTX:NT], z(T_K, lat)).then_inc(loads["k"], 16)
            sp.dma_start(q[:], z(T_Q, lat)).then_inc(loads["q"], 16)
            sp.dma_start(ng[:], z(T_NG, lat)).then_inc(loads["g"], 16)
            sp.dma_start(pp[:, EDGE:EDGE + SEQ], t["zT"][T_PP, :, lat]).then_inc(pool_in, 16)
            sp.dma_start(pg[:], z(T_PG, lat)).then_inc(pg_in, 16)
            sp.wait_ge(plw_set, 1)
            for g in range(4):
                sp.dma_start(plw[half(g % 2), g // 2, half(g % 2)], t["pl_w"][0, g, :, :]).then_inc(plw_in, 16)
            sp.dma_start(pls[:], t["pl_scale"].rearrange("l (m p) -> p (l m)", p=P)).then_inc(plw_in, 16)
            sp.wait_ge(diff_set, 1)
            sp.dma_start(pp[:, EDGE:EDGE + SEQ], t["zT"][T_PP + 1, :, lat]).then_inc(pool_in, 16)
            bv.after(sp, ROWS - 1, "g")
            sp.dma_start(t["branchT"][2:4, :, :].rearrange("m p t -> p m t"), ng[:]).then_inc(stored, 16)
            sp.wait_ge(pl_out, NB)
            sp.dma_start(t["branchT"][6:8, :, :].rearrange("m p t -> p m t"), pg[:]).then_inc(pl_stored, 16)
            sp.wait_ge(stored, 16)
            sp.wait_ge(pl_stored, 16)

        @block.gpsimd
        def _(pool):
            nc.gpsimd.memset(qs[:], 0.0).then_inc(qz, 1)
            pool.wait_ge(bias_in, 16 * 4)
            for h in range(2):
                w = bias[half(h), :, :].rearrange("p m (r c) -> p (m r) c", c=GRID)
                bias_set.step(pool, nc.gpsimd.affine_select(out=w[:, :, 0:GRID - 16], in_=w[:, :, 0:GRID - 16], compare_op=ALU.is_ge,
                                                            fill=-1e30, base=8, pattern=[[0, 2 * NDR], [1, GRID - 16]], channel_multiplier=-1))
                bias_set.step(pool, nc.gpsimd.affine_select(out=w[:, :, 16:GRID], in_=w[:, :, 16:GRID], compare_op=ALU.is_gt,
                                                            fill=-1e30, base=8 - 16, pattern=[[0, 2 * NDR], [-1, GRID - 16]], channel_multiplier=1))

            nc.gpsimd.memset(plw[:], 0.0).then_inc(plw_set, 1)
            estep.step(pool, nc.gpsimd.memset(edge[:], 1.0))
            for g, w in enumerate((2, 4, 8, 16)):
                r = w // 2
                for i in range(r):
                    estep.step(pool, nc.gpsimd.memset(edge[half(g % 2), g // 2, 0, i:i + 1], w / (i + r)))
                for i in range(EDGE - (r - 1), EDGE):
                    estep.step(pool, nc.gpsimd.memset(edge[half(g % 2), g // 2, 1, i:i + 1], w / (r + EDGE - i)))
            for side in (0, SEQ + EDGE):
                estep.step(pool, nc.gpsimd.memset(pp[:, side:side + EDGE], 0.0))
            step = lambda ins: pstep.step(pool, ins)
            G = nc.gpsimd
            W = SEQ + 2 * EDGE
            mid = slice(EDGE, EDGE + SEQ)
            for p in range(2):
                pool.wait_ge(pool_in, 16 * (p + 1))
                step(G.tensor_tensor(s2[:, 1:W], pp[:, 0:W - 1], pp[:, 1:W], ALU.add))
                step(G.tensor_tensor(s4[:, 2:W - 1], s2[:, 1:W - 2], s2[:, 3:W], ALU.add))
                if p:
                    step(G.tensor_tensor(s8[:, 4:W - 3], s4[:, 2:W - 5], s4[:, 6:W - 1], ALU.add))
                    step(G.tensor_tensor(s2[half(1), 8:W - 7], s8[half(1), 4:W - 11], s8[half(1), 12:W - 3], ALU.add))
                for h, src in enumerate((s8, s2) if p else (s2, s4)):
                    c, w = half(h), 2 << (2 * p + h)
                    for side, cols in ((0, slice(EDGE, 2 * EDGE)), (1, slice(SEQ, SEQ + EDGE))):
                        step(G.tensor_tensor(src[c, cols], src[c, cols], edge[c, p, side, :], ALU.mult))
                    step(G.tensor_scalar(src[c, mid], src[c, mid], 1.0 / w, None, ALU.mult))
                    last = G.tensor_tensor(dd[c, p, :], src[c, mid], pp[c, mid], ALU.subtract)
                    step(last)
                pool.sem_inc(diff_set, 1)

        @block.scalar
        def _(act):
            for n in range(17):
                act.wait_ge(v_turned, n + 1)
                dst = ve[:, 2 * n:2 * n + 2, :] if n < 9 else vo[:, 2 * (n - 9):min(2 * (n - 9) + 2, 15), :]
                w = dst.shape[1]
                A.copy(dst, ps[:, n % 4, 0:w * BR].rearrange("p (a c) -> p a c", c=BR)).then_inc(v_copied, 1)
            act.wait_ge(loads["q"], 16)
            act.wait_ge(qz, 1)

            def queries(r, par):
                for h in range(2):
                    fs.own(act, r, A.activation(qs[half(h), par, :, half(h)], q[half(h), :, bass.ds(r * GRID, GRID)],
                                                ACT.Copy, scale=CH ** -0.5), f"q{h}")

            def step(r, at, before, at_before, last, par):
                for p in range(2):
                    if before is not None:
                        bp.after(act, before, f"T{p}")
                        bs.own(act, before, A.copy(prt[:, p, 0:BAND], ps[:, 4 + p, :]), f"P{p}")
                    if r is not None:
                        fv.after(act, r, f"n{p}")
                        fs.own(act, r, A.activation(pr[:, par, p, 0:BAND], sband[:, p, :], ACT.Exp, bias=st[:, par, p, 2:3],
                                                    accum_out=st[:, par, p, 3:4]), f"e{p}")
                        fs.own(act, r, A.activation(pr[:, par, p, BAND:KEYS], ps[:, 2 + p, 0:CTX], ACT.Exp, bias=st[:, par, p, 2:3],
                                                    accum_out=st[:, par, p, 4:5]), f"c{p}")
                if not (r is None or (isinstance(r, int) and r == ROWS - 1)):
                    queries(r + 1, 1 - par)
            queries(0, 0)
            act.wait_ge(loads["g"], 16)
            A.activation(ng[:], ng[:], ACT.Silu).then_inc(silu_done, 1)
            steps(act, step)
            act.wait_ge(pg_in, 16)
            A.activation(pg[:], pg[:], ACT.Silu).then_inc(pl_silu, 1)

        @block.vector
        def _(dve):
            dve.wait_ge(bias_set.sem, 4)

            def step(r, at, before, at_before, last, par):
                for p in range(2):
                    if r is not None:
                        win = at[2]
                        fp.after(dve, r, f"S{p}")
                        fv.done(V.reduce_max(st[:, par, p, 1:2], ps[:, 2 + p, 0:CTX], AX.X), f"m{p}")
                        fv.own(dve, r, V.tensor_tensor_reduce(out=sband[:, p, :], in0=ps[:, p, :], in1=bias[:, p, win:win + BAND], scale=1.0,
                                                              scalar=-3e38, op0=ALU.add, op1=ALU.max, accum_out=st[:, par, p, 0:1]), f"b{p}")
                        fv.own(dve, r, V.tensor_scalar(st[:, par, p, 2:3], st[:, par, p, 0:1], st[:, par, p, 1:2], -1.0, ALU.max, ALU.mult), f"n{p}")
                    if p == 0 and last is not None:
                        if isinstance(last, int) and last == 0:
                            dve.wait_ge(silu_done, 1)
                        bp.after(dve, last, "OT")
                        for h in range(2):
                            cols = ng[half(h), :, bass.ds(last * GRID, GRID)]
                            turned = ps[half(h), 7, BR:2 * BR].rearrange("c (p q) -> c p q", p=2)[:, :, half(h)]
                            ins = V.tensor_tensor(cols, turned, cols, ALU.mult)
                        bv.own(dve, last, ins, "g")
                    if before is not None:
                        bp.after(dve, before, f"T{p}")
                        bv.own(dve, before, V.tensor_copy(prt[:, p, BAND:KEYS], ps[:, 6, p * CTX:(p + 1) * CTX]), f"P{p}")
                if before is not None:
                    fs.after(dve, before, "c1")
                    old = st[:, 1 - par, :, :]
                    bv.own(dve, before, V.tensor_tensor(rsum[:, 0, :], old[:, :, 3], old[:, :, 4], ALU.add), "s")
                    bv.own(dve, before, V.reciprocal(rsum[:, 1, :], rsum[:, 0, :]), "r")
                    bp.after(dve, before, "O")
                    by_pair = rsum[:, 1, :].rearrange("p (m o) -> p m o", o=1).to_broadcast([P, 2, P])
                    bv.own(dve, before, V.tensor_tensor(on[:], ps[:, 7, 0:BR].rearrange("p (m c) -> p m c", m=2), by_pair, ALU.mult), "o")
            steps(dve, step)
            dve.wait_ge(plw_in, 16 * 5)
            dve.wait_ge(pl_silu, 1)
            for b in range(NB):
                dve.wait_ge(pl_ps, b + 1)
                for p in range(2):
                    gate = pg[:, p, b * BLK:(b + 1) * BLK]
                    last = V.scalar_tensor_tensor(gate, ps[:, 2 * (b % 2) + p, :], pls[:, p:p + 1], gate, ALU.mult, ALU.mult)
                last.then_inc(pl_out, 1)

        @block.tensor
        def _(pe):
            pe.wait_ge(loads["v"], 32)
            for n in range(17):
                if n >= 4:
                    pe.wait_ge(v_copied, n - 3)
                tiles = [P * a for a in (2 * n, 2 * n + 1)] if n < 9 else [CTX + CH + P * a for a in range(2 * (n - 9), min(2 * (n - 9) + 2, 15))]
                for a, c0 in enumerate(tiles):
                    for p in range(2):
                        last = T.transpose(ps[:, n % 4, a * BR + p * P:a * BR + (p + 1) * P], v[:, p, c0:c0 + P], s["ident"][:])
                last.then_inc(v_turned, 1)
            pe.wait_ge(v_copied, 17)
            pe.wait_ge(loads["k"], 32)

            def scores(r, par, p, start):
                fs.after(pe, r, "q1")
                T.matmul(ps[:, p, :], qs[:, par, p, :], k[:, p, bass.ds(start * GRID + CTX, BAND)], start=True, stop=True)
                fp.done(T.matmul(ps[:, 2 + p, 0:CTX], qs[:, par, p, :], k[:, p, 0:CTX], start=True, stop=True), f"S{p}")

            def turn_probs(r, par, p):
                fs.after(pe, r, f"c{p}")
                if p:
                    bv.after(pe, r, "P0")
                for j in range(6):
                    to = ps[:, 4 + p, j * P:(j + 1) * P] if j < 4 else ps[:, 6, p * CTX + (j - 4) * P:p * CTX + (j - 3) * P]
                    last = T.transpose(to, pr[:, par, p, j * P:(j + 1) * P], s["ident"][:])
                bp.done(last, f"T{p}")

            def values(r, p, start, vpar, win, tile=None):
                bs.after(pe, r, f"P{p}")
                bv.after(pe, r, f"P{p}")
                for j in range(6):
                    if j >= 4:
                        rhs = ve[:, j - 4, p * P:(p + 1) * P]
                    elif isinstance(start, int):
                        rhs = (vo[:, start // 2 + j, p * P:(p + 1) * P] if vpar else ve[:, 2 + start // 2 + j, p * P:(p + 1) * P])
                    else:
                        rhs = (vo if vpar else ve)[:, bass.ds(tile + (j if vpar else 2 + j), 1), p * P:(p + 1) * P]
                        rhs = rhs.rearrange("p a c -> p (a c)")
                    last = T.matmul(ps[:, 7, p * P:(p + 1) * P], prt[:, p, j * P:(j + 1) * P], rhs, start=(j == 0), stop=(j == 5))
                if p:
                    bp.done(last, "O")

            def step(r, at, before, at_before, last, par):
                if r is not None:
                    scores(r, par, 0, at[0])
                if last is not None:
                    bv.after(pe, last, "o")
                    for p in range(2):
                        ins = T.transpose(ps[:, 7, BR + p * P:BR + (p + 1) * P], on[:, p, :], s["ident"][:])
                    bp.done(ins, "OT")
                if before is not None:
                    turn_probs(before, 1 - par, 0)
                if r is not None:
                    scores(r, par, 1, at[0])
                if before is not None:
                    turn_probs(before, 1 - par, 1)
                    for p in range(2):
                        values(before, p, *at_before)
            steps(pe, step)
            pe.wait_ge(diff_set, 2)
            pe.wait_ge(plw_in, 16 * 5)
            bv.after(pe, ROWS - 1, "g")
            for b in range(NB):
                if b >= 2:
                    pe.wait_ge(pl_out, b - 1)
                for p in range(2):
                    last = T.matmul(ps[:, 2 * (b % 2) + p, :], plw[:, p, :], dd[:, p, b * BLK:(b + 1) * BLK], start=True, stop=True)
                last.then_inc(pl_ps, 1)


def merge_stage(nc, t, s):
    with ExitStack() as ctx:
        sb = lambda name, shape, dt=F32: ctx.enter_context(nc.sbuf_tensor(name, shape, dt))
        sem = lambda name: ctx.enter_context(nc.semaphore(name))
        b_hi, b_lo = sb("mb_hi", [P, 8, SEQ], F32R), sb("mb_lo", [P, 8, SEQ], F32R)
        raw = sb("mb_raw", [P, 4, SEQ // 2])
        w_raw, w_hi, w_lo = sb("mw_raw", [P, 4, 2, P]), sb("mw_hi", [P, 2, 4, 2, P], F32R), sb("mw_lo", [P, 2, 4, 2, P], F32R)
        gate, y, prod = sb("m_gate", [P, 2, SEQ]), sb("m_y", [P, 2, SEQ]), sb("m_prod", [P, SEQ])
        ps = ctx.enter_context(nc.psum_tensor("merge_ps", [P, 2, NB, BLK], F32))
        raw_in, gate_in = [sem(f"raw_in{i}") for i in range(4)], [sem("gate_in0"), sem("gate_in1")]
        raw_hi, w_loaded, w_hi_ready, w_lo_ready = (sem(n) for n in ("raw_hi", "mw_loaded", "mw_hi_ready", "mw_lo_ready"))
        raw_lo = [sem("raw_lo_even"), sem("raw_lo_odd")]
        proj_ps, gated, y_added, y_stored = sem("proj_ps"), sem("gated"), sem("y_added"), [sem("y_stored0"), sem("y_stored1")]
        block = ctx.enter_context(nc.Block())
        V, A, T = nc.vector, nc.scalar, nc.tensor
        NR = 16
        piece = lambda n: (n // 2, slice((n % 2) * (SEQ // 2), (n % 2 + 1) * (SEQ // 2)))
        w_brs = t["w_br"].rearrange("l i (k p) n -> p (l i k) n", p=P)

        def over_columns(eng, body):
            body(0, 0, 0)
            body(1, 1, 0)
            with eng.Fori(1, KT // 2 - 1) as n:
                body(n * 2, 0, n)
                body(n * 2 + 1, 1, n)
            body(KT - 2, 0, KT // 2 - 1)
            body(KT - 1, 1, KT // 2 - 1)
        is_int = lambda j, *of: isinstance(j, int) and j in of

        @block.sync
        def _(sp):
            def load_w(j):
                sp.dma_start(w_raw[:].rearrange("p i k n -> p (i k) n"), w_brs[:, :, bass.ds(j * P, P)]).then_inc(w_loaded, 16)

            load_w(0)
            for n in range(NR):
                m, cols = piece(n)
                if n >= 4:
                    sp.wait_ge(raw_lo[n % 2], n // 2 - 1)
                sp.dma_start(raw[:, n % 4, :], t["branchT"][m, :, cols]).then_inc(raw_in[n % 4], 16)
                if n in (3, 7):
                    sp.dma_start(gate[:, n // 4, :], t["gatesT"][8 * (n // 4), :, :]).then_inc(gate_in[n // 4], 16)

            def column(j, par, m):
                if not is_int(j, KT - 1):
                    sp.wait_ge(w_lo_ready, j + 1)
                    load_w(j + 1)
                for i in range(2 if is_int(j, KT - 1) else 4):
                    at = j + (8 * (i + 2) if i < 2 else 8 * (i - 2) + 1)
                    sp.wait_ge(gated, j * 4 + (i + 1))
                    sp.dma_start(gate[:, i % 2, :], t["gatesT"][bass.ds(at, 1), :, :].rearrange("a p t -> p (a t)")).then_inc(gate_in[i % 2], 16)
                sp.wait_ge(y_added, j * 4 + 4)
                sp.dma_start(t["mergedT"][bass.ds(j, 1), :, :].rearrange("a p t -> p (a t)"), y[:, par, :]).then_inc(y_stored[par], 16)
            over_columns(sp, column)
            for par in range(2):
                sp.wait_ge(y_stored[par], 16 * KT // 2)

        @block.gpsimd
        def _(pool):
            for n in range(0, NR, 2):
                m, cols = piece(n)
                pool.wait_ge(raw_hi, n + 1)
                nc.gpsimd.tensor_tensor(b_lo[:, m, cols], raw[:, n % 4, :], b_hi[:, m, cols].bitcast(F32), ALU.subtract).then_inc(raw_lo[n % 2], 1)

        @block.scalar
        def _(act):
            def split_w(j, par, m):
                if is_int(j, 0):
                    act.wait_ge(w_loaded, 16)
                    A.copy(w_hi[:, 0, :, :, :], w_raw[:]).then_inc(w_hi_ready, 1)
                    for n in range(NR):
                        i, cols = piece(n)
                        act.wait_ge(raw_in[n % 4], 16 * (n // 4) + 16)
                        A.copy(b_hi[:, i, cols], raw[:, n % 4, :]).then_inc(raw_hi, 1)
                    return
                act.wait_ge(w_loaded, j * 16 + 16)
                if not is_int(j, 1):
                    act.wait_ge(proj_ps, j * 4 - 4)
                A.copy(w_hi[:, par, :, :, :], w_raw[:]).then_inc(w_hi_ready, 1)
            over_columns(act, split_w)

        @block.vector
        def _(dve):
            def split_w(j, par):
                dve.wait_ge(w_hi_ready, j + 1)
                V.tensor_tensor(w_lo[:, par, :, :, :], w_raw[:], w_hi[:, par, :, :, :].bitcast(F32), ALU.subtract).then_inc(w_lo_ready, 1)

            def column(j, par, m):
                for i in range(4):
                    dve.wait_ge(gate_in[i % 2], j * 32 + (16 * (i // 2) + 16))
                    dve.wait_ge(proj_ps, j * 4 + (i + 1))
                    if i == 0 and not is_int(j, 0, 1):
                        dve.wait_ge(y_stored[par], m * 16)
                    elif i >= 2:
                        dve.wait_ge(y_added, j * 4 + i)
                    to = prod[:] if i else y[:, par, :]
                    V.tensor_tensor(to.rearrange("p (b t) -> p b t", t=BLK), gate[:, i % 2, :].rearrange("p (b t) -> p b t", t=BLK),
                                    ps[:, i % 2, :, :], ALU.mult).then_inc(gated, 1)
                    dve.wait_ge(gated, j * 4 + (i + 1))
                    if i:
                        V.tensor_tensor(y[:, par, :], y[:, par, :], prod[:], ALU.add).then_inc(y_added, 1)
                    else:
                        dve.sem_inc(y_added, 1)
                    if i == 1 and not is_int(j, KT - 1):
                        split_w(j + 1, 1 - par)
            split_w(0, 0)
            for n in range(1, NR, 2):
                i, cols = piece(n)
                dve.wait_ge(raw_hi, n + 1)
                V.tensor_tensor(b_lo[:, i, cols], raw[:, n % 4, :], b_hi[:, i, cols].bitcast(F32), ALU.subtract).then_inc(raw_lo[n % 2], 1)
            over_columns(dve, column)

        @block.tensor
        def _(pe):
            def column(j, par, before):
                pe.wait_ge(w_lo_ready, j + 1)
                for i in range(4):
                    if is_int(j, 0):
                        for half in range(2):
                            pe.wait_ge(raw_lo[half], 2 * i + 2)
                    if not (is_int(j, 0) and i < 2):
                        pe.wait_ge(gated, j * 4 + (i - 1))
                    for b in range(NB):
                        cols = slice(b * BLK, (b + 1) * BLK)
                        for k in range(2):
                            o, m = ps[:, i % 2, b, :], 2 * i + k
                            T.matmul(o, w_hi[:, par, i, k, :], b_hi[:, m, cols], start=(k == 0), stop=False)
                            T.matmul(o, w_hi[:, par, i, k, :], b_lo[:, m, cols], start=False, stop=False)
                            last = T.matmul(o, w_lo[:, par, i, k, :], b_hi[:, m, cols], start=False, stop=(k == 1))
                    last.then_inc(proj_ps, 1)
            over_columns(pe, column)


def output_stage(nc, t, s):
    with ExitStack() as ctx:
        sb = lambda name, shape, dt=F32: ctx.enter_context(nc.sbuf_tensor(name, shape, dt))
        sem = lambda name: ctx.enter_context(nc.semaphore(name))
        wo_raw = sb("wo_raw", [P, 4, D])
        wo_hi, wo_lo = sb("wo_hi", [P, KT, D], F32R), sb("wo_lo", [P, KT, D], F32R)
        yr = sb("y_raw", [P, 2, KT, P])
        yh, yl = sb("y_hi", [P, 2, KT, P], F32R), sb("y_lo", [P, 2, KT, P], F32R)
        xr = sb("x_res", [P, 2, D])
        gb, fg = sb("gate_rows", [P, D]), sb("final_g_rows", [P, D])
        gcol = sb("gate_cols", [P, P])
        junk = sb("out_junk", [P, D])
        ss, rt, rs = sb("out_ss", [P, 2]), sb("out_rt", [P, 2]), sb("out_rs", [P, 2])
        ps = ctx.enter_context(nc.psum_tensor("out_ps", [P, 4, BLK], F32))
        gps = ctx.enter_context(nc.psum_tensor("gate_ps", [P, 2, BLK], F32))
        wo_in = [sem(f"wo_in{i}") for i in range(4)]
        wo_h, wo_l, fg_in = sem("wo_hi_ready"), sem("wo_lo_ready"), sem("final_g_in")
        y_in, x_in = [sem("y_in0"), sem("y_in1")], [sem("xr_in0"), sem("xr_in1")]
        y_h, y_l, prod = sem("y_hi_ready"), sem("y_lo_ready"), sem("out_products")
        gcol_set, gate_mm = sem("gate_cols_set"), sem("gate_turned")
        vec = Results(ctx, nc, "out_vector", ["gated", "res", "rec", "norm"])
        sca = Results(ctx, nc, "out_scalar", ["ss", "rt"])
        gstep = Signal(ctx, nc, "gate_rows_set")
        stored = [sem("out_stored0"), sem("out_stored1")]
        block = ctx.enter_context(nc.Block())
        V, A, T = nc.vector, nc.scalar, nc.tensor
        NTT = SEQ // P
        x_rows = t["x"].rearrange("a (n p) d -> (a n) p d", p=P)
        o_rows = t["out"].rearrange("a (n p) d -> (a n) p d", p=P)

        def over_tiles(eng, body):
            body(0, 0, 0)
            body(1, 1, 0)
            with eng.Fori(1, NTT // 2) as n:
                body(n * 2, 0, n)
                body(n * 2 + 1, 1, n)

        @block.sync
        def _(sp):
            w = t["w_out"].rearrange("l (k p) n -> (l k) p n", p=P)
            sp.dma_start(fg[:], t["final_g"].rearrange("(a d) -> a d", a=1).to_broadcast([P, D])).then_inc(fg_in, 16)
            def load(n, par, m):
                if not isinstance(n, int):
                    sp.wait_ge(y_l, n - 1)
                sp.dma_start(yr[:, par, :, :], t["mergedT"][:, :, bass.ds(n * P, P)].rearrange("k p t -> p k t")).then_inc(y_in[par], 16)
                if not isinstance(n, int):
                    sp.wait_ge(stored[par], m * 16)
                sp.dma_start(xr[:, par, :], x_rows[bass.ds(n, 1), :, :].rearrange("a p d -> p (a d)")).then_inc(x_in[par], 16)

            def load_later(n, par, m):
                if not isinstance(n, int):
                    load(n, par, m)
            load(0, 0, 0)
            for k in range(KT):
                if k >= 4:
                    sp.wait_ge(wo_l, k - 3)
                sp.dma_start(wo_raw[:, k % 4, :], w[k]).then_inc(wo_in[k % 4], 16)
            load(1, 1, 0)
            over_tiles(sp, load_later)

        @block.gpsimd
        def _(pool):
            def split(n, par, m):
                pool.wait_ge(y_h, n + 1)
                nc.gpsimd.tensor_tensor(yl[:, par, :, :], yr[:, par, :, :], yh[:, par, :, :].bitcast(F32), ALU.subtract).then_inc(y_l, 1)
                if isinstance(n, int) and n == 0:
                    for k in range(KT):
                        pool.wait_ge(wo_h, k + 1)
                        nc.gpsimd.tensor_tensor(wo_lo[:, k, :], wo_raw[:, k % 4, :], wo_hi[:, k, :].bitcast(F32), ALU.subtract).then_inc(wo_l, 1)
            over_tiles(pool, split)

        @block.scalar
        def _(act):
            def hi(n, par, m):
                act.wait_ge(y_in[par], m * 16 + 16)
                if not isinstance(n, int):
                    act.wait_ge(prod, n - 1)
                A.copy(yh[:, par, :, :], yr[:, par, :, :]).then_inc(y_h, 1)

            def norm(n, par, m):
                vec.after(act, n, "res")
                sca.own(act, n, A.activation(junk[:], xr[:, par, :], ACT.Square, accum_out=ss[:, par:par + 1]), "ss")
                sca.own(act, n, A.activation(rt[:, par:par + 1], ss[:, par:par + 1], ACT.Sqrt, bias=s["eps"][:], scale=1.0 / D), "rt")
                vec.after(act, n, "norm")
                act.dma_start(o_rows[bass.ds(n, 1), :, :].rearrange("a p d -> p (a d)"), xr[:, par, :]).then_inc(stored[par], 16)
            hi(0, 0, 0)
            for k in range(KT):
                act.wait_ge(wo_in[k % 4], 16 * (k // 4 + 1))
                A.copy(wo_hi[:, k, :], wo_raw[:, k % 4, :]).then_inc(wo_h, 1)
            hi(1, 1, 0)
            norm(0, 0, 0)
            with act.Fori(1, NTT // 2) as n:
                hi(n * 2, 0, n)
                norm(n * 2 - 1, 1, n - 1)
                hi(n * 2 + 1, 1, n)
                norm(n * 2, 0, n)
            norm(NTT - 1, 1, NTT // 2 - 1)
            for par in range(2):
                act.wait_ge(stored[par], 16 * NTT // 2)

        @block.vector
        def _(dve):
            for k in range(KT):
                gstep.step(dve, V.tensor_copy(gcol[:], s["mod"][:, 0, 2 * KT + k:2 * KT + k + 1].to_broadcast([P, P])))
                dve.wait_ge(gate_mm, k + 1)
            V.tensor_copy(gb[:].rearrange("p (b d) -> p b d", b=2), gps[:]).then_inc(gcol_set, 1)
            dve.wait_ge(gcol_set, 1)
            dve.wait_ge(fg_in, 16)

            def tile(n, par, m):
                dve.wait_ge(prod, n + 1)
                dve.wait_ge(x_in[par], m * 16 + 16)
                gated = ps[:, 2 * par:2 * par + 2, :]
                vec.own(dve, n, V.tensor_tensor(gated, gated, gb[:].rearrange("p (b d) -> p b d", b=2), ALU.mult), "gated")
                xv = xr[:, par, :].rearrange("p (b d) -> p b d", b=2)
                vec.own(dve, n, V.tensor_tensor(xv, xv, gated, ALU.add), "res")
                sca.after(dve, n, "rt")
                vec.own(dve, n, V.reciprocal(rs[:, par:par + 1], rt[:, par:par + 1]), "rec")
                vec.own(dve, n, V.scalar_tensor_tensor(xr[:, par, :], xr[:, par, :], rs[:, par:par + 1], fg[:], ALU.mult, ALU.mult), "norm")
            over_tiles(dve, tile)

        @block.tensor
        def _(pe):
            for k in range(KT):
                pe.wait_ge(gstep.sem, k + 1)
                T.matmul(gps[:, k // 4, (k % 4) * P:(k % 4 + 1) * P], gcol[:], s["ident"][:], start=True, stop=True).then_inc(gate_mm, 1)

            def tile(n, par, m):
                pe.wait_ge(y_l, n + 1)
                if not isinstance(n, int):
                    vec.after(pe, n - 2, "res")
                for k in range(KT):
                    if isinstance(n, int) and n == 0:
                        pe.wait_ge(wo_l, k + 1)
                    for b in range(2):
                        o = ps[:, 2 * par + b, :]
                        cols = slice(b * BLK, (b + 1) * BLK)
                        T.matmul(o, yh[:, par, k, :], wo_hi[:, k, cols], start=(k == 0), stop=False)
                        T.matmul(o, yh[:, par, k, :], wo_lo[:, k, cols], start=False, stop=False)
                        last = T.matmul(o, yl[:, par, k, :], wo_hi[:, k, cols], start=False, stop=(k == KT - 1))
                last.then_inc(prod, 1)
            over_tiles(pe, tile)


STAGES = (modulation_stage, projection_stage, recurrence_stage, attention_stage, merge_stage, output_stage)


_INS = ["x", "c", "ctx", "c_ctx", "ada_w", "ada_b", "norm_g", "w_in", "gm_ln_g", "gm_ln_b", "gm_ws", "gm_bs", "na_rpb",
        "rw_mu", "rw_w0", "rw_w2", "rw_a0", "rw_a2", "rw_kk", "rw_ka", "rw_rk", "rw_gn_g", "rw_gn_b", "pl_w", "pl_scale",
        "w_br", "w_out", "final_g"]


def hybrid_layer_kernel(nc, t, stages=None):
    with ExitStack() as ctx:
        ctx.enter_context(nc.allow_non_contiguous_dma(reason="parameters as columns"))
        s = {name: ctx.enter_context(nc.sbuf_tensor(name, shape, F32)) for name, shape in (
            ("ident", [P, P]), ("ones", [P, P]), ("heads", [P, P]), ("head_mean", [P, P]), ("eps", [P, 1]), ("gn_eps", [P, 1]),
            ("mod", [P, 2, 24]), ("gscale", [P, 2, KT]))}
        for stage in (stages or STAGES):
            stage(nc, t, s)


SCRATCH = {"zT": (T_END, P, ZPAD), "gT": (2, 2, P, NT), "yT": (2, 2, P, NT),
           "bonusT": (2, P, NT), "branchT": (8, P, SEQ), "rpbPad": (60, GRID, 2 * GRID), "mergedT": (KT, P, SEQ), "gatesT": (32, P, SEQ)}


def kernel(**inputs):
    import numpy as _np
    import concourse.bacc as _bacc
    from concourse import mybir as _mybir
    from concourse.bass_utils import run_bass_kernel_spmd as _run

    nc = _bacc.Bacc("TRN2", target_bir_lowering=False, num_devices=1)
    arrays, t = {}, {}
    for name in _INS:
        a = _np.ascontiguousarray(inputs[name])
        arrays[f"in_{name}"] = a
        t[name] = nc.dram_tensor(f"in_{name}", a.shape, _mybir.dt.from_np(a.dtype), kind="ExternalInput").ap()
    for name, shape in SCRATCH.items():
        t[name] = nc.dram_tensor(f"scratch_{name}", shape, F32, kind="Internal").ap()
    t["out"] = nc.dram_tensor("out", (1, SEQ, D), F32, kind="ExternalOutput").ap()
    hybrid_layer_kernel(nc, t)
    r = _run(nc, [arrays], core_ids=[0])
    return r.results[0]["out"]
```
